# Optimizing a Trainium2 kernel written in Bass

```python
import math
import jax, jax.numpy as jnp
from jax import lax
import numpy as np

D_MODEL = 1024
BATCH = 1
SEQ = 512
DEPTH = 1

GRID_W = 64
CTX_LEN = 256
D_HYENA = 512
HYENA_ORDER = 2
FILTER_EMB = 33
FILTER_WIDTH = 64
FILTER_TARGET = 1e-2
FAST_DECAY_PCT = 0.3
SLOW_DECAY_PCT = 1.5
N_HEADS = 4
HEAD_DIM = 64
D_ATTN = N_HEADS * 2 * HEAD_DIM
ROPE_BASE = 10000.0
Q_BLOCK = 128
D_FF = ((8 * D_MODEL + 3 * 256 - 1) // (3 * 256)) * 256
EPS = 1e-6
OFF_Q = (HYENA_ORDER + 1) * D_HYENA
OFF_K = OFF_Q + D_ATTN
OFF_V = OFF_K + D_ATTN
OFF_G = OFF_V + D_ATTN
N_COLS = OFF_G + 2 * D_MODEL


def rmsnorm(x, g):
    xf = x.astype(jnp.float32)
    y = xf * lax.rsqrt(jnp.mean(xf * xf, axis=-1, keepdims=True) + EPS)
    return (y * g.astype(jnp.float32)).astype(x.dtype)

def modulate(h, shift, scale):
    return h * (1.0 + scale) + shift

def short_conv(u, w, b):
    L = u.shape[1]
    up = jnp.pad(u, ((0, 0), (1, 1), (0, 0)))
    return up[:, :L] * w[0] + up[:, 1:L + 1] * w[1] + up[:, 2:] * w[2] + b

def hyena_filters(L, fw1, fb1, fw2, fb2, fw3, fb3, ffreq):
    f32 = jnp.float32
    bands = (FILTER_EMB - 1) // 2
    t = jnp.linspace(0.0, 1.0, L, dtype=f32)[:, None]
    w = (2.0 * math.pi / L) * jnp.arange(L, dtype=f32)[:, None]
    fr = jnp.linspace(1e-4, bands - 1, bands, dtype=f32)[None, :]
    z = jnp.concatenate([t, jnp.cos(fr * w), -jnp.sin(fr * w)], axis=-1)
    freq = ffreq.astype(f32)
    hdn = jnp.sin(freq * (z @ fw1.astype(f32) + fb1.astype(f32)))
    hdn = jnp.sin(freq * (hdn @ fw2.astype(f32) + fb2.astype(f32)))
    h = (hdn @ fw3.astype(f32) + fb3.astype(f32)).reshape(L, HYENA_ORDER, 2, D_HYENA)
    deltas = jnp.abs(jnp.linspace(math.log(FILTER_TARGET) / SLOW_DECAY_PCT,
                                  math.log(FILTER_TARGET) / FAST_DECAY_PCT, D_HYENA, dtype=f32))
    h = h * jnp.exp(-t * deltas)[:, None, None, :]
    h_fwd, h_bwd = h[:, :, 0], h[:, :, 1]
    circ = jnp.concatenate([h_fwd, jnp.zeros((1, HYENA_ORDER, D_HYENA), f32), h_bwd[:0:-1]], axis=0)
    return jnp.fft.rfft(circ, axis=0)

def fftconv(u, hk, dbias):
    L = u.shape[1]
    uf = u.astype(jnp.float32)
    y = jnp.fft.irfft(jnp.fft.rfft(uf, n=2 * L, axis=1) * hk[None], n=2 * L, axis=1)[:, :L]
    return (y + uf * dbias.astype(jnp.float32)).astype(u.dtype)

def hyena_branch(u, conv_w, conv_b, fw1, fb1, fw2, fb2, fw3, fb3, ffreq, dbias):
    L = u.shape[1]
    u = short_conv(u, conv_w, conv_b)
    parts = jnp.split(u, HYENA_ORDER + 1, axis=-1)
    hk = hyena_filters(L, fw1, fb1, fw2, fb2, fw3, fb3, ffreq)
    z = parts[0]
    for n in range(HYENA_ORDER):
        z = parts[n + 1] * fftconv(z, hk[:, n], dbias[n])
    return z

def _rotate(x, pos):
    half = x.shape[-1] // 2
    inv = ROPE_BASE ** (-jnp.arange(half, dtype=jnp.float32) / half)
    ang = pos.astype(jnp.float32)[:, None] * inv[None, :]
    cos = jnp.cos(ang)[None, :, None, None, :].astype(x.dtype)
    sin = jnp.sin(ang)[None, :, None, None, :].astype(x.dtype)
    x1, x2 = x[..., :half], x[..., half:]
    return jnp.concatenate([x1 * cos - x2 * sin, x1 * sin + x2 * cos], axis=-1)

def rope_2d(x, row, col):
    h = x.shape[-1] // 2
    return jnp.concatenate([_rotate(x[..., :h], row), _rotate(x[..., h:], col)], axis=-1)

def diff_attention(q, k, v, lam):
    B, H, _, Lq, d = q.shape
    nb = Lq // Q_BLOCK
    qb = jnp.moveaxis(q.reshape(B, H, 2, nb, Q_BLOCK, d), 3, 0)
    scale = HEAD_DIM ** -0.5

    def block(qi):
        s = jnp.einsum('bhiqd,bhikd->bhiqk', qi, k).astype(jnp.float32) * scale
        p = jax.nn.softmax(s, axis=-1)
        a = (p[:, :, 0] - lam * p[:, :, 1]).astype(v.dtype)
        return jnp.einsum('bhqk,bhkv->bhqv', a, v)

    o = lax.map(block, qb)
    return jnp.moveaxis(o, 0, 2).reshape(B, H, Lq, 2 * d)

def heads_out(o, subln_g, lam_init):
    B, H, L, dv = o.shape
    o = rmsnorm(o, subln_g) * (1.0 - lam_init)
    return o.transpose(0, 2, 1, 3).reshape(B, L, H * dv)

def swiglu(h, w_gate, w_up, w_down):
    return (jax.nn.silu(h @ w_gate) * (h @ w_up)) @ w_down

def first_inputs(seed: int = 0) -> dict:
    key = jax.random.key(seed)
    ks = jax.random.split(key, 40)
    f32 = jnp.float32

    def nrm(i, shape, s):
        return jax.random.normal(ks[i], shape, f32) * s

    return {
        'x': nrm(0, (BATCH, SEQ, D_MODEL), 1.0),
        'c': nrm(1, (BATCH, D_MODEL), 1.0),
        'ctx': nrm(2, (BATCH, CTX_LEN, D_MODEL), 1.0),
        'c_ctx': nrm(3, (D_MODEL,), 1.0),
        'w_ada': nrm(4, (DEPTH, D_MODEL, 6 * D_MODEL), 0.5 * D_MODEL ** -0.5),
        'b_ada': nrm(5, (DEPTH, 6 * D_MODEL), 0.01),
        'g_mix_pre': 1.0 + nrm(6, (DEPTH, D_MODEL), 0.05),
        'g_mix_post': 1.0 + nrm(7, (DEPTH, D_MODEL), 0.05),
        'g_ffn_pre': 1.0 + nrm(8, (DEPTH, D_MODEL), 0.05),
        'g_ffn_post': 1.0 + nrm(9, (DEPTH, D_MODEL), 0.05),
        'w_in': nrm(10, (DEPTH, D_MODEL, N_COLS), D_MODEL ** -0.5),
        'hy_conv_w': nrm(11, (DEPTH, 3, (HYENA_ORDER + 1) * D_HYENA), 0.5),
        'hy_conv_b': nrm(12, (DEPTH, (HYENA_ORDER + 1) * D_HYENA), 0.01),
        'hy_f_w1': nrm(13, (DEPTH, FILTER_EMB, FILTER_WIDTH), FILTER_EMB ** -0.5),
        'hy_f_b1': nrm(14, (DEPTH, FILTER_WIDTH), 0.1),
        'hy_f_w2': nrm(15, (DEPTH, FILTER_WIDTH, FILTER_WIDTH), FILTER_WIDTH ** -0.5),
        'hy_f_b2': nrm(16, (DEPTH, FILTER_WIDTH), 0.1),
        'hy_f_w3': nrm(17, (DEPTH, FILTER_WIDTH, HYENA_ORDER * 2 * D_HYENA), 0.03 * FILTER_WIDTH ** -0.5),
        'hy_f_b3': nrm(18, (DEPTH, HYENA_ORDER * 2 * D_HYENA), 0.003),
        'hy_f_freq': 1.0 + nrm(19, (DEPTH, FILTER_WIDTH), 0.05),
        'hy_bias': nrm(20, (DEPTH, HYENA_ORDER, D_HYENA), 1.0),
        'lambda_q1': nrm(21, (DEPTH, HEAD_DIM), 0.1),
        'lambda_k1': nrm(22, (DEPTH, HEAD_DIM), 0.1),
        'lambda_q2': nrm(23, (DEPTH, HEAD_DIM), 0.1),
        'lambda_k2': nrm(24, (DEPTH, HEAD_DIM), 0.1),
        'att_subln_g': 1.0 + nrm(25, (DEPTH, 2 * HEAD_DIM), 0.05),
        'w_hy_up': nrm(26, (DEPTH, D_HYENA, D_MODEL), D_HYENA ** -0.5),
        'w_att_up': nrm(27, (DEPTH, D_ATTN, D_MODEL), D_ATTN ** -0.5),
        'w_out': nrm(28, (DEPTH, D_MODEL, D_MODEL), D_MODEL ** -0.5),
        'w_ffn_gate': nrm(29, (DEPTH, D_MODEL, D_FF), D_MODEL ** -0.5),
        'w_ffn_up': nrm(30, (DEPTH, D_MODEL, D_FF), D_MODEL ** -0.5),
        'w_ffn_down': nrm(31, (DEPTH, D_FF, D_MODEL), D_FF ** -0.5),
    }

def first_block(x, c, ctx, c_ctx, w_ada, b_ada, g_mix_pre, g_mix_post, g_ffn_pre, g_ffn_post,
              w_in, hy_conv_w, hy_conv_b, hy_f_w1, hy_f_b1, hy_f_w2, hy_f_b2, hy_f_w3, hy_f_b3,
              hy_f_freq, hy_bias, lambda_q1, lambda_k1, lambda_q2, lambda_k2, att_subln_g,
              w_hy_up, w_att_up, w_out, w_ffn_gate, w_ffn_up, w_ffn_down):
    B, L, D = x.shape
    C = ctx.shape[1]
    rows = L // GRID_W
    row = jnp.repeat(jnp.arange(rows, dtype=jnp.int32), GRID_W)
    col = jnp.tile(jnp.arange(GRID_W, dtype=jnp.int32), rows)
    f32 = jnp.float32

    for layer in range(DEPTH):
        last = layer == DEPTH - 1
        hy_p = (hy_conv_w[layer], hy_conv_b[layer], hy_f_w1[layer], hy_f_b1[layer], hy_f_w2[layer],
                hy_f_b2[layer], hy_f_w3[layer], hy_f_b3[layer], hy_f_freq[layer], hy_bias[layer])
        ada = jax.nn.silu(c) @ w_ada[layer] + b_ada[layer]
        sh1, sc1, g1, sh2, sc2, g2 = jnp.split(ada[:, None, :], 6, axis=-1)
        ada_c = jax.nn.silu(c_ctx) @ w_ada[layer] + b_ada[layer]
        csh1, csc1, cg1, csh2, csc2, cg2 = jnp.split(ada_c, 6, axis=-1)

        lam_init = 0.8 - 0.6 * math.exp(-0.3 * layer)
        lam = (jnp.exp(jnp.sum(lambda_q1[layer].astype(f32) * lambda_k1[layer].astype(f32)))
               - jnp.exp(jnp.sum(lambda_q2[layer].astype(f32) * lambda_k2[layer].astype(f32))) + lam_init)

        hc = modulate(rmsnorm(ctx, g_mix_pre[layer]), csh1, csc1)
        if last:
            kv_c = hc @ w_in[layer][:, OFF_K:OFF_G]
        else:
            proj_c = hc @ w_in[layer]
            kv_c = proj_c[..., OFF_K:OFF_G]
        k_c = kv_c[..., :D_ATTN].reshape(B, C, N_HEADS, 2, HEAD_DIM)
        v_c = kv_c[..., D_ATTN:].reshape(B, C, N_HEADS, 2 * HEAD_DIM)

        h = modulate(rmsnorm(x, g_mix_pre[layer]), sh1, sc1)
        proj = h @ w_in[layer]
        y_hy = hyena_branch(proj[..., :OFF_Q], *hy_p) @ w_hy_up[layer]
        q = rope_2d(proj[..., OFF_Q:OFF_K].reshape(B, L, N_HEADS, 2, HEAD_DIM), row, col)
        k = rope_2d(proj[..., OFF_K:OFF_V].reshape(B, L, N_HEADS, 2, HEAD_DIM), row, col)
        v = proj[..., OFF_V:OFF_G].reshape(B, L, N_HEADS, 2 * HEAD_DIM)
        k_all = jnp.concatenate([k, k_c], axis=1).transpose(0, 2, 3, 1, 4)
        v_all = jnp.concatenate([v, v_c], axis=1).transpose(0, 2, 1, 3)
        o = diff_attention(q.transpose(0, 2, 3, 1, 4), k_all, v_all, lam)
        y_att = heads_out(o, att_subln_g[layer], lam_init) @ w_att_up[layer]
        g_hy, g_att = jnp.split(jax.nn.sigmoid(proj[..., OFF_G:]), 2, axis=-1)
        mixed = (g_hy * y_hy + g_att * y_att) @ w_out[layer]
        x = x + g1 * rmsnorm(mixed, g_mix_post[layer])
        hf = modulate(rmsnorm(x, g_ffn_pre[layer]), sh2, sc2)
        f = swiglu(hf, w_ffn_gate[layer], w_ffn_up[layer], w_ffn_down[layer])
        x = x + g2 * rmsnorm(f, g_ffn_post[layer])

        if not last:
            qc = proj_c[..., OFF_Q:OFF_K].reshape(B, C, N_HEADS, 2, HEAD_DIM).transpose(0, 2, 3, 1, 4)
            oc = diff_attention(qc, k_c.transpose(0, 2, 3, 1, 4), v_c.transpose(0, 2, 1, 3), lam)
            yc_att = heads_out(oc, att_subln_g[layer], lam_init) @ w_att_up[layer]
            yc_hy = hyena_branch(proj_c[..., :OFF_Q], *hy_p) @ w_hy_up[layer]
            gc_hy, gc_att = jnp.split(jax.nn.sigmoid(proj_c[..., OFF_G:]), 2, axis=-1)
            mixed_c = (gc_hy * yc_hy + gc_att * yc_att) @ w_out[layer]
            ctx = ctx + cg1 * rmsnorm(mixed_c, g_mix_post[layer])
            hfc = modulate(rmsnorm(ctx, g_ffn_pre[layer]), csh2, csc2)
            fc = swiglu(hfc, w_ffn_gate[layer], w_ffn_up[layer], w_ffn_down[layer])
            ctx = ctx + cg2 * rmsnorm(fc, g_ffn_post[layer])
    return x


DEPTH_2 = 2

N_MIXERS = 2
CHUNK = 128
GMLP_WIDTH = 2 * D_MODEL
GMLP_GROUPS = 8
GMLP_GROUP_DIM = GMLP_WIDTH // GMLP_GROUPS
FOX_HEAD_DIM = 64
FOX_HEADS = D_MODEL // FOX_HEAD_DIM
FOX_WIDTH = FOX_HEADS * FOX_HEAD_DIM
D_FF_2 = 4 * D_MODEL
N_GMLP = (DEPTH_2 + 1) // 2
N_FOX = DEPTH_2 // 2
RMS_EPS = 1e-6
LN_EPS = 1e-5


def rms_norm(x, g):
    xf = x.astype(jnp.float32)
    y = xf * lax.rsqrt(jnp.mean(xf * xf, axis=-1, keepdims=True) + RMS_EPS)
    return (y * g.astype(jnp.float32)).astype(x.dtype)

def layer_norm(x, g, b):
    xf = x.astype(jnp.float32)
    mu = jnp.mean(xf, axis=-1, keepdims=True)
    xc = xf - mu
    var = jnp.mean(xc * xc, axis=-1, keepdims=True)
    y = xc * lax.rsqrt(var + LN_EPS) * g.astype(jnp.float32) + b.astype(jnp.float32)
    return y.astype(x.dtype)

def gmlp_mixer(h, w_in, ln_g, ln_b, w_s, b_s, w_out):
    B, S, _ = h.shape
    z = jax.nn.gelu(h @ w_in)
    u, v = jnp.split(z, 2, axis=-1)
    v = layer_norm(v, ln_g, ln_b)
    v = v.reshape(B, S // CHUNK, CHUNK, GMLP_GROUPS, GMLP_GROUP_DIM)
    causal = jnp.tril(jnp.ones((CHUNK, CHUNK), dtype=bool))
    w = jnp.where(causal[None], w_s, jnp.zeros((), w_s.dtype))
    s = jnp.einsum('gts,bnsgc->bntgc', w, v) + b_s.T[None, None, :, :, None]
    out = u * s.reshape(B, S, GMLP_WIDTH)
    return out @ w_out

def fox_mixer(h, w_in, b_f, q_g, k_g, w_out):
    B, S, _ = h.shape
    W, H, Dh = FOX_WIDTH, FOX_HEADS, FOX_HEAD_DIM
    p = h @ w_in
    q, k, v, gate, f_logit = jnp.split(p, [W, 2 * W, 3 * W, 4 * W], axis=-1)
    q = rms_norm(q.reshape(B, S, H, Dh), q_g).transpose(0, 2, 1, 3)
    k = rms_norm(k.reshape(B, S, H, Dh), k_g).transpose(0, 2, 1, 3)
    v = v.reshape(B, S, H, Dh).transpose(0, 2, 1, 3)
    log_f = jax.nn.log_sigmoid((f_logit + b_f).astype(jnp.float32))
    c = jnp.cumsum(log_f, axis=1).transpose(0, 2, 1)
    scale = Dh ** -0.5
    outs = []
    for i in range(S // Q_BLOCK):
        q0 = i * Q_BLOCK
        kend = q0 + Q_BLOCK
        qb = q[:, :, q0:kend]
        kb = k[:, :, :kend]
        vb = v[:, :, :kend]
        logits = jnp.einsum('bhtd,bhsd->bhts', qb, kb).astype(jnp.float32) * scale
        logits = logits + c[:, :, q0:kend, None] - c[:, :, None, :kend]
        t_idx = q0 + jnp.arange(Q_BLOCK)[:, None]
        s_idx = jnp.arange(kend)[None, :]
        logits = jnp.where(t_idx >= s_idx, logits, -jnp.inf)
        probs = jax.nn.softmax(logits, axis=-1).astype(vb.dtype)
        outs.append(jnp.einsum('bhts,bhsd->bhtd', probs, vb))
    o = jnp.concatenate(outs, axis=2).transpose(0, 2, 1, 3).reshape(B, S, W)
    o = o * jax.nn.sigmoid(gate)
    return o @ w_out

def sqrelu_mlp(h, w1, w2):
    return jnp.square(jax.nn.relu(h @ w1)) @ w2

def second_inputs(seed: int = 0) -> dict:
    key = jax.random.key(seed)
    ks = jax.random.split(key, 20)
    f32 = jnp.float32
    D, E, G, W, H, Dh = D_MODEL, GMLP_WIDTH, GMLP_GROUPS, FOX_WIDTH, FOX_HEADS, FOX_HEAD_DIM
    nrm = lambda k, shape, s: jax.random.normal(k, shape, f32) * s
    x = nrm(ks[0], (BATCH, SEQ, D), 1.0)
    gmlp_w_in = nrm(ks[1], (N_GMLP, D, 2 * E), D ** -0.5)
    gmlp_ln_g = 1.0 + nrm(ks[2], (N_GMLP, E), 0.02)
    gmlp_ln_b = nrm(ks[3], (N_GMLP, E), 0.02)
    gmlp_w_s = nrm(ks[4], (N_GMLP, G, CHUNK, CHUNK), CHUNK ** -0.5)
    gmlp_b_s = 1.0 + nrm(ks[5], (N_GMLP, G, CHUNK), 0.1)
    gmlp_w_out = nrm(ks[6], (N_GMLP, E, D), E ** -0.5)
    fox_w_in = nrm(ks[7], (N_FOX, D, 4 * W + H), D ** -0.5)
    fox_b_f = jnp.linspace(0.0, 4.0, H, dtype=f32)[None, :] + nrm(ks[8], (N_FOX, H), 0.1)
    fox_q_g = 1.0 + nrm(ks[9], (N_FOX, Dh), 0.02)
    fox_k_g = 1.0 + nrm(ks[10], (N_FOX, Dh), 0.02)
    fox_w_out = nrm(ks[11], (N_FOX, W, D), W ** -0.5)
    mix_norm_g = 1.0 + nrm(ks[12], (DEPTH_2, D), 0.02)
    mlp_norm_g = 1.0 + nrm(ks[13], (DEPTH_2, D), 0.02)
    mlp_w1 = nrm(ks[14], (DEPTH_2, D, D_FF_2), D ** -0.5)
    mlp_w2 = nrm(ks[15], (DEPTH_2, D_FF_2, D), D_FF_2 ** -0.5)
    return {"x": x, "gmlp_w_in": gmlp_w_in, "gmlp_ln_g": gmlp_ln_g, "gmlp_ln_b": gmlp_ln_b,
            "gmlp_w_s": gmlp_w_s, "gmlp_b_s": gmlp_b_s, "gmlp_w_out": gmlp_w_out,
            "fox_w_in": fox_w_in, "fox_b_f": fox_b_f, "fox_q_g": fox_q_g, "fox_k_g": fox_k_g,
            "fox_w_out": fox_w_out, "mix_norm_g": mix_norm_g, "mlp_norm_g": mlp_norm_g,
            "mlp_w1": mlp_w1, "mlp_w2": mlp_w2}

def second_block(x, gmlp_w_in, gmlp_ln_g, gmlp_ln_b, gmlp_w_s, gmlp_b_s, gmlp_w_out,
              fox_w_in, fox_b_f, fox_q_g, fox_k_g, fox_w_out,
              mix_norm_g, mlp_norm_g, mlp_w1, mlp_w2):
    for i in range(DEPTH_2):
        h = rms_norm(x, mix_norm_g[i])
        j = i // N_MIXERS
        if i % N_MIXERS == 0:
            x = x + gmlp_mixer(h, gmlp_w_in[j], gmlp_ln_g[j], gmlp_ln_b[j],
                               gmlp_w_s[j], gmlp_b_s[j], gmlp_w_out[j])
        else:
            x = x + fox_mixer(h, fox_w_in[j], fox_b_f[j], fox_q_g[j], fox_k_g[j], fox_w_out[j])
        h = rms_norm(x, mlp_norm_g[i])
        x = x + sqrelu_mlp(h, mlp_w1[i], mlp_w2[i])
    return x


def setup_inputs(seed=0):
    out = dict(first_inputs(seed))
    for name, value in second_inputs(seed + 1).items():
        if name != "x":
            out[name + "_2"] = value
    return out


def reference(
    x, c, ctx, c_ctx, w_ada, b_ada, g_mix_pre, g_mix_post, g_ffn_pre, g_ffn_post, w_in,
    hy_conv_w, hy_conv_b, hy_f_w1, hy_f_b1, hy_f_w2, hy_f_b2, hy_f_w3, hy_f_b3, hy_f_freq,
    hy_bias, lambda_q1, lambda_k1, lambda_q2, lambda_k2, att_subln_g, w_hy_up, w_att_up, w_out,
    w_ffn_gate, w_ffn_up, w_ffn_down, gmlp_w_in_2, gmlp_ln_g_2, gmlp_ln_b_2, gmlp_w_s_2,
    gmlp_b_s_2, gmlp_w_out_2, fox_w_in_2, fox_b_f_2, fox_q_g_2, fox_k_g_2, fox_w_out_2,
    mix_norm_g_2, mlp_norm_g_2, mlp_w1_2, mlp_w2_2,
):
    x = first_block(
        x, c, ctx, c_ctx, w_ada, b_ada, g_mix_pre, g_mix_post, g_ffn_pre, g_ffn_post, w_in,
        hy_conv_w, hy_conv_b, hy_f_w1, hy_f_b1, hy_f_w2, hy_f_b2, hy_f_w3, hy_f_b3, hy_f_freq,
        hy_bias, lambda_q1, lambda_k1, lambda_q2, lambda_k2, att_subln_g, w_hy_up, w_att_up,
        w_out, w_ffn_gate, w_ffn_up, w_ffn_down,
    )
    return second_block(
        x, gmlp_w_in_2, gmlp_ln_g_2, gmlp_ln_b_2, gmlp_w_s_2, gmlp_b_s_2, gmlp_w_out_2,
        fox_w_in_2, fox_b_f_2, fox_q_g_2, fox_k_g_2, fox_w_out_2, mix_norm_g_2, mlp_norm_g_2,
        mlp_w1_2, mlp_w2_2,
    )


_drawn_inputs = setup_inputs


def setup_inputs(seed=0):
    import zlib

    import numpy as np

    out = dict(_drawn_inputs(seed))
    spreads = {}
    factors = {'g_mix_post': 2.955,
     'g_ffn_post': 3.081,
     'hy_conv_b': 8.0,
     'hy_f_b1': 3.416,
     'hy_f_b2': 2.826,
     'hy_f_freq': 8.0,
     'lambda_q1': 8.0,
     'lambda_k1': 8.0,
     'lambda_q2': 3.493,
     'att_subln_g': 4.174,
     'gmlp_ln_g_2': 7.426,
     'gmlp_ln_b_2': 7.322,
     'fox_q_g_2': 8.0,
     'fox_k_g_2': 8.0,
     'mix_norm_g_2': 3.221}
    for name, (base, spread) in spreads.items():
        noise = np.random.default_rng([zlib.crc32(name.encode()), seed]).standard_normal(out[name].shape)
        drawn = base * np.exp(spread * noise) if base else spread * noise
        out[name] = __import__('jax').numpy.asarray(drawn.astype(out[name].dtype))
    for name, factor in factors.items():
        out[name] = (out[name] * factor).astype(out[name].dtype)
    return out
```

```python
import math
from contextlib import ExitStack

import concourse.bass as bass
from concourse import mybir

F32 = mybir.dt.float32
F32R = mybir.dt.float32r
ALU = mybir.AluOpType
ACT = mybir.ActivationFunctionType
AX = mybir.AxisListType

P = 128
D = 1024
KD = D // P
L = 512
NT = L // P
CTX = 256
NKEY = L + CTX
KT = NKEY // P
HEADS = 4
HY = 512
HC = HY // P
FF = 2816
FC = FF // P
EPS = 1e-6
LN_EPS = 1e-5
LAM_INIT = 0.2
MAGIC = 12582912.0
RING = 4

ADA_T = 48
PHASES = [("hyena", 12, 12), ("qkv", 12, 12), ("mix", 24, 32), ("wout", 8, 8), ("gateup", 44, 44),
          ("down", 24, 8), ("g_in", 32, 32), ("g_out", 16, 8),
          ("up0a", 16, 16), ("dn0a", 16, 8), ("up0b", 16, 16), ("dn0b", 16, 8),
          ("fox", 32, 32), ("fox_out", 8, 8),
          ("up1a", 16, 16), ("dn1a", 16, 8), ("up1b", 16, 16), ("dn1b", 16, 8)]
TB, CB = {}, {}
_t, _c = 0, RING
for _n, _nt, _nc in PHASES:
    TB[_n], CB[_n] = _t, _c
    _t += _nt
    _c += _nc
TILES = _t

COLS, NCOLS = {}, 0
for _n, _w in [("g_mix_pre", 8), ("g_mix_post", 8), ("g_ffn_pre", 8), ("g_ffn_post", 8), ("b_ada", 96),
               ("conv_w", 36), ("conv_b", 12), ("subln", 1), ("ln_g", 16), ("ln_b", 16),
               ("mixn", 16), ("mlpn", 16), ("q_g", 1), ("k_g", 1), ("b_f", 1), ("c", 16),
               ("lam_q", 2), ("lam_k", 2), ("fb1", 1), ("fb2", 1), ("freq", 1)]:
    COLS[_n] = NCOLS
    NCOLS += _w

NORMS = ["mix_pre", "ctx", "mix_post", "ffn_pre", "ffn_post", "g_mix", "mlp0", "fox", "mlp1"]


def build(nc, a):
    ctx = ExitStack()
    with ctx:
        def sb(name, shape, dt=F32):
            return ctx.enter_context(nc.sbuf_tensor(name, shape, dt))

        def sem(name):
            return ctx.enter_context(nc.semaphore(name))

        def overlay(start, specs):
            with ExitStack() as s:
                if start:
                    s.enter_context(nc.sbuf_tensor(f"gap_{specs[0][0]}", [P, start // 4], F32))
                return [s.enter_context(nc.sbuf_tensor(n, sh, dt)) for n, sh, dt in specs]

        KB = 1024
        raw = [sb(f"w_raw{i}", [P, 8, P]) for i in range(RING)]
        whi = [sb(f"w_hi{i}", [P, 8, P], F32R) for i in range(RING)]
        wlo = [sb(f"w_lo{i}", [P, 8, P], F32R) for i in range(RING)]
        xT = sb("xT", [P, KD, L])
        cols = sb("cols", [P, NCOLS])
        ada = sb("ada", [P, ADA_T * 2])
        csil = sb("csil", [P, 16])
        ones = sb("ones", [P, P])
        ones_d = sb("ones_d", [P, P])
        ones_hd = sb("ones_hd", [P, P])
        blk64 = sb("blk64", [P, P])
        ident = sb("ident", [P, P])
        rot = sb("rot", [P, P])
        cmask = sb("cmask", [P, P])
        acol = sb("acol", [P, 64])
        small = sb("small", [P, 96])
        zcol = sb("zcol", [P, 1])
        epsc = sb("epsc", [P, 2])
        sq = [sb(f"sq{i}", [P, L]) for i in range(2)]
        tmp = [sb(f"tmp{i}", [P, L]) for i in range(2)]
        std = sb("std", [P, L])
        rstd = sb("rstd", [P, L])

        HB = 0
        BIG = 32 * KB
        hh, hl = overlay(HB, [("h_hi", [P, KD, L], F32R), ("h_lo", [P, KD, L], F32R)])
        fE, fO = overlay(HB, [("filt_e", [P, NT, 2 * HY], F32), ("filt_o", [P, NT, 2 * HY], F32)])
        (ff_out,) = overlay(HB, [("ff_out", [P, KD, L], F32)])
        (ghi,) = overlay(HB, [("gate_hi", [P, 16, L], F32R)])
        Gr0, Gs0, Gr1, Gs1 = overlay(BIG, [(n, [P, NT, HY], F32) for n in ("gr0", "gs0", "gr1", "gs1")])
        Gr, Gs = [Gr0, Gr1], [Gs0, Gs1]
        C0, S0, dec, fw3, zT, fw1, fw2, hd, targ, tn, fab = overlay(BIG + 32 * KB, [
            ("c_int", [P, NT, HY], F32), ("s_int", [P, NT, HY], F32), ("decay", [P, 5, HY], F32),
            ("fw3", [65, 2048], F32), ("zT", [33, L], F32), ("fw1", [33, 64], F32), ("fw2", [64, 64], F32),
            ("hd", [65, L], F32), ("targ", [64, L], F32), ("tn", [64, L], F32), ("fab", [P, 2, 2, HY], F32)])
        hb = overlay(BIG + 83 * KB, [("hbias", [1, 2, HY], F32)])[0]
        Cm, Sm, n0, n1, x2T, uT, pad0, pad1 = overlay(BIG + 32 * KB, [
            ("c_half", [P, NT, HY], F32), ("s_half", [P, NT, HY], F32), ("n0", [P, NT, HY], F32),
            ("n1", [P, NT, HY], F32), ("x2T", [P, HC, L], F32), ("uT", [P, 8, L], F32),
            ("pad0", [P, L + 2], F32), ("pad1", [P, L + 2], F32)])
        pads = [pad0, pad1]
        (pw,) = overlay(BIG + 72 * KB, [("pointwise", [P, 2, 4, L], F32)])
        zhi, zlo, ohi, olo = overlay(BIG, [("z_hi", [P, HC, L], F32R), ("z_lo", [P, HC, L], F32R),
                                           ("o_hi", [P, HC, L], F32R), ("o_lo", [P, HC, L], F32R)])
        hch, hcl, qT, kT, vN, cxT, cosT, sinT, qe, r1, r2 = overlay(BIG + 16 * KB, [
            ("hc_hi", [P, KD, CTX], F32R), ("hc_lo", [P, KD, CTX], F32R), ("qT", [P, HEADS, L], F32),
            ("kT", [P, HEADS, NKEY], F32), ("vN", [P, HEADS, KT, P], F32), ("ctxT", [P, KD, CTX], F32),
            ("cosT", [P, L], F32), ("sinT", [P, L], F32), ("qe", [P, 2, NKEY], F32),
            ("r1", [P, L], F32), ("r2", [P, L], F32)])
        pp, aT = overlay(BIG + 64 * KB, [("pp", [P, 2, 2, NKEY], F32), ("aT", [P, KT, L], F32)])
        mxh, mxl, sgm, mt = overlay(BIG + 32 * KB, [("mixed_hi", [P, KD, L], F32R), ("mixed_lo", [P, KD, L], F32R),
                                              ("sgm", [P, 2, 2, L], F32), ("mt", [P, 2, 2, L], F32)])
        (mo,) = overlay(BIG, [("mix_out", [P, KD, L], F32)])
        hidh, hidl, sil = overlay(BIG, [("hid_hi", [P, FC, L], F32R), ("hid_lo", [P, FC, L], F32R),
                                        ("silu", [P, 2, L], F32)])
        vT, guT, wsT, bsb, vn, gt, mean, lrs = overlay(BIG, [
            ("g_v", [P, 16, L], F32), ("g_u", [P, 16, L], F32), ("wsT", [P, 8, P], F32), ("bsb", [P, 8, P], F32),
            ("vn", [P, 2, L], F32), ("gt", [P, 2, 2, L], F32), ("lmean", [P, L], F32), ("lrs", [P, L], F32)])
        (glo,) = overlay(BIG, [("gate_lo", [P, 16, L], F32R)])
        mh, ml, = overlay(BIG, [("mlp_hi", [P, 16, L], F32R), ("mlp_lo", [P, 16, L], F32R)])
        (foh, fol, wf, lf, cpos, cneg, fsq, frs, qa, ka, fvT, fvn, fsg, fp, fpT) = overlay(BIG, [
            ("fo_hi", [P, KD, L], F32R), ("fo_lo", [P, KD, L], F32R), ("wf", [P, KD, 16], F32),
            ("lf", [16, 4, L], F32), ("cpos", [16, L], F32), ("cneg", [16, L], F32),
            ("fsq", [P, 2, L], F32), ("frs", [P, L], F32),
            ("qa", [66, 2, L], F32), ("ka", [66, 2, L], F32), ("fvT", [P, L], F32), ("fvn", [P, NT, P], F32),
            ("fsg", [P, L], F32), ("fp", [P, 2, L], F32), ("fpT", [P, NT, L], F32)])

        with ExitStack() as s:
            bank = [s.enter_context(nc.psum_tensor(f"bank{i}", [P, L], F32)) for i in range(8)]
        acc, aux = bank[0:4], bank[4:8]
        with ExitStack() as s:
            sc0, sc1, trT = (s.enter_context(nc.psum_tensor(n, [P, 2 * L], F32)) for n in ("scores0", "scores1", "weightsT"))
        scores = [sc0, sc1]

        w_landed = [sem(f"w_landed{i}") for i in range(RING)]
        w_hi, w_lo, w_used, ada_used, c_free = (sem(n) for n in ("w_hi", "w_lo", "w_used", "ada_used", "c_free"))
        d_cols, d_filt, d_dft, d_att, d_x, d_ws, d_wf, d_c, d_crow, d_out, d_filt2 = (sem(n) for n in (
            "d_cols", "d_filt", "d_dft", "d_att", "d_x", "d_ws", "d_wf", "d_c", "d_crow", "d_out", "d_filt2"))
        consts, c_silu, ada_ready, lam_prod, lam_mm, lam_exp, lam_ready = (sem(n) for n in (
            "consts", "c_silu", "ada_ready", "lam_prod", "lam_mm", "lam_exp", "lam_ready"))
        f_mm, f_arg, f_sin, f_ab, f_eo, g_mm, g_used, f_dve, f_dec = (sem(n) for n in (
            "f_mm", "f_arg", "f_sin", "f_ab", "f_eo", "g_mm", "g_used", "f_dve", "f_dec"))
        nm_sq, nm_sum, nm_std, nm_rstd, nm_tmp, h_hi, h_lo, x_new = (sem(n) for n in (
            "nm_sq", "nm_sum", "nm_std", "nm_rstd", "nm_tmp", "h_hi_s", "h_lo_s", "x_new"))
        acol_ready = sem("acol_ready")
        hy_pad, hy_conv, hy_tr, hy_nat = (sem(n) for n in ("hy_pad", "hy_conv", "hy_tr", "hy_nat"))
        hy_u, hy_pw, hy_y, hy_inv, hy_yd, hy_z, hy_zhi, hy_zlo = (sem(n) for n in (
            "hy_u", "hy_pw", "hy_y", "hy_inv", "hy_yd", "hy_z", "hy_zhi", "hy_zlo"))
        v_step = sem("v_step")
        x_rd = sem("x_rd")
        kv_ev, q_rot, q_done, v_tr, v_nat = (sem(n) for n in (
            "kv_ev", "q_rot", "q_done", "v_tr", "v_nat"))
        a_s, a_mx, a_p, a_cm, a_tr, a_ev, a_o, a_sq, a_ss, a_std, a_tmp, a_hi, a_lo, a_ch = (sem(n) for n in (
            "a_s", "a_mx", "a_p", "a_cm", "a_tr", "a_ev", "a_o", "a_sq", "a_ss", "a_std", "a_tmp", "a_hi", "a_lo", "a_ch"))
        m_sg, m_t, m_sum, m_hi, m_lo = (sem(n) for n in ("m_sg", "m_t", "m_sum", "m_hi", "m_lo"))
        o_ev = sem("o_ev")
        s_silu, s_prod, s_hi, s_lo, f_ev = (sem(n) for n in ("s_silu", "s_prod", "s_hi", "s_lo", "f_ev"))
        gl, gmean, gxc, gsq, gss, gstd, grs, gvt, gv, gtr, gvn, gsp, gta, gtm, ghis, glos, gws = (sem(n) for n in (
            "g_gelu", "g_mean_mm", "g_xc", "g_sq", "g_ss", "g_std", "g_rs", "g_vt", "g_vdone", "g_tr", "g_vn",
            "g_sp", "g_ta", "g_tm", "g_his", "g_los", "g_ws"))
        gmd = sem("g_mean_done")
        m_r, m_rsq, m_rhi, m_rlo, m_dn = (sem(n) for n in ("m_relu", "m_rsq", "m_rhi", "m_rlo", "m_dn"))
        x_fl, x_lf, x_c, x_ini = (sem(n) for n in ("x_fl", "x_lf", "x_c", "x_ini"))
        x_lfv = sem("x_lfv")
        x_sq, x_ss, x_std, x_rs, x_qk, x_vt, x_vtr, x_vn, x_sg, x_s, x_mk, x_mx, x_p, x_rc, x_pn, x_pt, x_pe, x_o, x_og, x_hi, x_lo = (
            sem(n) for n in ("x_sq", "x_ss", "x_std", "x_rs", "x_qk", "x_vt", "x_vtr", "x_vn", "x_sg", "x_s", "x_mk",
                             "x_mx", "x_p", "x_rc", "x_pn", "x_pt", "x_pe", "x_o", "x_og", "x_hi", "x_lo"))

        def col(name, k=0, n=1, rows=P):
            return cols[0:rows, COLS[name] + k:COLS[name] + k + n]

        ACOL = {"mix_pre": 0, "ctx": 8, "mix_post": 16, "ffn_pre": 24, "ffn_post": 32}

        def adac(part, k, which=0):
            m = (part * KD + k) * 2 + which
            return ada[:, m:m + 1]

        def norm_of(name):
            if name == "ctx":
                return cxT, (lambda k: acol[:, 8 + k:9 + k]), (lambda k: adac(0, k, 1)), hch, hcl, CTX
            if name == "mix_pre":
                return xT, (lambda k: acol[:, k:k + 1]), (lambda k: adac(0, k)), hh, hl, L
            if name == "ffn_pre":
                return xT, (lambda k: acol[:, 24 + k:25 + k]), (lambda k: adac(3, k)), hh, hl, L
            if name == "mix_post":
                return mo, (lambda k: acol[:, 16 + k:17 + k]), None, None, None, L
            if name == "ffn_post":
                return ff_out, (lambda k: acol[:, 32 + k:33 + k]), None, None, None, L
            g, o = {"g_mix": ("mixn", 0), "mlp0": ("mlpn", 0), "fox": ("mixn", 8), "mlp1": ("mlpn", 8)}[name]
            return xT, (lambda k: col(g, o + k)), (lambda k: zcol[:, 0:1]), hh, hl, L

        PRE = [n for n in NORMS if n not in ("mix_post", "ffn_post")]
        POST = ["mix_post", "ffn_post"]
        TAIL = "dn1b"

        block = ctx.enter_context(nc.Block())

        @block.sync
        def _(sp):
            sp.dma_start(cols[:], a["cols"]).then_inc(d_cols, 16)
            sp.dma_start(zT[:], a["zT"]).then_inc(d_filt, 16)
            sp.dma_start(fw1[:], a["fw1"]).then_inc(d_filt, 16)
            sp.dma_start(fw2[:], a["fw2"]).then_inc(d_filt, 16)
            sp.dma_start(fw3[:], a["fw3"]).then_inc(d_filt2, 16)
            sp.dma_start(dec[:], a["decay"]).then_inc(d_filt2, 16)
            sp.dma_start(hb[:], a["hbias"]).then_inc(d_filt2, 16)
            sp.dma_start(C0[:], a["dft"][0]).then_inc(d_filt2, 16)
            sp.dma_start(S0[:], a["dft"][1]).then_inc(d_filt2, 16)
            for s in range(RING):
                sp.dma_start(raw[s][:], a["w"][s:s + 1].rearrange("o p k n -> p (o k) n")).then_inc(w_landed[s], 16)
            with sp.Fori(1, ADA_T // RING) as i:
                for s in range(RING):
                    sp.wait_ge(ada_used, i * RING + (s - RING + 1))
                    sp.dma_start(raw[s][:], a["w"][bass.ds(i * RING + s, 1)].rearrange("o p k n -> p (o k) n")).then_inc(w_landed[s], 16)
            for s in range(RING):
                sp.wait_ge(ada_used, ADA_T - RING + s + 1)
                sp.dma_start(raw[s][:], a["w"][ADA_T + s:ADA_T + s + 1].rearrange("o p k n -> p (o k) n")).then_inc(w_landed[s], 16)
            with sp.Fori(1, TILES // RING) as i:
                for s in range(RING):
                    sp.wait_ge(w_lo, i * RING + (s - RING + 1))
                    sp.dma_start(raw[s][:], a["w"][bass.ds(i * RING + (s + ADA_T), 1)].rearrange("o p k n -> p (o k) n")).then_inc(w_landed[s], 16)

        @block.gpsimd
        def _(g):
            g.memset(ones[:], 1.0)
            g.memset(ones_d[:], 1.0 / D)
            g.memset(ones_hd[:], 1.0 / P)
            g.memset(zcol[:], 0.0)
            g.memset(epsc[:, 0:1], EPS)
            g.memset(epsc[:, 1:2], LN_EPS)
            g.memset(blk64[:], 0.0).then_inc(consts, 1)
            g.wait_ge(consts, 1)
            g.memset(blk64[0:64, 0:64], 1.0 / 64)
            g.memset(blk64[64:128, 64:128], 1.0 / 64).then_inc(consts, 1)
            with g.Fori(0, TB["g_in"] // RING) as i:
                for s in range(RING):
                    g.wait_ge(w_hi, i * RING + (s + 1))
                    g.tensor_tensor(wlo[s][:], raw[s][:], whi[s][:].bitcast(F32), ALU.subtract).then_inc(w_lo, 1)
            g.wait_ge(d_ws, 32)
            g.affine_select(out=wsT[:], in_=wsT[:], compare_op=ALU.is_ge, fill=0.0, base=0,
                            pattern=[[0, 8], [1, P]], channel_multiplier=-1).then_inc(gws, 1)
            with g.Fori(TB["g_in"] // RING, TILES // RING) as i:
                for s in range(RING):
                    g.wait_ge(w_hi, i * RING + (s + 1))
                    g.tensor_tensor(wlo[s][:], raw[s][:], whi[s][:].bitcast(F32), ALU.subtract).then_inc(w_lo, 1)

        @block.scalar
        def _(act):
            A = nc.scalar.activation
            act.dma_start(xT[:], a["xT"]).then_inc(d_x, 16)
            act.dma_start(ident[:], a["ident"]).then_inc(d_x, 16)
            act.dma_start(rot[:], a["rot"]).then_inc(d_x, 16)
            act.dma_start(cmask[:], a["cmask"]).then_inc(d_x, 16)

            def one(ap):
                return ap.rearrange("p (o n) -> p o n", o=1)

            def hi_split(v, s, first=False):
                act.wait_ge(w_landed[s], v * 4 + (16 * (ADA_T // RING) + 16 - 4 * s))
                if not first:
                    act.wait_ge(w_used, v - (RING - 1))
                A(whi[s][:], raw[s][:], ACT.Copy).then_inc(w_hi, 1)

            def norm_act(name):
                n = NORMS.index(name)
                act.wait_ge(nm_sum, n * KD + KD)
                W = norm_of(name)[5]
                A(std[:, 0:W], aux[3][:, 0:W], ACT.Sqrt, bias=epsc[:, 0:1]).then_inc(nm_std, 1)

            def norm_apply_act(name):
                n = PRE.index(name)
                _, _, sh, hi_, _, W = norm_of(name)
                for k in range(KD):
                    act.wait_ge(nm_tmp, n * KD + k + 1)
                    A(hi_[:, k, :], tmp[k % 2][:, 0:W], ACT.Identity, bias=sh(k)).then_inc(h_hi, 1)

            act.wait_ge(d_cols, 16)
            A(csil[:], col("c", 0, 16), ACT.Silu).then_inc(c_silu, 1)
            for j in range(2):
                act.wait_ge(f_arg, j + 1)
                A(hd[0:64, :], tn[:], ACT.Sin).then_inc(f_sin, 1)
            act.wait_ge(lam_mm, 1)
            A(small[:, 0:2], acc[1][:, 0:2], ACT.Exp).then_inc(lam_exp, 1)
            for q in range(8):
                o, f = q // 4, q % 4
                act.wait_ge(g_mm, q + 1)
                A(Gr[o][:, f, :], aux[2 * (q % 2)][:], ACT.Copy, scale=1.0 / HY)
                A(Gs[o][:, f, :], aux[2 * (q % 2) + 1][:], ACT.Copy, scale=1.0 / HY).then_inc(g_used, 1)
            act.wait_ge(g_mm, 8)
            act.dma_start(Cm[:], a["dft"][2]).then_inc(d_dft, 16)
            act.dma_start(Sm[:], a["dft"][3]).then_inc(d_dft, 16)

            norm_act("mix_pre")
            hi_split(0, 0, True)
            hi_split(1, 1, True)
            norm_apply_act("mix_pre")

            for u in range(12):
                if u + 2 < RING:
                    hi_split(u + 2, u + 2, True)
                else:
                    hi_split(u + 2, (u + 2) % RING)
                act.wait_ge(w_used, u + 1)
                if u == 0:
                    act.wait_ge(hy_pad, 1)
                if u >= 2:
                    act.wait_ge(hy_conv, u - 1)
                A(pads[u % 2][:, 1:L + 1], acc[u % 4][:], ACT.Copy).then_inc(c_free, 1)
            for c in range(8):
                act.wait_ge(hy_tr, c + 1)
                dst = n0 if c < 4 else n1
                A(dst[:, :, (c % 4) * P:(c % 4 + 1) * P], aux[c % 2][:].rearrange("p (t n) -> p t n", t=NT), ACT.Copy).then_inc(hy_nat, 1)
            for c in range(HC):
                act.wait_ge(hy_z, c + 1)
                A(zhi[:, c, :], tmp[c % 2][:], ACT.Copy).then_inc(hy_zhi, 1)
            act.wait_ge(hy_zlo, HC)
            act.dma_start(cxT[:], a["ctxT"]).then_inc(d_att, 16)
            act.dma_start(cosT[:], a["rope"][0]).then_inc(d_att, 16)
            act.dma_start(sinT[:], a["rope"][1]).then_inc(d_att, 16)
            norm_act("ctx")
            norm_apply_act("ctx")

            def v_natural(h):
                act.wait_ge(v_tr, h + 1)
                A(vN[:, h, 0:4, :], aux[2][:].rearrange("p (t n) -> p t n", t=4), ACT.Copy)
                A(vN[:, h, 4:6, :], aux[3][:, 0:CTX].rearrange("p (t n) -> p t n", t=2), ACT.Copy).then_inc(v_nat, 1)

            for u in range(12):
                t = TB["qkv"] + u
                hi_split(t + 2, (t + 2) % RING)
                act.wait_ge(w_used, t + 1)
                if 2 <= u < 10:
                    act.wait_ge(q_done, u - 1)
                if u >= 10:
                    act.wait_ge(v_tr, u - 9)
                A(qe[:, u % 2, 0:L], acc[t % 4][:], ACT.Copy).then_inc(c_free, 1)
                if u >= 4:
                    A(kT[:, u - 4, L:NKEY] if u < 8 else qe[:, u % 2, L:NKEY], aux[u % 2][:, 0:CTX], ACT.Copy).then_inc(kv_ev, 1)
                if u >= 9:
                    v_natural(u - 9)
            v_natural(3)

            for h in range(HEADS):
                for qi in range(NT):
                    for m in range(2):
                        n = (h * NT + qi) * 2 + m
                        act.wait_ge(a_mx, n + 1)
                        A(pp[:, qi % 2, m, :], scores[m][:, 0:NKEY], ACT.Exp, bias=small[:, 8 + 4 * (n % 4):9 + 4 * (n % 4)], scale=0.125,
                          accum_out=small[:, 9 + 4 * (n % 4):10 + 4 * (n % 4)]).then_inc(a_p, 1)
                    act.wait_ge(a_tr, h * NT + qi + 1)
                    if qi == 0 and h >= 1:
                        act.wait_ge(a_o, h)
                    A(aT[:, 0:4, qi * P:(qi + 1) * P], trT[:, 0:L].rearrange("p (t n) -> p t n", t=4), ACT.Copy)
                    A(aT[:, 4:6, qi * P:(qi + 1) * P], trT[:, L:NKEY].rearrange("p (t n) -> p t n", t=2), ACT.Copy).then_inc(a_ev, 1)
                act.wait_ge(a_o, h + 1)
                A(sq[0][:], aux[2][:], ACT.Square).then_inc(a_sq, 1)
                act.wait_ge(a_ss, h + 1)
                A(std[:], aux[3][:], ACT.Sqrt, bias=epsc[:, 0:1]).then_inc(a_std, 1)
                act.wait_ge(a_tmp, h + 1)
                A(ohi[:, h, :], tmp[0][:], ACT.Copy).then_inc(a_hi, 1)

            with act.Fori(0, 2) as i:
                for jj in range(4):
                    t = i * 12 + (TB["mix"] + 3 * jj)
                    hi_split(t + 2, (3 * jj + 2) % RING)
                    act.wait_ge(w_used, t + 1)
                    A(sgm[:, jj % 2, 0, :], acc[0][:], ACT.Sigmoid)
                    hi_split(t + 3, (3 * jj + 3) % RING)
                    act.wait_ge(w_used, t + 2)
                    A(sgm[:, jj % 2, 1, :], acc[1][:], ACT.Sigmoid).then_inc(m_sg, 1)
                    hi_split(t + 4, (3 * jj + 4) % RING)
                    act.wait_ge(m_sum, i * 4 + (jj + 1))
                    A(mxh[:, bass.ds(i * 4 + jj, 1), :], one(mt[:, jj % 2, 0, :]), ACT.Copy).then_inc(m_hi, 1)

            for u in range(8):
                t = TB["wout"] + u
                hi_split(t + 2, (t + 2) % RING)
            norm_act("mix_post")
            norm_act("ffn_pre")
            norm_apply_act("ffn_pre")

            with act.Fori(0, FC // 2) as i:
                for s in range(RING):
                    v = i * RING + (TB["gateup"] + s)
                    p = s // 2
                    hi_split(v + 2, (s + 2) % RING)
                    if s % 2 == 0:
                        act.wait_ge(w_used, v + 1)
                        A(sil[:, p, :], acc[s][:], ACT.Silu).then_inc(s_silu, 1)
                    else:
                        act.wait_ge(c_free, i * RING + (CB["gateup"] + s + 1))
                        A(hidh[:, bass.ds(i * 2 + p, 1), :], one(tmp[p][:]), ACT.Copy).then_inc(s_hi, 1)
            for v in range(TB["down"], TB["down"] + 24):
                hi_split(v + 2, (v + 2) % RING)
            norm_act("ffn_post")
            act.dma_start(wsT[:], a["ws"]).then_inc(d_ws, 16)
            act.dma_start(bsb[:], a["bs"]).then_inc(d_ws, 16)
            norm_act("g_mix")
            norm_apply_act("g_mix")

            with act.Fori(0, 4) as i:
                for s in range(RING):
                    v = i * RING + (TB["g_in"] + s)
                    hi_split(v + 2, (s + 2) % RING)
                    act.wait_ge(w_used, v + 1)
                    A(vT[:, bass.ds(i * 4 + s, 1), :], acc[s][:].rearrange("p (o n) -> p o n", o=1), ACT.Gelu_apprx_tanh).then_inc(c_free, 1)
            act.wait_ge(gmean, 1)
            A(mean[:], aux[0][:], ACT.Copy, scale=0.5).then_inc(gmd, 1)
            with act.Fori(0, 4) as i:
                for s in range(RING):
                    v = i * RING + (TB["g_in"] + 16 + s)
                    hi_split(v + 2, (s + 2) % RING)
                    act.wait_ge(w_used, v + 1)
                    A(guT[:, bass.ds(i * 4 + s, 1), :], acc[s][:].rearrange("p (o n) -> p o n", o=1), ACT.Gelu_apprx_tanh).then_inc(c_free, 1)
            for c in range(16):
                act.wait_ge(gxc, c + 1)
                if c >= 2:
                    act.wait_ge(gss, c - 1)
                A(sq[c % 2][:], vT[:, c, :], ACT.Square).then_inc(gsq, 1)
            act.wait_ge(gss, 16)
            A(std[:], aux[1][:], ACT.Sqrt, bias=epsc[:, 1:2], scale=0.5).then_inc(gstd, 1)
            for c in range(16):
                act.wait_ge(gvt, c + 1)
                A(vT[:, c, :], vT[:, c, :], ACT.Identity, bias=col("ln_b", c)).then_inc(gv, 1)
            for c in range(16):
                act.wait_ge(gtr, c + 1)
                if c >= 2:
                    act.wait_ge(gsp, c - 1)
                A(vn[:, c % 2, :], aux[c % 2][:], ACT.Copy).then_inc(gvn, 1)
                if c >= 1:
                    act.wait_ge(gtm, c)
                    A(ghi[:, c - 1, :], gt[:, (c - 1) % 2, 1, :], ACT.Copy).then_inc(ghis, 1)
            act.wait_ge(gtm, 16)
            A(ghi[:, 15, :], gt[:, 1, 1, :], ACT.Copy).then_inc(ghis, 1)
            for v in range(TB["g_out"], TB["g_out"] + 16):
                hi_split(v + 2, (v + 2) % RING)

            def mlp_up(i, base, nbase):
                for s in range(RING):
                    v = i * RING + (base + s)
                    hi_split(v + 2, (s + 2) % RING)
                    act.wait_ge(w_used, v + 1)
                    A(sq[s % 2][:], acc[s][:], ACT.Relu).then_inc(c_free, 1)
                    act.wait_ge(m_rsq, i * RING + (nbase + s + 1))
                    A(mh[:, bass.ds(i * 4 + s, 1), :], tmp[s % 2][:].rearrange("p (o n) -> p o n", o=1), ACT.Copy).then_inc(m_rhi, 1)

            def mlp(layer, last):
                for half in range(2):
                    n = layer * 2 + half
                    with act.Fori(0, 4) as i:
                        mlp_up(i, TB[f"up{layer}{'ab'[half]}"], n * 16)
                    b = TB[f"dn{layer}{'ab'[half]}"]
                    for v in range(b, b + 16):
                        if v + 2 < TILES:
                            hi_split(v + 2, (v + 2) % RING)

            norm_act("mlp0")
            norm_apply_act("mlp0")
            mlp(0, False)

            norm_act("fox")
            norm_apply_act("fox")
            act.dma_start(wf[:], a["wf"]).then_inc(d_wf, 16)
            act.wait_ge(x_fl, 1)
            A(lf[:, 0, :], aux[0][0:16, :], ACT.Identity, bias=col("b_f", rows=16)).then_inc(x_lf, 1)
            act.wait_ge(x_lf, 1)
            A(lf[:, 1, :], lf[:, 0, :], ACT.Abs).then_inc(x_lf, 1)
            act.wait_ge(x_lf, 2)
            A(lf[:, 2, :], lf[:, 1, :], ACT.Exp, scale=-1.0).then_inc(x_lf, 1)
            act.wait_ge(x_lf, 3)
            A(lf[:, 1, :], lf[:, 2, :], ACT.Ln, bias=ones[0:16, 0:1]).then_inc(x_lf, 1)
            act.wait_ge(x_c, 2)
            act.dma_start(a["scratch"][0], cpos[:]).then_inc(d_c, 16)
            act.dma_start(a["scratch"][1], cneg[:]).then_inc(d_c, 16)
            act.wait_ge(d_c, 32)
            act.wait_ge(x_ini, 2)

            with act.Fori(0, 8) as i:
                for e in range(2):
                    act.dma_start(qa[65:66, e, :], a["scratch"][0, bass.ds(i * 2 + e, 1), :]).then_inc(d_crow, 16)
                    act.dma_start(ka[64:65, e, :], a["scratch"][1, bass.ds(i * 2 + e, 1), :]).then_inc(d_crow, 16)
                for s in range(RING):
                    v = i * RING + (TB["fox"] + s)
                    hi_split(v + 2, (s + 2) % RING)
                    act.wait_ge(w_used, v + 1)
                    if s < 2:
                        A(fsq[:, s, :], acc[s][:], ACT.Square).then_inc(x_sq, 1)
                        act.wait_ge(x_ss, i * 2 + (s + 1))
                        act.wait_ge(x_rs, i * 2 + s) if s else None
                        A(std[:], aux[3][:], ACT.Sqrt, bias=epsc[:, 0:1]).then_inc(x_std, 1)
                    elif s == 2:
                        A(fvT[:], acc[2][:], ACT.Copy).then_inc(x_vt, 1)
                        act.wait_ge(x_vtr, i + 1)
                        A(fvn[:], aux[3][:].rearrange("p (t n) -> p t n", t=NT), ACT.Copy).then_inc(x_vn, 1)
                    else:
                        A(fsg[:], acc[3][:], ACT.Sigmoid).then_inc(x_sg, 1)
                for e in range(2):
                    for qi in range(NT):
                        n = e * 4 + qi
                        W = (qi + 1) * P
                        act.wait_ge(x_mx, i * 8 + (n + 1))
                        A(fp[:, qi % 2, 0:W], aux[qi % 2][:, 0:W], ACT.Exp, bias=small[:, 40 + n:41 + n],
                          accum_out=small[:, 48 + n:49 + n]).then_inc(x_p, 1)
                        act.wait_ge(x_pt, i * 8 + (n + 1))
                        if qi == 0 and e == 1:
                            act.wait_ge(x_o, i * 2 + 1)
                        A(fpT[:, 0:qi + 1, qi * P:(qi + 1) * P], aux[2][:, 0:W].rearrange("p (t n) -> p t n", n=P), ACT.Copy).then_inc(x_pe, 1)
                act.wait_ge(x_og, i + 2)
                A(foh[:, bass.ds(i, 1), :], tmp[0][:].rearrange("p (o n) -> p o n", o=1), ACT.Copy).then_inc(x_hi, 1)
            for v in range(TB["fox_out"], TB["fox_out"] + 8):
                hi_split(v + 2, (v + 2) % RING)
            norm_act("mlp1")
            norm_apply_act("mlp1")
            mlp(1, True)
            for k in range(KD):
                act.wait_ge(c_free, CB["dn1b"] + k + 1)
                act.dma_start(a["out"][:, k, :], xT[:, k, :]).then_inc(d_out, 16)
            act.wait_ge(d_out, 16 * KD)

        @block.tensor
        def _(pe):
            mm = nc.tensor.matmul

            def tile(v, s, bank_, xh, xl, blocks=8, start=True, stop=True, last=True, first_block=0, free=None):
                pe.wait_ge(w_lo, v + 1)
                if free is not None:
                    pe.wait_ge(c_free, free)
                for k in range(blocks):
                    b = first_block + k
                    m1 = mm(bank_, whi[s][:, b, :], xh[k], start=start and k == 0, stop=False)
                    mm(bank_, whi[s][:, b, :], xl[k], start=False, stop=False)
                    m1 = mm(bank_, wlo[s][:, b, :], xh[k], start=False, stop=stop and k == blocks - 1)
                if last:
                    m1.then_inc(w_used, 1)

            def chunks(t, n0, n1):
                return [t[:, k, :] for k in range(n0, n1)]

            def norm_pe(name):
                n = NORMS.index(name)
                W = norm_of(name)[5]
                for k in range(KD):
                    pe.wait_ge(nm_sq, n * KD + k + 1)
                    mm(aux[3][:, 0:W], ones_d[:], sq[k % 2][:, 0:W], start=k == 0, stop=k == KD - 1).then_inc(nm_sum, 1)

            H = (chunks(hh, 0, KD), chunks(hl, 0, KD))

            pe.wait_ge(d_filt, 48)
            mm(aux[0][0:64, :], fw1[:], zT[:], start=True, stop=True).then_inc(f_mm, 1)
            pe.wait_ge(consts, 2)
            pe.wait_ge(lam_prod, 1)
            mm(acc[1][:, 0:2], ones[0:64, :], small[0:64, 4:6], start=True, stop=True).then_inc(lam_mm, 1)
            pe.wait_ge(f_sin, 1)
            mm(aux[1][0:64, :], fw2[:], hd[0:64, :], start=True, stop=True).then_inc(f_mm, 1)
            pe.wait_ge(f_sin, 2)
            pe.wait_ge(d_filt2, 80)
            for p in range(8):
                o, t = p // 4, p % 4
                if p >= 2:
                    pe.wait_ge(f_dec, p - 1)
                for d in range(2):
                    m1 = mm(aux[2 * (p % 2) + d][:], hd[0:65, t * P:(t + 1) * P], fw3[:, (2 * o + d) * HY:(2 * o + d + 1) * HY],
                            start=True, stop=True)
                m1.then_inc(f_ab, 1)
            pe.wait_ge(f_eo, 8)
            for q in range(8):
                o, f = q // 4, q % 4
                if q >= 2:
                    pe.wait_ge(g_used, q - 1)
                for r, (mat, src) in enumerate(((C0, fE), (S0, fO))):
                    for t in range(NT):
                        m1 = mm(aux[2 * (q % 2) + r][:], mat[:, t, f * P:(f + 1) * P], src[:, t, o * HY:(o + 1) * HY],
                                start=t == 0, stop=t == NT - 1)
                m1.then_inc(g_mm, 1)

            pe.wait_ge(c_silu, 1)
            with pe.Fori(0, ADA_T // RING) as i:
                for s in range(RING):
                    pe.wait_ge(w_landed[s], i * 16 + 16)
                    for k in range(KD):
                        m1 = mm(acc[0][:, bass.ds(i * 8 + 2 * s, 2)], raw[s][:, k, :], csil[:, 2 * k:2 * k + 2],
                                start=k == 0, stop=k == KD - 1)
                    m1.then_inc(ada_used, 1)

            pe.wait_ge(g_used, 8)
            norm_pe("mix_pre")
            pe.wait_ge(h_lo, KD)

            pe.wait_ge(c_free, RING)
            for u in range(12):
                tile(u, u % 4, acc[u % 4][:], *H, free=CB["hyena"] + u - 3)
            pe.wait_ge(d_x, 64)
            for c in range(8):
                pe.wait_ge(hy_conv, c + 1)
                if c >= 2:
                    pe.wait_ge(hy_nat, c - 1)
                for t in range(NT):
                    m1 = nc.tensor.transpose(aux[c % 2][:, t * P:(t + 1) * P], uT[:, c, t * P:(t + 1) * P], ident[:])
                m1.then_inc(hy_tr, 1)
            pe.wait_ge(hy_nat, 8)
            pe.wait_ge(d_dft, 32)
            pe.wait_ge(c_free, CB["qkv"])
            for o in range(2):
                if o:
                    pe.wait_ge(hy_yd, NT)
                for f in range(4):
                    if o * 4 + f >= 2:
                        pe.wait_ge(hy_pw, o * 4 + f - 1)
                    for r, mat in enumerate((Cm, Sm)):
                        for t in range(NT):
                            m1 = mm(aux[2 * (f % 2) + r][:], mat[:, t, f * P:(f + 1) * P], n0[:, t, :],
                                    start=t == 0, stop=t == NT - 1)
                    m1.then_inc(hy_u, 1)
                pe.wait_ge(hy_y, o * 4 + 4)
                for t in range(NT):
                    for r, (mat, y) in enumerate(((Cm, Gr[o]), (Sm, Gs[o]))):
                        for f in range(4):
                            lhs, rhs = (mat, y) if o == 0 else (y, mat)
                            m1 = mm(acc[t][:], lhs[:, f, t * P:(t + 1) * P], rhs[:, f, :],
                                    start=(r == 0 and f == 0), stop=(r == 1 and f == 3))
                    m1.then_inc(hy_inv, 1)

            norm_pe("ctx")
            pe.wait_ge(h_lo, 2 * KD)
            pe.wait_ge(hy_z, HC)

            def rotate(u):
                pe.wait_ge(c_free, CB["qkv"] + u + 1)
                if u:
                    pe.wait_ge(q_done, u)
                mm(aux[2][:], rot[:], qe[:, u % 2, 0:L], start=True, stop=True).then_inc(q_rot, 1)

            def v_transposes(h):
                pe.wait_ge(c_free, CB["qkv"] + h + 9)
                pe.wait_ge(kv_ev, h + 5)
                if h == 0:
                    pe.wait_ge(q_done, 8)
                else:
                    pe.wait_ge(v_nat, h)
                for t in range(KT):
                    b = aux[2] if t < 4 else aux[3]
                    m1 = nc.tensor.transpose(b[:, (t % 4) * P:(t % 4 + 1) * P], qe[:, h % 2, t * P:(t + 1) * P], ident[:])
                m1.then_inc(v_tr, 1)

            for u in range(12):
                v = TB["qkv"] + u
                tile(v, v % 4, acc[v % 4][:], *H, free=CB["qkv"] + u - 3, last=u < 4)
                if u >= 4:
                    if u >= 6:
                        pe.wait_ge(kv_ev, u - 5)
                    for k in range(KD):
                        b = aux[u % 2][:, 0:CTX]
                        mm(b, whi[v % 4][:, k, :], hch[:, k, :], start=k == 0, stop=False)
                        mm(b, whi[v % 4][:, k, :], hcl[:, k, :], start=False, stop=False)
                        m1 = mm(b, wlo[v % 4][:, k, :], hch[:, k, :], start=False, stop=k == KD - 1)
                    m1.then_inc(w_used, 1)
                if 1 <= u < 9:
                    rotate(u - 1)
                if u >= 9:
                    v_transposes(u - 9)
            v_transposes(3)

            pe.wait_ge(c_free, CB["mix"])
            pe.wait_ge(kv_ev, 8)
            pe.wait_ge(q_done, 8)
            pe.wait_ge(v_nat, 4)
            for h in range(HEADS):
                def score(qi):
                    for m in range(2):
                        n = (h * NT + qi) * 2 + m
                        if n >= 2:
                            pe.wait_ge(a_p, n - 1)
                        r = slice(64 * m, 64 * m + 64)
                        mm(scores[m][:, 0:L], qT[r, h, qi * P:(qi + 1) * P], kT[r, h, 0:L], start=True, stop=True)
                        mm(scores[m][:, L:NKEY], qT[r, h, qi * P:(qi + 1) * P], kT[r, h, L:NKEY], start=True, stop=True).then_inc(a_s, 1)

                def weights_t(qi):
                    n = h * NT + qi
                    pe.wait_ge(a_cm, n + 1)
                    if n:
                        pe.wait_ge(a_ev, n)
                    for t in range(KT):
                        m1 = nc.tensor.transpose(trT[:, t * P:(t + 1) * P], pp[:, qi % 2, 0, t * P:(t + 1) * P], ident[:])
                    m1.then_inc(a_tr, 1)

                for qi in range(NT):
                    score(qi)
                    if qi:
                        weights_t(qi - 1)
                weights_t(NT - 1)
                pe.wait_ge(a_ev, h * NT + NT)
                if h:
                    pe.wait_ge(a_tmp, h)
                for t in range(KT):
                    m1 = mm(aux[2][:], vN[:, h, t, :], aT[:, t, :], start=t == 0, stop=t == KT - 1)
                m1.then_inc(a_o, 1)
                pe.wait_ge(a_sq, h + 1)
                mm(aux[3][:], ones_hd[:], sq[0][:], start=True, stop=True).then_inc(a_ss, 1)

            pe.wait_ge(a_lo, HEADS)
            with pe.Fori(0, 2) as i:
                for jj in range(4):
                    v = i * 12 + (TB["mix"] + 3 * jj)
                    c = i * 16 + (CB["mix"] + 4 * jj)
                    tile(v, (3 * jj) % 4, acc[0][:], *H, free=c - 3)
                    tile(v + 1, (3 * jj + 1) % 4, acc[1][:], *H)
                    s = (3 * jj + 2) % 4
                    tile(v + 2, s, acc[2][:], chunks(zhi, 0, 4), chunks(zlo, 0, 4), blocks=4, last=False)
                    tile(v + 2, s, acc[3][:], chunks(ohi, 0, 4), chunks(olo, 0, 4), blocks=4, first_block=4)

            pe.wait_ge(c_free, CB["wout"])
            pe.wait_ge(m_lo, KD)
            with pe.Fori(0, 2) as i:
                for s in range(4):
                    tile(i * 4 + (TB["wout"] + s), s, acc[s][:], chunks(mxh, 0, KD), chunks(mxl, 0, KD), free=i * 4 + (CB["wout"] + s - 3))
            norm_pe("mix_post")
            norm_pe("ffn_pre")
            pe.wait_ge(h_lo, 3 * KD)
            pe.wait_ge(c_free, CB["gateup"])
            with pe.Fori(0, FC // 2) as i:
                for s in range(4):
                    tile(i * 4 + (TB["gateup"] + s), s, acc[s][:], *H, free=i * 4 + (CB["gateup"] + s - 3))
            pe.wait_ge(c_free, CB["down"])
            pe.wait_ge(s_lo, FC)
            with pe.Fori(0, 2) as i:
                for cc in range(4):
                    for part in range(3):
                        n0_, n1_ = 8 * part, min(8 * part + 8, FC)
                        s = (3 * cc + part) % 4
                        tile(i * 12 + (TB["down"] + 3 * cc + part), s, acc[cc][:], chunks(hidh, n0_, n1_), chunks(hidl, n0_, n1_),
                             blocks=n1_ - n0_, start=part == 0, stop=part == 2,
                             free=i * 4 + (CB["down"] + cc - 3) if part == 0 else None)
            norm_pe("ffn_post")
            norm_pe("g_mix")
            pe.wait_ge(h_lo, 4 * KD)
            pe.wait_ge(c_free, CB["g_in"])

            def g_in(first):
                with pe.Fori(0, 4) as i:
                    for s in range(4):
                        tile(i * 4 + (TB["g_in"] + first + s), s, acc[s][:], *H, free=i * 4 + (CB["g_in"] + first + s - 3))
            g_in(0)
            pe.wait_ge(c_free, CB["g_in"] + 16)
            for c in range(16):
                m1 = mm(aux[0][:], ones_d[:], vT[:, c, :], start=c == 0, stop=c == 15)
            m1.then_inc(gmean, 1)
            g_in(16)
            for c in range(16):
                pe.wait_ge(gsq, c + 1)
                mm(aux[1][:], ones_d[:], sq[c % 2][:], start=c == 0, stop=c == 15).then_inc(gss, 1)
            pe.wait_ge(c_free, CB["g_out"])
            pe.wait_ge(gws, 1)
            pe.wait_ge(gstd, 1)

            def spatial(c):
                pe.wait_ge(gvn, c + 1)
                if c >= 4:
                    pe.wait_ge(gta, c - 3)
                for t in range(NT):
                    m1 = mm(acc[c % 4][:, t * P:(t + 1) * P], vn[:, c % 2, t * P:(t + 1) * P], wsT[:, c // 2, :], start=True, stop=True)
                m1.then_inc(gsp, 1)
            for c in range(16):
                pe.wait_ge(gv, c + 1)
                if c >= 2:
                    pe.wait_ge(gvn, c - 1)
                for t in range(NT):
                    m1 = nc.tensor.transpose(aux[c % 2][:, t * P:(t + 1) * P], vT[:, c, t * P:(t + 1) * P], ident[:])
                m1.then_inc(gtr, 1)
                if c:
                    spatial(c - 1)
            spatial(15)
            pe.wait_ge(gta, 16)
            pe.wait_ge(glos, 16)

            def wide(name, xh, xl):
                with pe.Fori(0, 2) as i:
                    for cc in range(4):
                        for part in range(2):
                            tile(i * 8 + (TB[name] + 2 * cc + part), (2 * cc + part) % 4, acc[cc][:], chunks(xh, 8 * part, 8 * part + 8),
                                 chunks(xl, 8 * part, 8 * part + 8), start=part == 0, stop=part == 1,
                                 free=i * 4 + (CB[name] + cc - 3) if part == 0 else None)
            wide("g_out", ghi, glo)

            def mlp(layer):
                for half in range(2):
                    up, dn = f"up{layer}{'ab'[half]}", f"dn{layer}{'ab'[half]}"
                    pe.wait_ge(c_free, CB[up])
                    with pe.Fori(0, 4) as i:
                        for s in range(4):
                            tile(i * 4 + (TB[up] + s), s, acc[s][:], *H, free=i * 4 + (CB[up] + s - 3))
                    pe.wait_ge(c_free, CB[dn])
                    pe.wait_ge(m_rlo, 16 * (layer * 2 + half + 1))
                    wide(dn, mh, ml)
            norm_pe("mlp0")
            pe.wait_ge(h_lo, 5 * KD)
            mlp(0)

            norm_pe("fox")
            pe.wait_ge(h_lo, 6 * KD)
            pe.wait_ge(d_wf, 16)
            for part in (hh, hl):
                for k in range(KD):
                    m1 = mm(aux[0][0:16, :], wf[:, k, :], part[:, k, :].bitcast(F32), start=part is hh and k == 0, stop=part is hl and k == KD - 1)
            m1.then_inc(x_fl, 1)
            pe.wait_ge(c_free, CB["fox"])
            pe.wait_ge(x_lf, 1)
            with pe.Fori(0, 8) as i:
                def project(s):
                    tile(i * 4 + (TB["fox"] + s), s, acc[s][:], *H, free=i * 4 + (CB["fox"] + s - 3))

                project(0)
                for s in range(2):
                    project(s + 1)
                    pe.wait_ge(x_sq, i * 2 + (s + 1))
                    if s == 0:
                        pe.wait_ge(x_og, i + 1)
                    else:
                        pe.wait_ge(x_std, i * 2 + 1)
                    mm(aux[3][:], blk64[:], fsq[:, s, :], start=True, stop=True).then_inc(x_ss, 1)
                project(3)
                pe.wait_ge(x_vt, i + 1)
                pe.wait_ge(x_std, i * 2 + 2)
                for t in range(NT):
                    m1 = nc.tensor.transpose(aux[3][:, t * P:(t + 1) * P], fvT[:, t * P:(t + 1) * P], ident[:])
                m1.then_inc(x_vtr, 1)
                pe.wait_ge(x_qk, i * 2 + 2)
                pe.wait_ge(d_crow, i * 64 + 64)

                def score(n):
                    e, qi = n // 4, n % 4
                    pe.wait_ge(x_p, i * 8 + (n + 7 if False else n - 1)) if n >= 2 else None
                    mm(aux[qi % 2][:, 0:(qi + 1) * P], qa[:, e, qi * P:(qi + 1) * P], ka[:, e, 0:(qi + 1) * P],
                       start=True, stop=True).then_inc(x_s, 1)

                def weights_t(n):
                    e, qi = n // 4, n % 4
                    pe.wait_ge(x_pn, i * 8 + (n + 1))
                    if n:
                        pe.wait_ge(x_pe, i * 8 + n)
                    for t in range(qi + 1):
                        m1 = nc.tensor.transpose(aux[2][:, t * P:(t + 1) * P], fp[:, qi % 2, t * P:(t + 1) * P], ident[:])
                    m1.then_inc(x_pt, 1)

                def out(e):
                    pe.wait_ge(x_pe, i * 8 + (4 * e + 4))
                    if e == 0:
                        pe.wait_ge(x_vn, i + 1)
                    r = slice(64 * e, 64 * e + 64)
                    for t in range(NT):
                        m1 = mm(aux[3][r, t * P:L], fvn[:, t, r], fpT[:, t, t * P:L], start=t == 0, stop=t == NT - 1)
                    m1.then_inc(x_o, 1)

                for n in range(8):
                    score(n)
                    if n:
                        weights_t(n - 1)
                    if n == 4:
                        out(0)
                weights_t(7)
                out(1)
            pe.wait_ge(c_free, CB["fox_out"])
            pe.wait_ge(x_lo, KD)
            with pe.Fori(0, 2) as i:
                for s in range(4):
                    tile(i * 4 + (TB["fox_out"] + s), s, acc[s][:], chunks(foh, 0, KD), chunks(fol, 0, KD), free=i * 4 + (CB["fox_out"] + s - 3))
            norm_pe("mlp1")
            pe.wait_ge(h_lo, 7 * KD)
            mlp(1)

        @block.vector
        def _(v):
            V = nc.vector
            TT = V.tensor_tensor
            STT = V.scalar_tensor_tensor
            step = [0]

            def then(ins):
                step[0] += 1
                ins.then_inc(v_step, 1)
                v.wait_ge(v_step, step[0])

            def one(ap):
                return ap.rearrange("p (o n) -> p o n", o=1)

            def norm_dve(name):
                n = NORMS.index(name)
                src, W = norm_of(name)[0], norm_of(name)[5]
                for k in range(KD):
                    if k >= 2:
                        v.wait_ge(nm_sum, n * KD + k - 1)
                    TT(sq[k % 2][:, 0:W], src[:, k, 0:W], src[:, k, 0:W], ALU.mult).then_inc(nm_sq, 1)
                v.wait_ge(nm_std, n + 1)
                then(V.reciprocal(rstd[:, 0:W], std[:, 0:W]))

            def norm_apply(name):
                n = PRE.index(name)
                src, g, sh, hi_, lo_, W = norm_of(name)

                def lo_of(k):
                    v.wait_ge(h_hi, n * KD + k + 1)
                    STT(out=lo_[:, k, :], in0=tmp[k % 2][:, 0:W], scalar=sh(k), in1=hi_[:, k, :].bitcast(F32), op0=ALU.add,
                        op1=ALU.subtract).then_inc(h_lo, 1)
                for k in range(KD):
                    if k >= 2:
                        lo_of(k - 2)
                        v.wait_ge(h_lo, n * KD + k - 1)
                    STT(out=tmp[k % 2][:, 0:W], in0=src[:, k, :], scalar=g(k), in1=rstd[:, 0:W], op0=ALU.mult, op1=ALU.mult).then_inc(nm_tmp, 1)
                lo_of(KD - 2)
                lo_of(KD - 1)
                v.wait_ge(h_lo, n * KD + KD)

            def residual(name):
                src, g = norm_of(name)[0:2]
                for k in range(KD):
                    then(STT(out=tmp[k % 2][:], in0=src[:, k, :], scalar=g(k), in1=rstd[:], op0=ALU.mult, op1=ALU.mult))
                    m1 = TT(xT[:, k, :], xT[:, k, :], tmp[k % 2][:], ALU.add)
                    if k == KD - 1:
                        then(m1)

            V.memset(hd[64:65, :], 1.0)
            V.memset(pad0[:, 0:1], 0.0)
            V.memset(pad0[:, L + 1:L + 2], 0.0)
            V.memset(pad1[:, 0:1], 0.0)
            V.memset(pad1[:, L + 1:L + 2], 0.0).then_inc(hy_pad, 1)
            v.wait_ge(d_cols, 16)
            TT(small[0:64, 4:6], col("lam_q", 0, 2, 64), col("lam_k", 0, 2, 64), ALU.mult).then_inc(lam_prod, 1)
            TT(small[:, 6:7], col("subln"), col("subln"), ALU.bypass) if False else None
            V.tensor_scalar(small[:, 6:7], col("subln"), 1.0 - LAM_INIT, None, ALU.mult)
            V.tensor_scalar(small[:, 7:8], col("q_g"), 0.125, None, ALU.mult)
            for j in range(2):
                v.wait_ge(f_mm, j + 1)
                then(V.tensor_scalar(targ[:], aux[j][0:64, :], col(("fb1", "fb2")[j], rows=64), col("freq", rows=64), ALU.add, ALU.mult))
                then(V.tensor_scalar(tn[:], targ[:], 1.0 / (2 * math.pi), MAGIC, ALU.mult, ALU.add))
                then(V.tensor_scalar(tn[:], tn[:], -MAGIC, None, ALU.add))
                then(STT(out=targ[:], in0=tn[:], scalar=-6.28125, in1=targ[:], op0=ALU.mult, op1=ALU.add))
                then(STT(out=targ[:], in0=tn[:], scalar=-(2 * math.pi - 6.28125), in1=targ[:], op0=ALU.mult, op1=ALU.add))
                V.tensor_scalar(tn[:], targ[:], 3.1415925, -3.1415925, ALU.min, ALU.max).then_inc(f_arg, 1)
            v.wait_ge(lam_exp, 1)
            then(TT(small[:, 2:3], small[:, 1:2], small[:, 0:1], ALU.subtract))
            then(V.tensor_scalar(small[:, 3:4], small[:, 2:3], -LAM_INIT, None, ALU.add))
            v.wait_ge(d_filt2, 80)
            for p in range(8):
                o, t = p // 4, p % 4
                v.wait_ge(f_ab, p + 1)
                TT(fab[:, p % 2, 0, :], aux[2 * (p % 2)][:], dec[:, t, :], ALU.mult)
                m1 = TT(fab[:, p % 2, 1, :], aux[2 * (p % 2) + 1][:], dec[:, 4 if t == 0 else t, :], ALU.mult)
                m1.then_inc(f_dec, 1)
                v.wait_ge(f_dec, p + 1)
                TT(fO[:, t, o * HY:(o + 1) * HY], fab[:, p % 2, 0, :], fab[:, p % 2, 1, :], ALU.subtract)
                m1 = TT(fE[:, t, o * HY:(o + 1) * HY], fab[:, p % 2, 0, :], fab[:, p % 2, 1, :], ALU.add)
                if t == 0:
                    then(m1)
                    m1 = TT(fE[0:1, 0, o * HY:(o + 1) * HY], fE[0:1, 0, o * HY:(o + 1) * HY], hb[:, o, :], ALU.add)
                m1.then_inc(f_eo, 1)

            v.wait_ge(ada_used, ADA_T)
            m1 = TT(ada[:], acc[0][:, 0:2 * ADA_T], col("b_ada", 0, 96), ALU.add)
            m1.then_inc(c_free, RING)
            v.wait_ge(c_free, RING)
            am = ada[:].rearrange("p (m w) -> p m w", w=2)
            STT(out=acol[:, 0:8], in0=am[:, 8:16, 0], scalar=1.0, in1=col("g_mix_pre", 0, 8), op0=ALU.add, op1=ALU.mult)
            STT(out=acol[:, 8:16], in0=am[:, 8:16, 1], scalar=1.0, in1=col("g_mix_pre", 0, 8), op0=ALU.add, op1=ALU.mult)
            TT(acol[:, 16:24], am[:, 16:24, 0], col("g_mix_post", 0, 8), ALU.mult)
            STT(out=acol[:, 24:32], in0=am[:, 32:40, 0], scalar=1.0, in1=col("g_ffn_pre", 0, 8), op0=ALU.add, op1=ALU.mult)
            then(TT(acol[:, 32:40], am[:, 40:48, 0], col("g_ffn_post", 0, 8), ALU.mult))
            v.wait_ge(d_x, 64)
            v.wait_ge(consts, 2)
            norm_dve("mix_pre")
            norm_apply("mix_pre")

            for u in range(12):
                v.wait_ge(c_free, CB["hyena"] + u + 1)
                p = pads[u % 2]
                dst = uT[:, u, :] if u < 8 else x2T[:, u - 8, :]
                w = lambda tap: col("conv_w", tap * 12 + u)
                then(V.tensor_scalar(tmp[0][:], p[:, 0:L], w(0), col("conv_b", u), ALU.mult, ALU.add))
                then(STT(out=tmp[1][:], in0=p[:, 1:L + 1], scalar=w(1), in1=tmp[0][:], op0=ALU.mult, op1=ALU.add))
                STT(out=dst, in0=p[:, 2:L + 2], scalar=w(2), in1=tmp[1][:], op0=ALU.mult, op1=ALU.add).then_inc(hy_conv, 1)
            v.wait_ge(hy_nat, 8)

            def z_lo(c):
                v.wait_ge(hy_zhi, c + 1)
                TT(zlo[:, c, :], tmp[c % 2][:], zhi[:, c, :].bitcast(F32), ALU.subtract).then_inc(hy_zlo, 1)
            for o in range(2):
                for f in range(4):
                    v.wait_ge(hy_u, o * 4 + f + 1)
                    uc, us = aux[2 * (f % 2)][:], aux[2 * (f % 2) + 1][:]
                    gr, gs = Gr[o][:, f, :], Gs[o][:, f, :]
                    t = [pw[:, f % 2, n, :] for n in range(4)]
                    TT(t[0], gr, uc, ALU.mult)
                    TT(t[1], gs, us, ALU.mult)
                    TT(t[2], gs, uc, ALU.mult)
                    TT(t[3], gr, us, ALU.mult).then_inc(hy_pw, 1)
                    v.wait_ge(hy_pw, o * 4 + f + 1)
                    TT(gr, t[0], t[1], ALU.subtract)
                    TT(gs, t[2], t[3], ALU.add).then_inc(hy_y, 1)
                for t in range(NT):
                    v.wait_ge(hy_inv, o * 4 + t + 1)
                    if o == 0:
                        TT(n0[:, t, :], acc[t][:], n1[:, t, :], ALU.mult).then_inc(hy_yd, 1)
                    else:
                        if t >= 2:
                            z_lo(t - 2)
                            v.wait_ge(hy_zlo, t - 1)
                        TT(tmp[t % 2][:], acc[t][:], x2T[:, t, :], ALU.mult).then_inc(hy_z, 1)
            z_lo(2)
            z_lo(3)
            v.wait_ge(d_att, 48)
            norm_dve("ctx")
            norm_apply("ctx")

            for u in range(8):
                v.wait_ge(c_free, CB["qkv"] + u + 1)
                if u:
                    v.wait_ge(q_done, u)
                TT(r1[:], qe[:, u % 2, 0:L], cosT[:], ALU.mult)
                v.wait_ge(q_rot, u + 1)
                then(TT(r2[:], aux[2][:], sinT[:], ALU.mult))
                TT(qT[:, u, :] if u < 4 else kT[:, u - 4, 0:L], r1[:], r2[:], ALU.add).then_inc(q_done, 1)

            for h in range(HEADS):
                for qi in range(NT):
                    n0_ = (h * NT + qi) * 2
                    for m in range(2):
                        n = n0_ + m
                        b = 8 + 4 * (n % 4)
                        v.wait_ge(a_s, n + 1)
                        then(V.reduce_max(small[:, b + 2:b + 3], scores[m][:, 0:NKEY], AX.X))
                        V.tensor_scalar(small[:, b:b + 1], small[:, b + 2:b + 3], -0.125, None, ALU.mult).then_inc(a_mx, 1)
                    b0, b1 = 8 + 4 * (n0_ % 4), 8 + 4 * ((n0_ + 1) % 4)
                    v.wait_ge(a_p, n0_ + 2)
                    V.reciprocal(small[:, b0 + 3:b0 + 4], small[:, b0 + 1:b0 + 2])
                    then(V.reciprocal(small[:, b1 + 3:b1 + 4], small[:, b1 + 1:b1 + 2]))
                    then(V.tensor_scalar(small[:, b1 + 2:b1 + 3], small[:, b1 + 3:b1 + 4], small[:, 3:4], None, ALU.mult))
                    p0, p1 = pp[:, qi % 2, 0, :], pp[:, qi % 2, 1, :]
                    then(V.tensor_scalar(p0, p0, small[:, b0 + 3:b0 + 4], None, ALU.mult))
                    STT(out=p0, in0=p1, scalar=small[:, b1 + 2:b1 + 3], in1=p0, op0=ALU.mult, op1=ALU.add).then_inc(a_cm, 1)
                v.wait_ge(a_std, h + 1)
                then(V.reciprocal(rstd[:], std[:]))
                STT(out=tmp[0][:], in0=aux[2][:], scalar=small[:, 6:7], in1=rstd[:], op0=ALU.mult, op1=ALU.mult).then_inc(a_tmp, 1)
                v.wait_ge(a_hi, h + 1)
                TT(olo[:, h, :], tmp[0][:], ohi[:, h, :].bitcast(F32), ALU.subtract).then_inc(a_lo, 1)

            with v.Fori(0, 2) as i:
                for jj in range(4):
                    b = jj % 2
                    v.wait_ge(m_sg, i * 4 + (jj + 1))
                    v.wait_ge(w_used, i * 12 + (TB["mix"] + 3 * jj + 3))
                    TT(mt[:, b, 0, :], sgm[:, b, 0, :], acc[2][:], ALU.mult)
                    TT(mt[:, b, 1, :], sgm[:, b, 1, :], acc[3][:], ALU.mult).then_inc(c_free, 4)
                    v.wait_ge(c_free, i * 16 + (CB["mix"] + 4 * jj + 4))
                    TT(mt[:, b, 0, :], mt[:, b, 0, :], mt[:, b, 1, :], ALU.add).then_inc(m_sum, 1)
                    v.wait_ge(m_hi, i * 4 + (jj + 1))
                    TT(mxl[:, bass.ds(i * 4 + jj, 1), :], one(mt[:, b, 0, :]), mxh[:, bass.ds(i * 4 + jj, 1), :].bitcast(F32),
                       ALU.subtract).then_inc(m_lo, 1)

            def evacuate(name, dst, n_tiles, add=False):
                with v.Fori(0, 2) as i:
                    for s in range(4):
                        v.wait_ge(w_used, i * (4 * n_tiles) + (TB[name] + n_tiles * (s + 1)))
                        d = dst[:, bass.ds(i * 4 + s, 1), :]
                        if add:
                            TT(d, one(acc[s][:]), d, ALU.add).then_inc(c_free, 1)
                        else:
                            V.tensor_copy(d, one(acc[s][:])).then_inc(c_free, 1)
                v.wait_ge(c_free, CB[name] + 8)
            evacuate("wout", mo, 1)
            norm_dve("mix_post")
            residual("mix_post")
            norm_dve("ffn_pre")
            norm_apply("ffn_pre")
            with v.Fori(0, FC // 2) as i:
                for p in range(2):
                    v.wait_ge(s_silu, i * 2 + (p + 1))
                    v.wait_ge(w_used, i * 4 + (TB["gateup"] + 2 * p + 2))
                    TT(tmp[p][:], sil[:, p, :], acc[2 * p + 1][:], ALU.mult).then_inc(c_free, 2)
                    v.wait_ge(s_hi, i * 2 + (p + 1))
                    TT(hidl[:, bass.ds(i * 2 + p, 1), :], one(tmp[p][:]), hidh[:, bass.ds(i * 2 + p, 1), :].bitcast(F32),
                       ALU.subtract).then_inc(s_lo, 1)
            evacuate("down", ff_out, 3)
            norm_dve("ffn_post")
            residual("ffn_post")
            norm_dve("g_mix")
            norm_apply("g_mix")

            v.wait_ge(gmd, 1)
            for c in range(16):
                TT(vT[:, c, :], vT[:, c, :], mean[:], ALU.subtract).then_inc(gxc, 1)
            v.wait_ge(gstd, 1)
            then(V.reciprocal(lrs[:], std[:]))
            for c in range(16):
                STT(out=vT[:, c, :], in0=vT[:, c, :], scalar=col("ln_g", c), in1=lrs[:], op0=ALU.mult, op1=ALU.mult).then_inc(gvt, 1)
            v.wait_ge(gws, 1)

            def g_lo(c):
                v.wait_ge(ghis, c + 1)
                TT(glo[:, c, :], gt[:, c % 2, 1, :], ghi[:, c, :].bitcast(F32), ALU.subtract).then_inc(glos, 1)
            for c in range(16):
                if c >= 2:
                    g_lo(c - 2)
                v.wait_ge(gsp, c + 1)
                TT(gt[:, c % 2, 0, :].rearrange("p (t n) -> p t n", n=P), acc[c % 4][:].rearrange("p (t n) -> p t n", n=P),
                   bsb[:, c // 2:c // 2 + 1, :].to_broadcast([P, NT, P]), ALU.add).then_inc(gta, 1)
                v.wait_ge(gta, c + 1)
                TT(gt[:, c % 2, 1, :], gt[:, c % 2, 0, :], guT[:, c, :], ALU.mult).then_inc(gtm, 1)
            g_lo(14)
            g_lo(15)
            evacuate("g_out", xT, 2, add=True)
            norm_dve("mlp0")
            norm_apply("mlp0")

            def mlp(layer):
                for half in range(2):
                    n = 16 * (layer * 2 + half)
                    with v.Fori(0, 4) as i:
                        for s in range(4):
                            v.wait_ge(c_free, i * 4 + (CB[f"up{layer}{'ab'[half]}"] + s + 1))
                            TT(tmp[s % 2][:], sq[s % 2][:], sq[s % 2][:], ALU.mult).then_inc(m_rsq, 1)
                            v.wait_ge(m_rhi, i * 4 + (n + s + 1))
                            TT(ml[:, bass.ds(i * 4 + s, 1), :], one(tmp[s % 2][:]), mh[:, bass.ds(i * 4 + s, 1), :].bitcast(F32),
                               ALU.subtract).then_inc(m_rlo, 1)
                    evacuate(f"dn{layer}{'ab'[half]}", xT, 2, add=True)
            mlp(0)

            V.memset(qa[64:66, :, :], 1.0).then_inc(x_ini, 1)
            V.memset(ka[64:66, :, :], 1.0).then_inc(x_ini, 1)
            norm_dve("fox")
            norm_apply("fox")
            v.wait_ge(x_lf, 4)
            then(V.memset(lf[:, 2, :], 1.0))
            then(STT(out=lf[:, 3, :], in0=lf[:, 0, :], scalar=0.0, in1=lf[:, 1, :], op0=ALU.min, op1=ALU.subtract))
            V.tensor_tensor_scan(cpos[:], lf[:, 2, :], lf[:, 3, :], 0.0, ALU.mult, ALU.add).then_inc(x_c, 1)
            v.wait_ge(x_c, 1)
            V.tensor_scalar(cneg[:], cpos[:], -1.0, None, ALU.mult).then_inc(x_c, 1)
            v.wait_ge(x_c, 2)
            V.memset(tmp[1][:, 0:1], 0.0).then_inc(x_og, 1)
            with v.Fori(0, 8) as i:
                for s in range(2):
                    v.wait_ge(x_std, i * 2 + (s + 1))
                    if s:
                        v.wait_ge(x_qk, i * 2 + 1)
                    V.reciprocal(frs[:], std[:]).then_inc(x_rs, 1)
                    v.wait_ge(x_rs, i * 2 + (s + 1))
                    if s:
                        v.wait_ge(x_sg, i + 1)
                    dst = (qa, ka)[s]
                    for e in range(2):
                        r = slice(64 * e, 64 * e + 64)
                        g_ = small[r, 7:8] if s == 0 else cols[r, COLS["k_g"]:COLS["k_g"] + 1]
                        m1 = STT(out=dst[0:64, e, :], in0=acc[s][r, :], scalar=g_, in1=frs[r, :], op0=ALU.mult, op1=ALU.mult)
                    m1.then_inc(x_qk, 1)
                v.wait_ge(x_qk, i * 2 + 2)
                V.memset(tmp[1][:, 0:1], 0.0).then_inc(c_free, 4)
                for n in range(8):
                    e, qi = n // 4, n % 4
                    W = (qi + 1) * P
                    b = aux[qi % 2]
                    v.wait_ge(x_s, i * 8 + (n + 1))
                    TT(b[:, qi * P:W], b[:, qi * P:W], cmask[:], ALU.add).then_inc(x_mk, 1)
                    v.wait_ge(x_mk, i * 8 + (n + 1))
                    V.reduce_max(small[:, 56 + n:57 + n], b[:, 0:W], AX.X).then_inc(x_rc, 1)
                    v.wait_ge(x_rc, i * 8 + (n + 1))
                    V.tensor_scalar(small[:, 40 + n:41 + n], small[:, 56 + n:57 + n], -1.0, None, ALU.mult).then_inc(x_mx, 1)
                    v.wait_ge(x_p, i * 8 + (n + 1))
                    V.reciprocal(small[:, 64 + n:65 + n], small[:, 48 + n:49 + n]).then_inc(x_rd, 1)
                    v.wait_ge(x_rd, i * 8 + (n + 1))
                    V.tensor_scalar(fp[:, qi % 2, 0:W], fp[:, qi % 2, 0:W], small[:, 64 + n:65 + n], None, ALU.mult).then_inc(x_pn, 1)
                v.wait_ge(x_o, i * 2 + 2)
                TT(tmp[0][:], aux[3][:], fsg[:], ALU.mult).then_inc(x_og, 1)
                v.wait_ge(x_hi, i + 1)
                TT(fol[:, bass.ds(i, 1), :], one(tmp[0][:]), foh[:, bass.ds(i, 1), :].bitcast(F32), ALU.subtract).then_inc(x_lo, 1)
            evacuate("fox_out", xT, 1, add=True)
            norm_dve("mlp1")
            norm_apply("mlp1")
            mlp(1)


def _tables(np):
    k = np.arange(L) + 0.5
    s = np.arange(L)
    w = 2 * np.pi / (2 * L)
    dft = np.stack([np.cos(w * np.outer(s, k)), np.sin(w * np.outer(s, k)),
                    np.cos(w * np.outer(s + 0.5, k)), np.sin(w * np.outer(s + 0.5, k))])
    dft = dft.reshape(4, NT, P, L).transpose(0, 2, 1, 3)
    bands = 16
    t = np.linspace(0.0, 1.0, L)
    ang = np.outer(np.linspace(1e-4, bands - 1, bands), 2 * np.pi / L * s)
    z = np.concatenate([t[None], np.cos(ang), -np.sin(ang)])
    deltas = np.abs(np.linspace(math.log(1e-2) / 1.5, math.log(1e-2) / 0.3, HY))
    dec = np.exp(-np.outer(t, deltas)).reshape(NT, P, HY)
    back = dec[0].copy()
    back[0] = 0.0
    dec = np.concatenate([dec, back[None]]).transpose(1, 0, 2)
    d = np.arange(P)
    pos = np.where((d % 64 < 32)[:, None], s[None] // 64, s[None] % 64)
    a = pos * (10000.0 ** (-(d % 16) / 16.0))[:, None]
    rope = np.stack([np.cos(a), np.sin(a)])
    rot = np.zeros((P, P))
    for m in range(P):
        if m % 32 < 16:
            rot[m + 16, m] = -1.0
        else:
            rot[m - 16, m] = 1.0
    cmask = np.where(d[:, None] >= d[None, :], 0.0, -1e30)
    out = {"dft": dft, "zT": z, "decay": dec, "rope": rope, "rot": rot, "cmask": cmask, "ident": np.eye(P)}
    return {n: np.ascontiguousarray(x.astype(np.float32)) for n, x in out.items()}


def _blocks(np, w):
    k, m = w.shape
    return w.reshape(k // P, P, m // P, P).transpose(2, 1, 0, 3)


def _layout(np, x):
    w_in = _blocks(np, x["w_in"][0])
    gate, up = _blocks(np, x["w_ffn_gate"][0]), _blocks(np, x["w_ffn_up"][0])
    hy_up, att_up = _blocks(np, x["w_hy_up"][0]), _blocks(np, x["w_att_up"][0])
    down = _blocks(np, x["w_ffn_down"][0])
    g_in, g_out = _blocks(np, x["gmlp_w_in_2"][0]), _blocks(np, x["gmlp_w_out_2"][0])
    fox = _blocks(np, x["fox_w_in_2"][0][:, :4096])
    n = ADA_T + TILES
    w = np.zeros((n, P, 8, P), np.float32)
    w[:ADA_T] = _blocks(np, x["w_ada"][0])
    w[ADA_T:ADA_T + 24] = w_in[:24]
    b = ADA_T + TB["mix"]
    w[b:b + 24:3] = w_in[24:32]
    w[b + 1:b + 24:3] = w_in[32:40]
    w[b + 2:b + 24:3, :, :4] = hy_up
    w[b + 2:b + 24:3, :, 4:] = att_up
    b = ADA_T + TB["wout"]
    w[b:b + 8] = _blocks(np, x["w_out"][0])
    b = ADA_T + TB["gateup"]
    w[b:b + 44:2] = gate
    w[b + 1:b + 44:2] = up
    b = ADA_T + TB["down"]
    for p in range(3):
        k = down[:, :, 8 * p:8 * p + 8]
        w[b + p:b + 24:3, :, :k.shape[2]] = k
    b = ADA_T + TB["g_in"]
    w[b:b + 16] = g_in[16:]
    w[b + 16:b + 32] = g_in[:16]

    def wide(name, m):
        b = ADA_T + TB[name]
        w[b:b + 16:2] = m[:, :, :8]
        w[b + 1:b + 16:2] = m[:, :, 8:]
    wide("g_out", g_out)
    for layer in range(2):
        w1, w2 = _blocks(np, x["mlp_w1_2"][layer]), _blocks(np, x["mlp_w2_2"][layer])
        for half in range(2):
            b = ADA_T + TB[f"up{layer}{'ab'[half]}"]
            w[b:b + 16] = w1[16 * half:16 * half + 16]
            wide(f"dn{layer}{'ab'[half]}", w2[:, :, 16 * half:16 * half + 16])
    b = ADA_T + TB["fox"]
    for p in range(4):
        w[b + p:b + 32:4] = fox[8 * p:8 * p + 8]
    b = ADA_T + TB["fox_out"]
    w[b:b + 8] = _blocks(np, x["fox_w_out_2"][0])

    cols = np.zeros((P, NCOLS), np.float32)

    def put(name, v, off=0, rows=P):
        v = np.asarray(v).reshape(-1, rows).T
        cols[:rows, COLS[name] + off:COLS[name] + off + v.shape[1]] = v
    for name in ("g_mix_pre", "g_mix_post", "g_ffn_pre", "g_ffn_post"):
        put(name, x[name][0])
    c0 = COLS["b_ada"]
    cols[:, c0:c0 + 96:2] = cols[:, c0 + 1:c0 + 96:2] = x["b_ada"][0].reshape(48, P).T
    put("conv_w", x["hy_conv_w"][0])
    put("conv_b", x["hy_conv_b"][0])
    put("subln", x["att_subln_g"][0])
    put("ln_g", x["gmlp_ln_g_2"][0])
    put("ln_b", x["gmlp_ln_b_2"][0])
    put("mixn", x["mix_norm_g_2"])
    put("mlpn", x["mlp_norm_g_2"])
    for name, src in (("q_g", "fox_q_g_2"), ("k_g", "fox_k_g_2")):
        cols[:64, COLS[name]] = cols[64:, COLS[name]] = x[src][0]
    put("b_f", x["fox_b_f_2"][0], rows=16)
    c0 = COLS["c"]
    cols[:, c0:c0 + 16:2] = x["c"][0].reshape(8, P).T
    cols[:, c0 + 1:c0 + 16:2] = x["c_ctx"].reshape(8, P).T
    for j in (1, 2):
        put("lam_q", x[f"lambda_q{j}"][0], j - 1, 64)
        put("lam_k", x[f"lambda_k{j}"][0], j - 1, 64)
    put("fb1", x["hy_f_b1"][0], rows=64)
    put("fb2", x["hy_f_b2"][0], rows=64)
    put("freq", x["hy_f_freq"][0], rows=64)

    def chunked(m):
        return np.ascontiguousarray(m.T.reshape(-1, P, m.shape[0]).transpose(1, 0, 2))
    return {
        "w": w, "cols": cols, "xT": chunked(x["x"][0]), "ctxT": chunked(x["ctx"][0]),
        "fw1": x["hy_f_w1"][0], "fw2": x["hy_f_w2"][0], "fw3": np.concatenate([x["hy_f_w3"][0], x["hy_f_b3"]]),
        "hbias": x["hy_bias"],
        "ws": np.ascontiguousarray(x["gmlp_w_s_2"][0].transpose(2, 0, 1)),
        "bs": np.ascontiguousarray(np.broadcast_to(x["gmlp_b_s_2"], (P, 8, P))),
        "wf": np.ascontiguousarray(x["fox_w_in_2"][0][:, 4096:].reshape(KD, P, 16).transpose(1, 0, 2)),
    }


def kernel(**inputs):
    import numpy as np
    import concourse.bacc as bacc
    from concourse.bass_utils import run_bass_kernel_spmd

    x = {n: np.asarray(v) for n, v in inputs.items()}
    arrays = {**_tables(np), **_layout(np, x)}
    nc = bacc.Bacc("TRN2", target_bir_lowering=False, num_devices=1)
    args, given = {}, {}
    for n, v in arrays.items():
        given[f"in_{n}"] = np.ascontiguousarray(v)
        args[n] = nc.dram_tensor(f"in_{n}", v.shape, F32, kind="ExternalInput").ap()
    args["scratch"] = nc.dram_tensor("scratch", (2, 16, L), F32, kind="Internal").ap()
    args["out"] = nc.dram_tensor("out", (P, KD, L), F32, kind="ExternalOutput").ap()
    build(nc, args)
    got = run_bass_kernel_spmd(nc, [given], core_ids=[0]).results[0]["out"]
    return np.ascontiguousarray(got.transpose(2, 1, 0).reshape(1, L, D))
```

```python
import math
from contextlib import ExitStack

import concourse.bass as bass
from concourse import mybir

F32 = mybir.dt.float32
F32R = mybir.dt.float32r
ALU = mybir.AluOpType
ACT = mybir.ActivationFunctionType
AX = mybir.AxisListType

P = 128
D = 1024
KD = D // P
L = 512
NT = L // P
CTX = 256
NKEY = L + CTX
KT = NKEY // P
HEADS = 4
HY = 512
HC = HY // P
FF = 2816
FC = FF // P
EPS = 1e-6
LN_EPS = 1e-5
LAM_INIT = 0.2
MAGIC = 12582912.0
RING = 4

ADA_T = 48
ADA_P = 1
PHASES = [("hyena", 12, 12), ("qkv", 12, 12), ("mix", 24, 32), ("wout", 8, 8), ("gateup", 44, 44),
          ("down", 24, 8), ("g_in", 32, 32), ("g_out", 16, 8),
          ("up0a", 16, 16), ("dn0a", 16, 8), ("up0b", 16, 16), ("dn0b", 16, 8),
          ("fox", 32, 32), ("fox_out", 8, 8),
          ("up1a", 16, 16), ("dn1a", 16, 8), ("up1b", 16, 16), ("dn1b", 16, 8)]
TB, CB = {}, {}
_t, _c = 0, RING
for _n, _nt, _nc in PHASES:
    TB[_n], CB[_n] = _t, _c
    _t += _nt
    _c += _nc
TILES = _t

COLS, NCOLS = {}, 0
for _n, _w in [("g_mix_pre", 8), ("g_mix_post", 8), ("g_ffn_pre", 8), ("g_ffn_post", 8), ("b_ada", 48),
               ("conv_w", 36), ("conv_b", 12), ("subln", 1), ("ln_g", 16), ("ln_b", 16),
               ("mixn", 16), ("mlpn", 16), ("q_g", 1), ("k_g", 1), ("b_f", 1),
               ("lam_q", 2), ("lam_k", 2), ("fb1", 1), ("fb2", 1), ("freq", 1)]:
    COLS[_n] = NCOLS
    NCOLS += _w

NORMS = ["mix_pre", "ctx", "mix_post", "ffn_pre", "ffn_post", "g_mix", "mlp0", "fox", "mlp1"]


def build(nc, a):
    ctx = ExitStack()
    with ctx:
        def sb(name, shape, dt=F32):
            return ctx.enter_context(nc.sbuf_tensor(name, shape, dt))

        def sem(name):
            return ctx.enter_context(nc.semaphore(name))

        def overlay(start, specs):
            with ExitStack() as s:
                if start:
                    s.enter_context(nc.sbuf_tensor(f"gap_{specs[0][0]}", [P, start // 4], F32))
                return [s.enter_context(nc.sbuf_tensor(n, sh, dt)) for n, sh, dt in specs]

        KB = 1024
        raw = [sb(f"w_raw{i}", [P, 8, P]) for i in range(RING)]
        whi = [sb(f"w_hi{i}", [P, 8, P], F32R) for i in range(RING)]
        wlo = [sb(f"w_lo{i}", [P, 8, P], F32R) for i in range(RING)]
        xT = sb("xT", [P, KD, L])
        cols = sb("cols", [P, NCOLS])
        ada = sb("ada", [P, ADA_T * 2])
        ones = sb("ones", [P, P])
        ones_d = sb("ones_d", [P, P])
        ones_hd = sb("ones_hd", [P, P])
        blk64 = sb("blk64", [P, P])
        ident = sb("ident", [P, P])
        rot = sb("rot", [P, P])
        cmask = sb("cmask", [P, P])
        acol = sb("acol", [P, 64])
        small = sb("small", [P, 96])
        zcol = sb("zcol", [P, 1])
        epsc = sb("epsc", [P, 2])
        work = sb("work", [P, 4, L])
        sq = [work[:, i, :] for i in range(2)]
        tmp = [work[:, 2 + i, :] for i in range(2)]
        std = sb("std", [P, L])
        rstd = sb("rstd", [P, L])

        cvec = work[:].rearrange("p (w a) n -> p w (a n)", w=2)

        HB = 0
        BIG = 32 * KB
        hh, hl = overlay(HB, [("h_hi", [P, KD, L], F32R), ("h_lo", [P, KD, L], F32R)])
        fE, fO = overlay(HB, [("filt_e", [P, NT, 2 * HY], F32), ("filt_o", [P, NT, 2 * HY], F32)])
        (ff_out,) = overlay(HB, [("ff_out", [P, KD, L], F32)])
        (ghi,) = overlay(HB, [("gate_hi", [P, 16, L], F32R)])
        Gr0, Gs0, Gr1, Gs1 = overlay(BIG, [(n, [P, NT, HY], F32) for n in ("gr0", "gs0", "gr1", "gs1")])
        Gr, Gs = [Gr0, Gr1], [Gs0, Gs1]
        C0, S0, dec, fw3, zT, fw1, fw2, hd, targ, tn, fab = overlay(BIG + 32 * KB, [
            ("c_int", [P, NT, HY], F32), ("s_int", [P, NT, HY], F32), ("decay", [P, 5, HY], F32),
            ("fw3", [65, 2048], F32), ("zT", [33, L], F32), ("fw1", [33, 64], F32), ("fw2", [64, 64], F32),
            ("hd", [65, L], F32), ("targ", [64, L], F32), ("tn", [64, L], F32), ("fab", [P, 2, 2, HY], F32)])
        hb, prod = overlay(BIG + 83 * KB, [("hbias", [1, 2, HY], F32), ("ada_prod", [P, D], F32)])
        Cm, Sm, n0, n1, x2T, uT, pad0, pad1 = overlay(BIG + 32 * KB, [
            ("c_half", [P, NT, HY], F32), ("s_half", [P, NT, HY], F32), ("n0", [P, NT, HY], F32),
            ("n1", [P, NT, HY], F32), ("x2T", [P, HC, L], F32), ("uT", [P, 8, L], F32),
            ("pad0", [P, L + 2], F32), ("pad1", [P, L + 2], F32)])
        pads = [pad0, pad1]
        (pw,) = overlay(BIG + 72 * KB, [("pointwise", [P, 2, 4, L], F32)])
        zhi, zlo, ohi, olo = overlay(BIG, [("z_hi", [P, HC, L], F32R), ("z_lo", [P, HC, L], F32R),
                                           ("o_hi", [P, HC, L], F32R), ("o_lo", [P, HC, L], F32R)])
        hch, hcl, qT, kT, vN, cxT, cosT, sinT, qe, r1, r2 = overlay(BIG + 16 * KB, [
            ("hc_hi", [P, KD, CTX], F32R), ("hc_lo", [P, KD, CTX], F32R), ("qT", [P, HEADS, L], F32),
            ("kT", [P, HEADS, NKEY], F32), ("vN", [P, HEADS, KT, P], F32), ("ctxT", [P, KD, CTX], F32),
            ("cosT", [P, L], F32), ("sinT", [P, L], F32), ("qe", [P, 2, NKEY], F32),
            ("r1", [P, L], F32), ("r2", [P, L], F32)])
        pp, aT = overlay(BIG + 64 * KB, [("pp", [P, 2, 2, NKEY], F32), ("aT", [P, KT, L], F32)])
        mxh, mxl, sgm, mt = overlay(BIG + 32 * KB, [("mixed_hi", [P, KD, L], F32R), ("mixed_lo", [P, KD, L], F32R),
                                              ("sgm", [P, 2, 2, L], F32), ("mt", [P, 2, 2, L], F32)])
        (mo,) = overlay(BIG, [("mix_out", [P, KD, L], F32)])
        hidh, hidl, sil = overlay(BIG, [("hid_hi", [P, FC, L], F32R), ("hid_lo", [P, FC, L], F32R),
                                        ("silu", [P, 2, L], F32)])
        vT, guT, wsT, bsb, vn, gt, mean, lrs = overlay(BIG, [
            ("g_v", [P, 16, L], F32), ("g_u", [P, 16, L], F32), ("wsT", [P, 8, P], F32), ("bsb", [P, 8, P], F32),
            ("vn", [P, 2, L], F32), ("gt", [P, 2, 2, L], F32), ("lmean", [P, L], F32), ("lrs", [P, L], F32)])
        (glo,) = overlay(BIG, [("gate_lo", [P, 16, L], F32R)])
        mh, ml, = overlay(BIG, [("mlp_hi", [P, 16, L], F32R), ("mlp_lo", [P, 16, L], F32R)])
        foh, fol, wf, fsq, qa, ka, fvT, fvn, fsg, fp, fog, fpT = overlay(BIG, [
            ("fo_hi", [P, KD, L], F32R), ("fo_lo", [P, KD, L], F32R), ("wf", [P, KD, 16], F32),
            ("fsq", [P, 2, L], F32),
            ("qa", [66, 2, 2, L], F32), ("ka", [66, 2, 2, L], F32), ("fvT", [P, L], F32), ("fvn", [P, 2, NT, P], F32),
            ("fsg", [P, 2, L], F32), ("fp", [P, 2, L], F32), ("fog", [P, L], F32), ("fpT", [P, 2, NT, L], F32)])
        lf, cpos, cneg = overlay(BIG + 76 * KB, [("lf", [16, 4, L], F32), ("cpos", [16, L], F32), ("cneg", [16, L], F32)])

        with ExitStack() as s:
            bank = [s.enter_context(nc.psum_tensor(f"bank{i}", [P, L], F32)) for i in range(8)]
        acc, aux = bank[0:4], bank[4:8]
        with ExitStack() as s:
            sc0, sc1, trT = (s.enter_context(nc.psum_tensor(n, [P, 2 * L], F32)) for n in ("scores0", "scores1", "weightsT"))
        scores = [sc0, sc1]

        w_landed = [sem(f"w_landed{i}") for i in range(RING)]
        w_hi, w_lo, w_used, ada_used, c_free = (sem(n) for n in ("w_hi", "w_lo", "w_used", "ada_used", "c_free"))
        d_cols, d_filt, d_dft, d_att, d_x, d_ws, d_wf, d_c, d_out, d_filt2 = (sem(n) for n in (
            "d_cols", "d_filt", "d_dft", "d_att", "d_x", "d_ws", "d_wf", "d_c", "d_out", "d_filt2"))
        d_cvec = sem("d_cvec")
        consts, c_silu, ada_ready, lam_prod, lam_mm, lam_exp, lam_ready = (sem(n) for n in (
            "consts", "c_silu", "ada_ready", "lam_prod", "lam_mm", "lam_exp", "lam_ready"))
        f_mm, f_arg, f_sin, f_ab, f_eo, g_mm, g_used, f_dve, f_dec = (sem(n) for n in (
            "f_mm", "f_arg", "f_sin", "f_ab", "f_eo", "g_mm", "g_used", "f_dve", "f_dec"))
        nm_sq, nm_sum, nm_std, nm_rstd, nm_tmp, h_hi, h_lo, x_new = (sem(n) for n in (
            "nm_sq", "nm_sum", "nm_std", "nm_rstd", "nm_tmp", "h_hi_s", "h_lo_s", "x_new"))
        acol_ready = sem("acol_ready")
        hy_pad, hy_conv, hy_tr, hy_nat = (sem(n) for n in ("hy_pad", "hy_conv", "hy_tr", "hy_nat"))
        hy_u, hy_pw, hy_y, hy_inv, hy_yd, hy_z, hy_zhi, hy_zlo = (sem(n) for n in (
            "hy_u", "hy_pw", "hy_y", "hy_inv", "hy_yd", "hy_z", "hy_zhi", "hy_zlo"))
        v_step = sem("v_step")
        x_sg, x_g1, x_gl, x_ln, log_done = (sem(n) for n in ("x_sg", "x_g1", "x_gl", "x_ln", "log_done"))
        d_crow = [sem(f"d_crow{i}") for i in range(2)]
        kv_ev, q_rot, q_done, v_tr, v_nat = (sem(n) for n in (
            "kv_ev", "q_rot", "q_done", "v_tr", "v_nat"))
        a_s, a_mx, a_p, a_cm, a_tr, a_ev, a_o, a_sq, a_ss, a_std, a_tmp, a_hi, a_lo, a_ch = (sem(n) for n in (
            "a_s", "a_mx", "a_p", "a_cm", "a_tr", "a_ev", "a_o", "a_sq", "a_ss", "a_std", "a_tmp", "a_hi", "a_lo", "a_ch"))
        m_sg, m_t, m_sum, m_hi, m_lo = (sem(n) for n in ("m_sg", "m_t", "m_sum", "m_hi", "m_lo"))
        o_ev = sem("o_ev")
        s_silu, s_prod, s_hi, s_lo, f_ev = (sem(n) for n in ("s_silu", "s_prod", "s_hi", "s_lo", "f_ev"))
        gl, gmean, gxc, gsq, gss, gstd, grs, gvt, gv, gtr, gvn, gsp, gta, gtm, ghis, glos, gws = (sem(n) for n in (
            "g_gelu", "g_mean_mm", "g_xc", "g_sq", "g_ss", "g_std", "g_rs", "g_vt", "g_vdone", "g_tr", "g_vn",
            "g_sp", "g_ta", "g_tm", "g_his", "g_los", "g_ws"))
        gmd = sem("g_mean_done")
        m_r, m_rsq, m_rhi, m_rlo, m_dn = (sem(n) for n in ("m_relu", "m_rsq", "m_rhi", "m_rlo", "m_dn"))
        x_fl, x_lf, x_c, x_ini = (sem(n) for n in ("x_fl", "x_lf", "x_c", "x_ini"))
        x_lfv = sem("x_lfv")
        x_sq, x_ss, x_std, x_qk, x_vt, x_vtr, x_vn, x_gt, x_s, x_mk, x_mx, x_p, x_rc, x_rd, x_pn, x_pt, x_pe, x_o, x_og, x_hi, x_lo = (
            sem(n) for n in ("x_sq", "x_ss", "x_std", "x_qk", "x_vt", "x_vtr", "x_vn", "x_gt", "x_s", "x_mk",
                             "x_mx", "x_p", "x_rc", "x_rd", "x_pn", "x_pt", "x_pe", "x_o", "x_og", "x_hi", "x_lo"))

        def col(name, k=0, n=1, rows=P):
            return cols[0:rows, COLS[name] + k:COLS[name] + k + n]

        ACOL = {"mix_pre": 0, "ctx": 8, "mix_post": 16, "ffn_pre": 24, "ffn_post": 32}

        def adac(part, k, which=0):
            m = (part * KD + k) * 2 + which
            return ada[:, m:m + 1]

        def norm_of(name):
            if name == "ctx":
                return cxT, (lambda k: acol[:, 8 + k:9 + k]), (lambda k: adac(0, k, 1)), hch, hcl, CTX
            if name == "mix_pre":
                return xT, (lambda k: acol[:, k:k + 1]), (lambda k: adac(0, k)), hh, hl, L
            if name == "ffn_pre":
                return xT, (lambda k: acol[:, 24 + k:25 + k]), (lambda k: adac(3, k)), hh, hl, L
            if name == "mix_post":
                return mo, (lambda k: acol[:, 16 + k:17 + k]), None, None, None, L
            if name == "ffn_post":
                return ff_out, (lambda k: acol[:, 32 + k:33 + k]), None, None, None, L
            g, o = {"g_mix": ("mixn", 0), "mlp0": ("mlpn", 0), "fox": ("mixn", 8), "mlp1": ("mlpn", 8)}[name]
            return xT, (lambda k: col(g, o + k)), (lambda k: zcol[:, 0:1]), hh, hl, L

        def fox_steps(engine, step):
            step(0, None, None, 0)
            step(1, 0, None, 1)
            with engine.Fori(0, 3) as j:
                step(j * 2 + 2, j * 2 + 1, j * 2, 0)
                step(j * 2 + 3, j * 2 + 2, j * 2 + 1, 1)
            step(None, 7, 6, 0)
            step(None, None, 7, 1)

        ATT_STEPS = HEADS * NT

        def att_col(n, m):
            return 8 + 8 * (n % 2) + 4 * m

        PRE = [n for n in NORMS if n not in ("mix_post", "ffn_post")]
        POST = ["mix_post", "ffn_post"]
        TAIL = "dn1b"

        block = ctx.enter_context(nc.Block())

        @block.sync
        def _(sp):
            sp.dma_start(cols[:], a["cols"]).then_inc(d_cols, 16)
            sp.dma_start(cvec, a["cvec"]).then_inc(d_cvec, 16)
            sp.dma_start(zT[:], a["zT"]).then_inc(d_filt, 16)
            sp.dma_start(fw1[:], a["fw1"]).then_inc(d_filt, 16)
            sp.dma_start(fw2[:], a["fw2"]).then_inc(d_filt, 16)
            sp.dma_start(fw3[:], a["fw3"]).then_inc(d_filt2, 16)
            sp.dma_start(dec[:], a["decay"]).then_inc(d_filt2, 16)
            sp.dma_start(hb[:], a["hbias"]).then_inc(d_filt2, 16)
            sp.dma_start(C0[:], a["dft"][0]).then_inc(d_filt2, 16)
            sp.dma_start(S0[:], a["dft"][1]).then_inc(d_filt2, 16)
            for s in range(RING):
                sp.dma_start(raw[s][:], a["w"][s:s + 1].rearrange("o p k n -> p (o k) n")).then_inc(w_landed[s], 16)
            with sp.Fori(1, ADA_T // RING) as i:
                for s in range(RING):
                    sp.wait_ge(ada_used, i * RING + (s - RING + 1))
                    sp.dma_start(raw[s][:], a["w"][bass.ds(i * RING + s, 1)].rearrange("o p k n -> p (o k) n")).then_inc(w_landed[s], 16)
            for s in range(RING):
                sp.wait_ge(ada_used, ADA_T - RING + s + 1)
                sp.dma_start(raw[s][:], a["w"][ADA_T + s:ADA_T + s + 1].rearrange("o p k n -> p (o k) n")).then_inc(w_landed[s], 16)
            with sp.Fori(1, TILES // RING) as i:
                for s in range(RING):
                    sp.wait_ge(w_lo, i * RING + (s - RING + 1))
                    sp.dma_start(raw[s][:], a["w"][bass.ds(i * RING + (s + ADA_T), 1)].rearrange("o p k n -> p (o k) n")).then_inc(w_landed[s], 16)

        @block.gpsimd
        def _(g):
            g.memset(ones[:], 1.0)
            g.memset(ones_d[:], 1.0 / D)
            g.memset(ones_hd[:], 1.0 / P)
            g.memset(zcol[:], 0.0)
            g.memset(epsc[:, 0:1], EPS)
            g.memset(epsc[:, 1:2], LN_EPS)
            g.memset(blk64[:], 0.0).then_inc(consts, 1)
            g.wait_ge(consts, 1)
            g.memset(blk64[0:64, 0:64], 1.0 / 64)
            g.memset(blk64[64:128, 64:128], 1.0 / 64).then_inc(consts, 1)
            with g.Fori(0, TB["g_in"] // RING) as i:
                for s in range(RING):
                    g.wait_ge(w_hi, i * RING + (s + 1))
                    g.tensor_tensor(wlo[s][:], raw[s][:], whi[s][:].bitcast(F32), ALU.subtract).then_inc(w_lo, 1)
            g.wait_ge(d_ws, 32)
            g.affine_select(out=wsT[:], in_=wsT[:], compare_op=ALU.is_ge, fill=0.0, base=0,
                            pattern=[[0, 8], [1, P]], channel_multiplier=-1).then_inc(gws, 1)
            with g.Fori(TB["g_in"] // RING, TILES // RING) as i:
                for s in range(RING):
                    g.wait_ge(w_hi, i * RING + (s + 1))
                    g.tensor_tensor(wlo[s][:], raw[s][:], whi[s][:].bitcast(F32), ALU.subtract).then_inc(w_lo, 1)

        @block.scalar
        def _(act):
            A = nc.scalar.activation
            act.dma_start(xT[:], a["xT"]).then_inc(d_x, 16)
            act.dma_start(ident[:], a["ident"]).then_inc(d_x, 16)
            act.dma_start(rot[:], a["rot"]).then_inc(d_x, 16)
            act.dma_start(cmask[:], a["cmask"]).then_inc(d_x, 16)

            def one(ap):
                return ap.rearrange("p (o n) -> p o n", o=1)

            def hi_split(v, s, first=False):
                act.wait_ge(w_landed[s], v * 4 + (16 * (ADA_T // RING) + 16 - 4 * s))
                if not first:
                    act.wait_ge(w_used, v - (RING - 1))
                A(whi[s][:], raw[s][:], ACT.Copy).then_inc(w_hi, 1)

            roots = [0]

            def inverse_root(out, mean_square, done, eps=0, scale=1.0, W=L):
                A(std[:, 0:W], mean_square, ACT.Ln, bias=epsc[:, eps:eps + 1], scale=scale).then_inc(log_done, 1)
                roots[0] += 1
                act.wait_ge(log_done, roots[0])
                A(out, std[:, 0:W], ACT.Exp, scale=-0.5).then_inc(done, 1)

            def roots_table():
                act.preload_act_table_set("natural_log_exp_and_others")

            def norm_act(name):
                n = NORMS.index(name)
                act.wait_ge(nm_sum, n * KD + KD)
                W = norm_of(name)[5]
                inverse_root(rstd[:, 0:W], aux[3][:, 0:W], nm_std, W=W)

            def norm_apply_act(name):
                n = PRE.index(name)
                _, _, sh, hi_, _, W = norm_of(name)
                for k in range(KD):
                    act.wait_ge(nm_tmp, n * KD + k + 1)
                    A(hi_[:, k, :], tmp[k % 2][:, 0:W], ACT.Identity, bias=sh(k)).then_inc(h_hi, 1)

            act.wait_ge(d_cvec, 16)
            A(cvec, cvec, ACT.Silu).then_inc(c_silu, 1)
            act.wait_ge(d_cols, 16)
            for j in range(2):
                act.wait_ge(f_arg, j + 1)
                A(hd[0:64, :], tn[:], ACT.Sin).then_inc(f_sin, 1)
            roots_table()
            act.wait_ge(lam_mm, 1)
            A(small[:, 0:2], acc[1][:, 0:2], ACT.Exp).then_inc(lam_exp, 1)
            for q in range(8):
                o, f = q // 4, q % 4
                act.wait_ge(g_mm, q + 1)
                A(Gr[o][:, f, :], aux[2 * (q % 2)][:], ACT.Copy, scale=1.0 / HY)
                A(Gs[o][:, f, :], aux[2 * (q % 2) + 1][:], ACT.Copy, scale=1.0 / HY).then_inc(g_used, 1)
            act.wait_ge(g_mm, 8)
            act.dma_start(Cm[:], a["dft"][2]).then_inc(d_dft, 16)
            act.dma_start(Sm[:], a["dft"][3]).then_inc(d_dft, 16)

            norm_act("mix_pre")
            hi_split(0, 0, True)
            hi_split(1, 1, True)
            norm_apply_act("mix_pre")

            for u in range(12):
                if u + 2 < RING:
                    hi_split(u + 2, u + 2, True)
                else:
                    hi_split(u + 2, (u + 2) % RING)
                act.wait_ge(w_used, u + 1)
                if u == 0:
                    act.wait_ge(hy_pad, 1)
                if u >= 2:
                    act.wait_ge(hy_conv, u - 1)
                A(pads[u % 2][:, 1:L + 1], acc[u % 4][:], ACT.Copy).then_inc(c_free, 1)
            for c in range(8):
                act.wait_ge(hy_tr, c + 1)
                dst = n0 if c < 4 else n1
                A(dst[:, :, (c % 4) * P:(c % 4 + 1) * P], aux[c % 2][:].rearrange("p (t n) -> p t n", t=NT), ACT.Copy).then_inc(hy_nat, 1)
            for c in range(HC):
                act.wait_ge(hy_z, c + 1)
                A(zhi[:, c, :], tmp[c % 2][:], ACT.Copy).then_inc(hy_zhi, 1)
            act.wait_ge(hy_zlo, HC)
            act.dma_start(cxT[:], a["ctxT"]).then_inc(d_att, 16)
            act.dma_start(cosT[:], a["rope"][0]).then_inc(d_att, 16)
            act.dma_start(sinT[:], a["rope"][1]).then_inc(d_att, 16)
            norm_act("ctx")
            norm_apply_act("ctx")

            def v_natural(h):
                act.wait_ge(v_tr, h + 1)
                A(vN[:, h, 0:4, :], aux[2][:].rearrange("p (t n) -> p t n", t=4), ACT.Copy)
                A(vN[:, h, 4:6, :], aux[3][:, 0:CTX].rearrange("p (t n) -> p t n", t=2), ACT.Copy).then_inc(v_nat, 1)

            for u in range(12):
                t = TB["qkv"] + u
                hi_split(t + 2, (t + 2) % RING)
                act.wait_ge(w_used, t + 1)
                if 2 <= u < 10:
                    act.wait_ge(q_done, u - 1)
                if u >= 10:
                    act.wait_ge(v_tr, u - 9)
                A(qe[:, u % 2, 0:L], acc[t % 4][:], ACT.Copy).then_inc(c_free, 1)
                if u >= 4:
                    A(kT[:, u - 4, L:NKEY] if u < 8 else qe[:, u % 2, L:NKEY], aux[u % 2][:, 0:CTX], ACT.Copy).then_inc(kv_ev, 1)
                if u >= 9:
                    v_natural(u - 9)
            v_natural(3)

            for n in range(ATT_STEPS + 4):
                if n < ATT_STEPS:
                    if n > 1:
                        act.wait_ge(a_tr, n - 1)
                    for m in range(2):
                        b = att_col(n, m)
                        act.wait_ge(a_mx, 2 * n + m + 1)
                        A(pp[:, n % 2, m, :], scores[m][:, 0:NKEY], ACT.Exp, bias=small[:, b:b + 1], scale=0.125,
                          accum_out=small[:, b + 1:b + 2]).then_inc(a_p, 1)
                if 2 <= n < ATT_STEPS + 2:
                    qi, h = (n - 2) % NT, (n - 2) // NT
                    act.wait_ge(a_tr, n - 1)
                    if qi == 0 and h:
                        act.wait_ge(a_o, h)
                    A(aT[:, 0:4, qi * P:(qi + 1) * P], trT[:, 0:L].rearrange("p (t n) -> p t n", t=4), ACT.Copy)
                    A(aT[:, 4:6, qi * P:(qi + 1) * P], trT[:, L:NKEY].rearrange("p (t n) -> p t n", t=2), ACT.Copy).then_inc(a_ev, 1)
                if n > NT:
                    h = (n - 2) // NT - 1
                    if n % NT == 2:
                        act.wait_ge(a_o, h + 1)
                        A(sq[0][:], aux[2][:], ACT.Square).then_inc(a_sq, 1)
                    if n % NT == 3:
                        act.wait_ge(a_ss, h + 1)
                        inverse_root(rstd[:], aux[3][:], a_std)
                    if n % NT == 0 and h >= 0:
                        act.wait_ge(a_tmp, h + 1)
                        A(ohi[:, h, :], tmp[0][:], ACT.Copy).then_inc(a_hi, 1)
            act.wait_ge(a_tmp, HEADS)
            A(ohi[:, HEADS - 1, :], tmp[0][:], ACT.Copy).then_inc(a_hi, 1)

            act.preload_act_table(ACT.Sigmoid)
            with act.Fori(0, 2) as i:
                for jj in range(4):
                    t = i * 12 + (TB["mix"] + 3 * jj)
                    hi_split(t + 2, (3 * jj + 2) % RING)
                    act.wait_ge(w_used, t + 1)
                    A(sgm[:, jj % 2, 0, :], acc[0][:], ACT.Sigmoid)
                    hi_split(t + 3, (3 * jj + 3) % RING)
                    act.wait_ge(w_used, t + 2)
                    A(sgm[:, jj % 2, 1, :], acc[1][:], ACT.Sigmoid).then_inc(m_sg, 1)
                    hi_split(t + 4, (3 * jj + 4) % RING)
                    act.wait_ge(m_sum, i * 4 + (jj + 1))
                    A(mxh[:, bass.ds(i * 4 + jj, 1), :], one(mt[:, jj % 2, 0, :]), ACT.Copy).then_inc(m_hi, 1)
            roots_table()

            for u in range(8):
                t = TB["wout"] + u
                hi_split(t + 2, (t + 2) % RING)
            norm_act("mix_post")
            norm_act("ffn_pre")
            norm_apply_act("ffn_pre")

            act.preload_act_table(ACT.Silu)
            with act.Fori(0, FC // 2) as i:
                for s in range(RING):
                    v = i * RING + (TB["gateup"] + s)
                    p = s // 2
                    hi_split(v + 2, (s + 2) % RING)
                    if s % 2 == 0:
                        act.wait_ge(w_used, v + 1)
                        A(sil[:, p, :], acc[s][:], ACT.Silu).then_inc(s_silu, 1)
                    else:
                        act.wait_ge(c_free, i * RING + (CB["gateup"] + s + 1))
                        A(hidh[:, bass.ds(i * 2 + p, 1), :], one(tmp[p][:]), ACT.Copy).then_inc(s_hi, 1)
            roots_table()
            for v in range(TB["down"], TB["down"] + 24):
                hi_split(v + 2, (v + 2) % RING)
            norm_act("ffn_post")
            act.dma_start(wsT[:], a["ws"]).then_inc(d_ws, 16)
            act.dma_start(bsb[:], a["bs"]).then_inc(d_ws, 16)
            norm_act("g_mix")
            norm_apply_act("g_mix")

            act.preload_act_table(ACT.Gelu_apprx_tanh)
            with act.Fori(0, 4) as i:
                for s in range(RING):
                    v = i * RING + (TB["g_in"] + s)
                    hi_split(v + 2, (s + 2) % RING)
                    act.wait_ge(w_used, v + 1)
                    A(vT[:, bass.ds(i * 4 + s, 1), :], acc[s][:].rearrange("p (o n) -> p o n", o=1), ACT.Gelu_apprx_tanh).then_inc(c_free, 1)
            act.wait_ge(gmean, 1)
            A(mean[:], aux[0][:], ACT.Copy, scale=0.5).then_inc(gmd, 1)
            with act.Fori(0, 4) as i:
                for s in range(RING):
                    v = i * RING + (TB["g_in"] + 16 + s)
                    hi_split(v + 2, (s + 2) % RING)
                    act.wait_ge(w_used, v + 1)
                    A(guT[:, bass.ds(i * 4 + s, 1), :], acc[s][:].rearrange("p (o n) -> p o n", o=1), ACT.Gelu_apprx_tanh).then_inc(c_free, 1)
            roots_table()
            for c in range(16):
                act.wait_ge(gxc, c + 1)
                if c >= 2:
                    act.wait_ge(gss, c - 1)
                A(sq[c % 2][:], vT[:, c, :], ACT.Square).then_inc(gsq, 1)
            act.wait_ge(gss, 16)
            inverse_root(lrs[:], aux[1][:], gstd, eps=1, scale=0.5)
            for c in range(16):
                act.wait_ge(gvt, c + 1)
                A(vT[:, c, :], vT[:, c, :], ACT.Identity, bias=col("ln_b", c)).then_inc(gv, 1)
            for c in range(16):
                act.wait_ge(gtr, c + 1)
                if c >= 2:
                    act.wait_ge(gsp, c - 1)
                A(vn[:, c % 2, :], aux[c % 2][:], ACT.Copy).then_inc(gvn, 1)
                if c >= 1:
                    act.wait_ge(gtm, c)
                    A(ghi[:, c - 1, :], gt[:, (c - 1) % 2, 1, :], ACT.Copy).then_inc(ghis, 1)
            act.wait_ge(gtm, 16)
            A(ghi[:, 15, :], gt[:, 1, 1, :], ACT.Copy).then_inc(ghis, 1)
            for v in range(TB["g_out"], TB["g_out"] + 16):
                hi_split(v + 2, (v + 2) % RING)

            def mlp_up(i, base, nbase):
                for s in range(RING):
                    v = i * RING + (base + s)
                    hi_split(v + 2, (s + 2) % RING)
                    act.wait_ge(w_used, v + 1)
                    A(sq[s % 2][:], acc[s][:], ACT.Relu).then_inc(c_free, 1)
                    act.wait_ge(m_rsq, i * RING + (nbase + s + 1))
                    A(mh[:, bass.ds(i * 4 + s, 1), :], tmp[s % 2][:].rearrange("p (o n) -> p o n", o=1), ACT.Copy).then_inc(m_rhi, 1)

            def mlp(layer, last):
                for half in range(2):
                    n = layer * 2 + half
                    with act.Fori(0, 4) as i:
                        mlp_up(i, TB[f"up{layer}{'ab'[half]}"], n * 16)
                    b = TB[f"dn{layer}{'ab'[half]}"]
                    for v in range(b, b + 16):
                        if v + 2 < TILES:
                            hi_split(v + 2, (v + 2) % RING)

            norm_act("mlp0")
            norm_apply_act("mlp0")
            mlp(0, False)

            norm_act("fox")
            norm_apply_act("fox")
            act.dma_start(wf[:], a["wf"]).then_inc(d_wf, 16)
            act.wait_ge(x_fl, 1)
            A(lf[:, 0, :], aux[0][0:16, :], ACT.Identity, bias=col("b_f", rows=16)).then_inc(x_lf, 1)
            act.wait_ge(x_lf, 1)
            A(lf[:, 1, :], lf[:, 0, :], ACT.Abs).then_inc(x_lf, 1)
            act.wait_ge(x_lf, 2)
            A(lf[:, 2, :], lf[:, 1, :], ACT.Exp, scale=-1.0).then_inc(x_lf, 1)
            act.wait_ge(x_lf, 3)
            A(lf[:, 1, :], lf[:, 2, :], ACT.Ln, bias=ones[0:16, 0:1]).then_inc(x_lf, 1)
            act.wait_ge(x_c, 2)
            act.dma_start(a["scratch"][0], cpos[:]).then_inc(d_c, 16)
            act.dma_start(a["scratch"][1], cneg[:]).then_inc(d_c, 16)
            act.wait_ge(d_c, 32)
            act.wait_ge(x_ini, 2)

            def fox_act(g, a_, b_, par):
                if g is not None:
                    v0 = g * RING + TB["fox"]
                    for e in range(2):
                        act.dma_start(qa[65:66, par, e, :], a["scratch"][0, one_of(g * 2 + e), :]).then_inc(d_crow[par], 16)
                        act.dma_start(ka[64:65, par, e, :], a["scratch"][1, one_of(g * 2 + e), :]).then_inc(d_crow[par], 16)

                def weights_out(pair, n):
                    e, qi = n // 4, n % 4
                    act.wait_ge(x_pt, pair * 8 + (n + 1))
                    A(fpT[:, e, 0:qi + 1, qi * P:(qi + 1) * P], aux[2][:, 0:(qi + 1) * P].rearrange("p (t n) -> p t n", n=P), ACT.Copy).then_inc(x_pe, 1)
                for n in range(8):
                    if g is not None:
                        if n in (2, 4):
                            s = n // 2 - 1
                            act.wait_ge(w_used, v0 + (s + 1))
                            A(fsq[:, s, :], acc[s][:], ACT.Square).then_inc(x_sq, 1)
                        if n == 6:
                            act.wait_ge(w_used, v0 + 3)
                            A(fvT[:], acc[2][:], ACT.Copy).then_inc(x_vt, 1)
                        if n == 7:
                            act.wait_ge(x_vtr, g + 1)
                            A(fvn[:, par, :, :], aux[3][:].rearrange("p (t n) -> p t n", t=NT), ACT.Copy).then_inc(x_vn, 1)
                        if n % 2 == 0:
                            hi_split(v0 + (n // 2 + 2), (n // 2 + 2) % RING)
                    if a_ is not None:
                        e, qi = n // 4, n % 4
                        W = (qi + 1) * P
                        act.wait_ge(x_mx, a_ * 8 + (n + 1))
                        A(fp[:, qi % 2, 0:W], aux[qi % 2][:, 0:W], ACT.Exp, bias=small[:, 40 + n:41 + n],
                          accum_out=small[:, 48 + n:49 + n]).then_inc(x_p, 1)
                        if n:
                            weights_out(a_, n - 1)
                        if n == 1:
                            act.wait_ge(x_g1, a_ + 1)
                            A(fsg[:, 1 - par, :], fsg[:, 1 - par, :], ACT.Ln).then_inc(x_gl, 1)
                        if n == 2:
                            act.wait_ge(x_gl, a_ + 1)
                            A(fsg[:, 1 - par, :], fsg[:, 1 - par, :], ACT.Exp, scale=-1.0).then_inc(x_sg, 1)
                    if b_ is not None:
                        if n == 0:
                            weights_out(b_, 7)
                        if n == 3:
                            act.wait_ge(x_og, b_ * 2 + 2)
                            A(foh[:, one_of(b_), :], one(fog[:]), ACT.Copy).then_inc(x_hi, 1)
                    if g is not None and n in (4, 5):
                        s = n - 4
                        r = (std, rstd)[s][:]
                        act.wait_ge(x_ss, g * 2 + (s + 1))
                        A(r, (aux[3], acc[3])[s][:], ACT.Ln, bias=epsc[:, 0:1]).then_inc(x_ln, 1)
                        act.wait_ge(x_ln, g * 2 + (s + 1))
                        A(r, r, ACT.Exp, scale=-0.5).then_inc(x_std, 1)
                if g is not None:
                    act.wait_ge(w_used, v0 + 4)
                    A(fsg[:, par, :], acc[3][:], ACT.Exp, scale=-1.0).then_inc(x_gt, 1)

            def one_of(index):
                return bass.ds(index, 1)
            fox_steps(act, fox_act)
            for v in range(TB["fox_out"], TB["fox_out"] + 8):
                hi_split(v + 2, (v + 2) % RING)
            norm_act("mlp1")
            norm_apply_act("mlp1")
            mlp(1, True)
            for k in range(KD):
                act.wait_ge(c_free, CB["dn1b"] + k + 1)
                act.dma_start(a["out"][:, k, :], xT[:, k, :]).then_inc(d_out, 16)
            act.wait_ge(d_out, 16 * KD)

        @block.tensor
        def _(pe):
            mm = nc.tensor.matmul

            def tile(v, s, bank_, xh, xl, blocks=8, start=True, stop=True, last=True, first_block=0, free=None):
                pe.wait_ge(w_lo, v + 1)
                if free is not None:
                    pe.wait_ge(c_free, free)
                for k in range(blocks):
                    b = first_block + k
                    m1 = mm(bank_, whi[s][:, b, :], xh[k], start=start and k == 0, stop=False)
                    mm(bank_, whi[s][:, b, :], xl[k], start=False, stop=False)
                    m1 = mm(bank_, wlo[s][:, b, :], xh[k], start=False, stop=stop and k == blocks - 1)
                if last:
                    m1.then_inc(w_used, 1)

            def chunks(t, n0, n1):
                return [t[:, k, :] for k in range(n0, n1)]

            def norm_pe(name):
                n = NORMS.index(name)
                W = norm_of(name)[5]
                for k in range(KD):
                    pe.wait_ge(nm_sq, n * KD + k + 1)
                    mm(aux[3][:, 0:W], ones_d[:], sq[k % 2][:, 0:W], start=k == 0, stop=k == KD - 1).then_inc(nm_sum, 1)

            H = (chunks(hh, 0, KD), chunks(hl, 0, KD))

            pe.wait_ge(d_filt, 48)
            mm(aux[0][0:64, :], fw1[:], zT[:], start=True, stop=True).then_inc(f_mm, 1)
            pe.wait_ge(consts, 2)
            pe.wait_ge(lam_prod, 1)
            mm(acc[1][:, 0:2], ones[0:64, :], small[0:64, 4:6], start=True, stop=True).then_inc(lam_mm, 1)
            pe.wait_ge(f_sin, 1)
            mm(aux[1][0:64, :], fw2[:], hd[0:64, :], start=True, stop=True).then_inc(f_mm, 1)
            pe.wait_ge(f_sin, 2)
            pe.wait_ge(d_filt2, 80)
            for p in range(8):
                o, t = p // 4, p % 4
                if p >= 2:
                    pe.wait_ge(f_dec, p - 1)
                for d in range(2):
                    m1 = mm(aux[2 * (p % 2) + d][:], hd[0:65, t * P:(t + 1) * P], fw3[:, (2 * o + d) * HY:(2 * o + d + 1) * HY],
                            start=True, stop=True)
                m1.then_inc(f_ab, 1)
            pe.wait_ge(f_eo, 8)
            for q in range(8):
                o, f = q // 4, q % 4
                if q >= 2:
                    pe.wait_ge(g_used, q - 1)
                for r, (mat, src) in enumerate(((C0, fE), (S0, fO))):
                    for t in range(NT):
                        m1 = mm(aux[2 * (q % 2) + r][:], mat[:, t, f * P:(f + 1) * P], src[:, t, o * HY:(o + 1) * HY],
                                start=t == 0, stop=t == NT - 1)
                m1.then_inc(g_mm, 1)

            pe.wait_ge(g_used, 8)
            norm_pe("mix_pre")
            pe.wait_ge(h_lo, KD)

            pe.wait_ge(c_free, RING)
            for u in range(12):
                tile(u, u % 4, acc[u % 4][:], *H, free=CB["hyena"] + u - 3)
            pe.wait_ge(d_x, 64)
            for c in range(8):
                pe.wait_ge(hy_conv, c + 1)
                if c >= 2:
                    pe.wait_ge(hy_nat, c - 1)
                for t in range(NT):
                    m1 = nc.tensor.transpose(aux[c % 2][:, t * P:(t + 1) * P], uT[:, c, t * P:(t + 1) * P], ident[:])
                m1.then_inc(hy_tr, 1)
            pe.wait_ge(hy_nat, 8)
            pe.wait_ge(d_dft, 32)
            pe.wait_ge(c_free, CB["qkv"])
            for o in range(2):
                if o:
                    pe.wait_ge(hy_yd, NT)
                for f in range(4):
                    if o * 4 + f >= 2:
                        pe.wait_ge(hy_pw, o * 4 + f - 1)
                    for r, mat in enumerate((Cm, Sm)):
                        for t in range(NT):
                            m1 = mm(aux[2 * (f % 2) + r][:], mat[:, t, f * P:(f + 1) * P], n0[:, t, :],
                                    start=t == 0, stop=t == NT - 1)
                    m1.then_inc(hy_u, 1)
                pe.wait_ge(hy_y, o * 4 + 4)
                for t in range(NT):
                    for r, (mat, y) in enumerate(((Cm, Gr[o]), (Sm, Gs[o]))):
                        for f in range(4):
                            lhs, rhs = (mat, y) if o == 0 else (y, mat)
                            m1 = mm(acc[t][:], lhs[:, f, t * P:(t + 1) * P], rhs[:, f, :],
                                    start=(r == 0 and f == 0), stop=(r == 1 and f == 3))
                    m1.then_inc(hy_inv, 1)

            norm_pe("ctx")
            pe.wait_ge(h_lo, 2 * KD)
            pe.wait_ge(hy_z, HC)

            def rotate(u):
                pe.wait_ge(c_free, CB["qkv"] + u + 1)
                if u:
                    pe.wait_ge(q_done, u)
                mm(aux[2][:], rot[:], qe[:, u % 2, 0:L], start=True, stop=True).then_inc(q_rot, 1)

            def v_transposes(h):
                pe.wait_ge(c_free, CB["qkv"] + h + 9)
                pe.wait_ge(kv_ev, h + 5)
                if h == 0:
                    pe.wait_ge(q_done, 8)
                else:
                    pe.wait_ge(v_nat, h)
                for t in range(KT):
                    b = aux[2] if t < 4 else aux[3]
                    m1 = nc.tensor.transpose(b[:, (t % 4) * P:(t % 4 + 1) * P], qe[:, h % 2, t * P:(t + 1) * P], ident[:])
                m1.then_inc(v_tr, 1)

            for u in range(12):
                v = TB["qkv"] + u
                tile(v, v % 4, acc[v % 4][:], *H, free=CB["qkv"] + u - 3, last=u < 4)
                if u >= 4:
                    if u >= 6:
                        pe.wait_ge(kv_ev, u - 5)
                    for k in range(KD):
                        b = aux[u % 2][:, 0:CTX]
                        mm(b, whi[v % 4][:, k, :], hch[:, k, :], start=k == 0, stop=False)
                        mm(b, whi[v % 4][:, k, :], hcl[:, k, :], start=False, stop=False)
                        m1 = mm(b, wlo[v % 4][:, k, :], hch[:, k, :], start=False, stop=k == KD - 1)
                    m1.then_inc(w_used, 1)
                if 1 <= u < 9:
                    rotate(u - 1)
                if u >= 9:
                    v_transposes(u - 9)
            v_transposes(3)

            pe.wait_ge(c_free, CB["mix"])
            pe.wait_ge(kv_ev, 8)
            pe.wait_ge(q_done, 8)
            pe.wait_ge(v_nat, 4)
            for n in range(ATT_STEPS + 4):
                if n < ATT_STEPS:
                    h, qi = n // NT, n % NT
                    for m in range(2):
                        if n:
                            pe.wait_ge(a_p, 2 * n + m - 1)
                        r = slice(64 * m, 64 * m + 64)
                        mm(scores[m][:, 0:L], qT[r, h, qi * P:(qi + 1) * P], kT[r, h, 0:L], start=True, stop=True)
                        mm(scores[m][:, L:NKEY], qT[r, h, qi * P:(qi + 1) * P], kT[r, h, L:NKEY], start=True, stop=True).then_inc(a_s, 1)
                if 2 <= n < ATT_STEPS + 2:
                    pe.wait_ge(a_cm, n - 1)
                    if n > 2:
                        pe.wait_ge(a_ev, n - 2)
                    for t in range(KT):
                        m1 = nc.tensor.transpose(trT[:, t * P:(t + 1) * P], pp[:, n % 2, 0, t * P:(t + 1) * P], ident[:])
                    m1.then_inc(a_tr, 1)
                h = (n - 1) // NT - 1
                if n > NT and n % NT in (1, 2):
                    pe.wait_ge(a_ev, NT * h + NT)
                    if h:
                        pe.wait_ge(a_tmp, h)
                    half = n % NT - 1
                    for t in range(3 * half, 3 * half + 3):
                        m1 = mm(aux[2][:], vN[:, h, t, :], aT[:, t, :], start=t == 0, stop=t == KT - 1)
                    if half:
                        m1.then_inc(a_o, 1)
                if n > NT and n % NT == 3:
                    pe.wait_ge(a_sq, h + 1)
                    mm(aux[3][:], ones_hd[:], sq[0][:], start=True, stop=True).then_inc(a_ss, 1)

            pe.wait_ge(a_lo, HEADS)
            with pe.Fori(0, 2) as i:
                for jj in range(4):
                    v = i * 12 + (TB["mix"] + 3 * jj)
                    c = i * 16 + (CB["mix"] + 4 * jj)
                    tile(v, (3 * jj) % 4, acc[0][:], *H, free=c - 3)
                    tile(v + 1, (3 * jj + 1) % 4, acc[1][:], *H)
                    s = (3 * jj + 2) % 4
                    tile(v + 2, s, acc[2][:], chunks(zhi, 0, 4), chunks(zlo, 0, 4), blocks=4, last=False)
                    tile(v + 2, s, acc[3][:], chunks(ohi, 0, 4), chunks(olo, 0, 4), blocks=4, first_block=4)

            pe.wait_ge(c_free, CB["wout"])
            pe.wait_ge(m_lo, KD)
            with pe.Fori(0, 2) as i:
                for s in range(4):
                    tile(i * 4 + (TB["wout"] + s), s, acc[s][:], chunks(mxh, 0, KD), chunks(mxl, 0, KD), free=i * 4 + (CB["wout"] + s - 3))
            norm_pe("mix_post")
            norm_pe("ffn_pre")
            pe.wait_ge(h_lo, 3 * KD)
            pe.wait_ge(c_free, CB["gateup"])
            with pe.Fori(0, FC // 2) as i:
                for s in range(4):
                    tile(i * 4 + (TB["gateup"] + s), s, acc[s][:], *H, free=i * 4 + (CB["gateup"] + s - 3))
            pe.wait_ge(c_free, CB["down"])
            pe.wait_ge(s_lo, FC)
            with pe.Fori(0, 2) as i:
                for cc in range(4):
                    for part in range(3):
                        n0_, n1_ = 8 * part, min(8 * part + 8, FC)
                        s = (3 * cc + part) % 4
                        tile(i * 12 + (TB["down"] + 3 * cc + part), s, acc[cc][:], chunks(hidh, n0_, n1_), chunks(hidl, n0_, n1_),
                             blocks=n1_ - n0_, start=part == 0, stop=part == 2,
                             free=i * 4 + (CB["down"] + cc - 3) if part == 0 else None)
            norm_pe("ffn_post")
            norm_pe("g_mix")
            pe.wait_ge(h_lo, 4 * KD)
            pe.wait_ge(c_free, CB["g_in"])

            def g_in(first):
                with pe.Fori(0, 4) as i:
                    for s in range(4):
                        tile(i * 4 + (TB["g_in"] + first + s), s, acc[s][:], *H, free=i * 4 + (CB["g_in"] + first + s - 3))
            g_in(0)
            pe.wait_ge(c_free, CB["g_in"] + 16)
            for c in range(16):
                m1 = mm(aux[0][:], ones_d[:], vT[:, c, :], start=c == 0, stop=c == 15)
            m1.then_inc(gmean, 1)
            g_in(16)
            for c in range(16):
                pe.wait_ge(gsq, c + 1)
                mm(aux[1][:], ones_d[:], sq[c % 2][:], start=c == 0, stop=c == 15).then_inc(gss, 1)
            pe.wait_ge(c_free, CB["g_out"])
            pe.wait_ge(gws, 1)
            pe.wait_ge(gstd, 1)

            def spatial(c):
                pe.wait_ge(gvn, c + 1)
                if c >= 4:
                    pe.wait_ge(gta, c - 3)
                for t in range(NT):
                    m1 = mm(acc[c % 4][:, t * P:(t + 1) * P], vn[:, c % 2, t * P:(t + 1) * P], wsT[:, c // 2, :], start=True, stop=True)
                m1.then_inc(gsp, 1)
            for c in range(16):
                pe.wait_ge(gv, c + 1)
                if c >= 2:
                    pe.wait_ge(gvn, c - 1)
                for t in range(NT):
                    m1 = nc.tensor.transpose(aux[c % 2][:, t * P:(t + 1) * P], vT[:, c, t * P:(t + 1) * P], ident[:])
                m1.then_inc(gtr, 1)
                if c:
                    spatial(c - 1)
            spatial(15)
            pe.wait_ge(gta, 16)
            pe.wait_ge(glos, 16)

            def wide(name, xh, xl):
                with pe.Fori(0, 2) as i:
                    for cc in range(4):
                        for part in range(2):
                            tile(i * 8 + (TB[name] + 2 * cc + part), (2 * cc + part) % 4, acc[cc][:], chunks(xh, 8 * part, 8 * part + 8),
                                 chunks(xl, 8 * part, 8 * part + 8), start=part == 0, stop=part == 1,
                                 free=i * 4 + (CB[name] + cc - 3) if part == 0 else None)
            wide("g_out", ghi, glo)

            def mlp(layer):
                for half in range(2):
                    up, dn = f"up{layer}{'ab'[half]}", f"dn{layer}{'ab'[half]}"
                    pe.wait_ge(c_free, CB[up])
                    with pe.Fori(0, 4) as i:
                        for s in range(4):
                            tile(i * 4 + (TB[up] + s), s, acc[s][:], *H, free=i * 4 + (CB[up] + s - 3))
                    pe.wait_ge(c_free, CB[dn])
                    pe.wait_ge(m_rlo, 16 * (layer * 2 + half + 1))
                    wide(dn, mh, ml)
            norm_pe("mlp0")
            pe.wait_ge(h_lo, 5 * KD)
            mlp(0)

            norm_pe("fox")
            pe.wait_ge(h_lo, 6 * KD)
            pe.wait_ge(d_wf, 16)
            for part in (hh, hl):
                for k in range(KD):
                    m1 = mm(aux[0][0:16, :], wf[:, k, :], part[:, k, :].bitcast(F32), start=part is hh and k == 0, stop=part is hl and k == KD - 1)
            m1.then_inc(x_fl, 1)
            pe.wait_ge(c_free, CB["fox"])
            pe.wait_ge(x_lf, 1)
            def fox_pe(g, a_, b_, par):
                ap_ = 1 - par

                def half(n):
                    s, part = n // 2, n % 2
                    if part == 0 and a_ is not None:
                        freed, count = ((x_qk, g * 2 - 1), (x_qk, g * 2), (x_vt, g), (x_gt, g))[s]
                        pe.wait_ge(freed, count)
                    if n == 6:
                        pe.wait_ge(x_std, g * 2 + 2)
                    tile(g * RING + (TB["fox"] + s), s, acc[s][:], chunks(hh, 4 * part, 4 * part + 4), chunks(hl, 4 * part, 4 * part + 4),
                         blocks=4, first_block=4 * part, start=part == 0, stop=part == 1, last=part == 1)

                def score(n):
                    e, qi = n // 4, n % 4
                    if n == 0:
                        pe.wait_ge(x_qk, a_ * 2 + 2)
                        pe.wait_ge(d_crow[ap_], a_ * 32 + (64 if ap_ == 0 else 32))
                    if n >= 2 or b_ is not None:
                        pe.wait_ge(x_p, a_ * 8 + (n - 1))
                    mm(aux[qi % 2][:, 0:(qi + 1) * P], qa[:, ap_, e, qi * P:(qi + 1) * P], ka[:, ap_, e, 0:(qi + 1) * P],
                       start=True, stop=True).then_inc(x_s, 1)

                def weights_t(pair, n):
                    e, qi = n // 4, n % 4
                    pe.wait_ge(x_pn, pair * 8 + (n + 1))
                    if n or b_ is not None:
                        pe.wait_ge(x_pe, pair * 8 + n)
                    for t in range(qi + 1):
                        m1 = nc.tensor.transpose(aux[2][:, t * P:(t + 1) * P], fp[:, qi % 2, t * P:(t + 1) * P], ident[:])
                    m1.then_inc(x_pt, 1)

                def out(pair, buf, e):
                    pe.wait_ge(x_pe, pair * 8 + (4 * e + 4))
                    r = slice(64 * e, 64 * e + 64)
                    for t in range(NT):
                        m1 = mm(aux[3][r, t * P:L], fvn[:, buf, t, r], fpT[:, e, t, t * P:L], start=t == 0, stop=t == NT - 1)
                    m1.then_inc(x_o, 1)

                for n in range(8):
                    if a_ is not None:
                        score(n)
                    if g is not None:
                        half(n)
                    if b_ is not None and n == 0:
                        weights_t(b_, 7)
                    if b_ is not None and n == 1:
                        if a_ is not None:
                            pe.wait_ge(x_vn, a_ + 1)
                        out(b_, par, 1)
                    if a_ is not None and n:
                        weights_t(a_, n - 1)
                    if g is not None and n == 3:
                        if b_ is not None:
                            pe.wait_ge(x_og, b_ * 2 + 2)
                        if a_ is not None:
                            pe.wait_ge(x_vn, a_ + 1)
                        pe.wait_ge(x_sq, g * 2 + 1)
                        mm(aux[3][:], blk64[:], fsq[:, 0, :], start=True, stop=True).then_inc(x_ss, 1)
                    if g is not None and n == 4:
                        if a_ is not None:
                            pe.wait_ge(x_gt, g)
                        pe.wait_ge(x_sq, g * 2 + 2)
                        mm(acc[3][:], blk64[:], fsq[:, 1, :], start=True, stop=True).then_inc(x_ss, 1)
                    if n == 5 and a_ is not None:
                        if g is not None:
                            pe.wait_ge(x_std, g * 2 + 1)
                        if g is None:
                            pe.wait_ge(x_og, b_ * 2 + 2)
                        out(a_, ap_, 0)
                    if n == 6 and g is not None:
                        pe.wait_ge(x_vt, g + 1)
                        if a_ is not None:
                            pe.wait_ge(x_og, a_ * 2 + 1)
                        for t in range(NT):
                            m1 = nc.tensor.transpose(aux[3][:, t * P:(t + 1) * P], fvT[:, t * P:(t + 1) * P], ident[:])
                        m1.then_inc(x_vtr, 1)
            fox_steps(pe, fox_pe)
            pe.wait_ge(c_free, CB["fox_out"])
            pe.wait_ge(x_lo, KD)
            with pe.Fori(0, 2) as i:
                for s in range(4):
                    tile(i * 4 + (TB["fox_out"] + s), s, acc[s][:], chunks(foh, 0, KD), chunks(fol, 0, KD), free=i * 4 + (CB["fox_out"] + s - 3))
            norm_pe("mlp1")
            pe.wait_ge(h_lo, 7 * KD)
            mlp(1)

        @block.vector
        def _(v):
            V = nc.vector
            TT = V.tensor_tensor
            STT = V.scalar_tensor_tensor
            step = [0]

            def then(ins):
                step[0] += 1
                ins.then_inc(v_step, 1)
                v.wait_ge(v_step, step[0])

            def one(ap):
                return ap.rearrange("p (o n) -> p o n", o=1)

            def norm_dve(name):
                n = NORMS.index(name)
                src, W = norm_of(name)[0], norm_of(name)[5]
                for k in range(KD):
                    if k >= 2:
                        v.wait_ge(nm_sum, n * KD + k - 1)
                    TT(sq[k % 2][:, 0:W], src[:, k, 0:W], src[:, k, 0:W], ALU.mult).then_inc(nm_sq, 1)
                v.wait_ge(nm_std, n + 1)

            def norm_apply(name):
                n = PRE.index(name)
                src, g, sh, hi_, lo_, W = norm_of(name)

                def lo_of(k):
                    v.wait_ge(h_hi, n * KD + k + 1)
                    STT(out=lo_[:, k, :], in0=tmp[k % 2][:, 0:W], scalar=sh(k), in1=hi_[:, k, :].bitcast(F32), op0=ALU.add,
                        op1=ALU.subtract).then_inc(h_lo, 1)
                for k in range(KD):
                    if k >= 2:
                        lo_of(k - 2)
                        v.wait_ge(h_lo, n * KD + k - 1)
                    STT(out=tmp[k % 2][:, 0:W], in0=src[:, k, :], scalar=g(k), in1=rstd[:, 0:W], op0=ALU.mult, op1=ALU.mult).then_inc(nm_tmp, 1)
                lo_of(KD - 2)
                lo_of(KD - 1)
                v.wait_ge(h_lo, n * KD + KD)

            def residual(name):
                src, g = norm_of(name)[0:2]
                for k in range(KD):
                    then(STT(out=tmp[k % 2][:], in0=src[:, k, :], scalar=g(k), in1=rstd[:], op0=ALU.mult, op1=ALU.mult))
                    m1 = TT(xT[:, k, :], xT[:, k, :], tmp[k % 2][:], ALU.add)
                    if k == KD - 1:
                        then(m1)

            V.memset(hd[64:65, :], 1.0)
            v.wait_ge(d_cols, 16)
            TT(small[0:64, 4:6], col("lam_q", 0, 2, 64), col("lam_k", 0, 2, 64), ALU.mult).then_inc(lam_prod, 1)
            V.tensor_scalar(small[:, 6:7], col("subln"), 1.0 - LAM_INIT, None, ALU.mult)
            V.tensor_scalar(small[:, 7:8], col("q_g"), 0.125, None, ALU.mult)
            for j in range(2):
                v.wait_ge(f_mm, j + 1)
                then(V.tensor_scalar(targ[:], aux[j][0:64, :], col(("fb1", "fb2")[j], rows=64), col("freq", rows=64), ALU.add, ALU.mult))
                then(V.tensor_scalar(tn[:], targ[:], 1.0 / (2 * math.pi), MAGIC, ALU.mult, ALU.add))
                then(V.tensor_scalar(tn[:], tn[:], -MAGIC, None, ALU.add))
                then(STT(out=targ[:], in0=tn[:], scalar=-6.28125, in1=targ[:], op0=ALU.mult, op1=ALU.add))
                then(STT(out=targ[:], in0=tn[:], scalar=-(2 * math.pi - 6.28125), in1=targ[:], op0=ALU.mult, op1=ALU.add))
                V.tensor_scalar(tn[:], targ[:], 3.1415925, -3.1415925, ALU.min, ALU.max).then_inc(f_arg, 1)
            v.wait_ge(lam_exp, 1)
            then(TT(small[:, 2:3], small[:, 1:2], small[:, 0:1], ALU.subtract))
            then(V.tensor_scalar(small[:, 3:4], small[:, 2:3], -LAM_INIT, None, ALU.add))
            am = ada[:].rearrange("p (m w) -> p m w", w=2)

            def modulation(t0, t1):
                for t in range(t0, t1):
                    v.wait_ge(w_landed[t % RING], 16 * (t // RING) + 16)
                    for which in range(2 if t < 16 else 1):
                        m1 = STT(out=prod[:], in0=raw[t % RING][:].rearrange("p k n -> p (k n)"), scalar=1.0, in1=cvec[:, which, :],
                                 op0=ALU.mult, op1=ALU.mult, accum_out=am[:, t, which:which + 1])
                        if which == 0 and t < 16:
                            then(m1)
                    m1.then_inc(ada_used, 1)
                    v.wait_ge(ada_used, t + 1)

            v.wait_ge(c_silu, 1)
            v.wait_ge(d_filt2, 80)
            for p in range(8):
                modulation(p * ADA_P, (p + 1) * ADA_P)
                o, t = p // 4, p % 4
                v.wait_ge(f_ab, p + 1)
                TT(fab[:, p % 2, 0, :], aux[2 * (p % 2)][:], dec[:, t, :], ALU.mult)
                m1 = TT(fab[:, p % 2, 1, :], aux[2 * (p % 2) + 1][:], dec[:, 4 if t == 0 else t, :], ALU.mult)
                m1.then_inc(f_dec, 1)
                v.wait_ge(f_dec, p + 1)
                TT(fO[:, t, o * HY:(o + 1) * HY], fab[:, p % 2, 0, :], fab[:, p % 2, 1, :], ALU.subtract)
                m1 = TT(fE[:, t, o * HY:(o + 1) * HY], fab[:, p % 2, 0, :], fab[:, p % 2, 1, :], ALU.add)
                if t == 0:
                    then(m1)
                    m1 = TT(fE[0:1, 0, o * HY:(o + 1) * HY], fE[0:1, 0, o * HY:(o + 1) * HY], hb[:, o, :], ALU.add)
                m1.then_inc(f_eo, 1)

            modulation(ADA_P * 8, ADA_T)
            TT(am[:, :, 0], am[:, :, 0], col("b_ada", 0, 48), ALU.add)
            TT(am[:, 0:16, 1], am[:, 0:16, 1], col("b_ada", 0, 16), ALU.add).then_inc(c_free, RING)
            v.wait_ge(c_free, RING)
            STT(out=acol[:, 0:8], in0=am[:, 8:16, 0], scalar=1.0, in1=col("g_mix_pre", 0, 8), op0=ALU.add, op1=ALU.mult)
            STT(out=acol[:, 8:16], in0=am[:, 8:16, 1], scalar=1.0, in1=col("g_mix_pre", 0, 8), op0=ALU.add, op1=ALU.mult)
            TT(acol[:, 16:24], am[:, 16:24, 0], col("g_mix_post", 0, 8), ALU.mult)
            STT(out=acol[:, 24:32], in0=am[:, 32:40, 0], scalar=1.0, in1=col("g_ffn_pre", 0, 8), op0=ALU.add, op1=ALU.mult)
            then(TT(acol[:, 32:40], am[:, 40:48, 0], col("g_ffn_post", 0, 8), ALU.mult))
            V.memset(pad0[:, 0:1], 0.0)
            V.memset(pad0[:, L + 1:L + 2], 0.0)
            V.memset(pad1[:, 0:1], 0.0)
            V.memset(pad1[:, L + 1:L + 2], 0.0).then_inc(hy_pad, 1)
            v.wait_ge(d_x, 64)
            v.wait_ge(consts, 2)
            norm_dve("mix_pre")
            norm_apply("mix_pre")

            for u in range(12):
                v.wait_ge(c_free, CB["hyena"] + u + 1)
                p = pads[u % 2]
                dst = uT[:, u, :] if u < 8 else x2T[:, u - 8, :]
                w = lambda tap: col("conv_w", tap * 12 + u)
                then(V.tensor_scalar(tmp[0][:], p[:, 0:L], w(0), col("conv_b", u), ALU.mult, ALU.add))
                then(STT(out=tmp[1][:], in0=p[:, 1:L + 1], scalar=w(1), in1=tmp[0][:], op0=ALU.mult, op1=ALU.add))
                STT(out=dst, in0=p[:, 2:L + 2], scalar=w(2), in1=tmp[1][:], op0=ALU.mult, op1=ALU.add).then_inc(hy_conv, 1)
            v.wait_ge(hy_nat, 8)

            def z_lo(c):
                v.wait_ge(hy_zhi, c + 1)
                TT(zlo[:, c, :], tmp[c % 2][:], zhi[:, c, :].bitcast(F32), ALU.subtract).then_inc(hy_zlo, 1)
            for o in range(2):
                for f in range(4):
                    v.wait_ge(hy_u, o * 4 + f + 1)
                    uc, us = aux[2 * (f % 2)][:], aux[2 * (f % 2) + 1][:]
                    gr, gs = Gr[o][:, f, :], Gs[o][:, f, :]
                    t = [pw[:, f % 2, n, :] for n in range(4)]
                    TT(t[0], gr, uc, ALU.mult)
                    TT(t[1], gs, us, ALU.mult)
                    TT(t[2], gs, uc, ALU.mult)
                    TT(t[3], gr, us, ALU.mult).then_inc(hy_pw, 1)
                    v.wait_ge(hy_pw, o * 4 + f + 1)
                    TT(gr, t[0], t[1], ALU.subtract)
                    TT(gs, t[2], t[3], ALU.add).then_inc(hy_y, 1)
                for t in range(NT):
                    v.wait_ge(hy_inv, o * 4 + t + 1)
                    if o == 0:
                        TT(n0[:, t, :], acc[t][:], n1[:, t, :], ALU.mult).then_inc(hy_yd, 1)
                    else:
                        if t >= 2:
                            z_lo(t - 2)
                            v.wait_ge(hy_zlo, t - 1)
                        TT(tmp[t % 2][:], acc[t][:], x2T[:, t, :], ALU.mult).then_inc(hy_z, 1)
            z_lo(2)
            z_lo(3)
            v.wait_ge(d_att, 48)
            norm_dve("ctx")
            norm_apply("ctx")

            for u in range(8):
                v.wait_ge(c_free, CB["qkv"] + u + 1)
                if u:
                    v.wait_ge(q_done, u)
                TT(r1[:], qe[:, u % 2, 0:L], cosT[:], ALU.mult)
                v.wait_ge(q_rot, u + 1)
                then(TT(r2[:], aux[2][:], sinT[:], ALU.mult))
                TT(qT[:, u, :] if u < 4 else kT[:, u - 4, 0:L], r1[:], r2[:], ALU.add).then_inc(q_done, 1)

            for n in range(ATT_STEPS + 4):
                if n < ATT_STEPS:
                    for m in range(2):
                        b = att_col(n, m)
                        v.wait_ge(a_s, 2 * n + m + 1)
                        then(V.reduce_max(small[:, b + 2:b + 3], scores[m][:, 0:NKEY], AX.X))
                        V.tensor_scalar(small[:, b:b + 1], small[:, b + 2:b + 3], -0.125, None, ALU.mult).then_inc(a_mx, 1)
                if 1 <= n <= ATT_STEPS:
                    b0, b1 = att_col(n - 1, 0), att_col(n - 1, 1)
                    v.wait_ge(a_p, 2 * n)
                    V.reciprocal(small[:, b0 + 3:b0 + 4], small[:, b0 + 1:b0 + 2])
                    then(V.reciprocal(small[:, b1 + 3:b1 + 4], small[:, b1 + 1:b1 + 2]))
                    then(V.tensor_scalar(small[:, b1 + 2:b1 + 3], small[:, b1 + 3:b1 + 4], small[:, 3:4], None, ALU.mult))
                    p0, p1 = pp[:, (n - 1) % 2, 0, :], pp[:, (n - 1) % 2, 1, :]
                    then(V.tensor_scalar(p0, p0, small[:, b0 + 3:b0 + 4], None, ALU.mult))
                    STT(out=p0, in0=p1, scalar=small[:, b1 + 2:b1 + 3], in1=p0, op0=ALU.mult, op1=ALU.add).then_inc(a_cm, 1)
                if n > NT:
                    h = (n - 3) // NT - 1
                    if n % NT == 3:
                        v.wait_ge(a_std, h + 1)
                        if h:
                            v.wait_ge(a_lo, h)
                        STT(out=tmp[0][:], in0=aux[2][:], scalar=small[:, 6:7], in1=rstd[:], op0=ALU.mult, op1=ALU.mult).then_inc(a_tmp, 1)
                    if n % NT == 0 and h >= 0:
                        v.wait_ge(a_hi, h + 1)
                        TT(olo[:, h, :], tmp[0][:], ohi[:, h, :].bitcast(F32), ALU.subtract).then_inc(a_lo, 1)
            v.wait_ge(a_hi, HEADS)
            TT(olo[:, HEADS - 1, :], tmp[0][:], ohi[:, HEADS - 1, :].bitcast(F32), ALU.subtract).then_inc(a_lo, 1)

            with v.Fori(0, 2) as i:
                for jj in range(4):
                    b = jj % 2
                    v.wait_ge(m_sg, i * 4 + (jj + 1))
                    v.wait_ge(w_used, i * 12 + (TB["mix"] + 3 * jj + 3))
                    TT(mt[:, b, 0, :], sgm[:, b, 0, :], acc[2][:], ALU.mult)
                    TT(mt[:, b, 1, :], sgm[:, b, 1, :], acc[3][:], ALU.mult).then_inc(c_free, 4)
                    v.wait_ge(c_free, i * 16 + (CB["mix"] + 4 * jj + 4))
                    TT(mt[:, b, 0, :], mt[:, b, 0, :], mt[:, b, 1, :], ALU.add).then_inc(m_sum, 1)
                    v.wait_ge(m_hi, i * 4 + (jj + 1))
                    TT(mxl[:, bass.ds(i * 4 + jj, 1), :], one(mt[:, b, 0, :]), mxh[:, bass.ds(i * 4 + jj, 1), :].bitcast(F32),
                       ALU.subtract).then_inc(m_lo, 1)

            def evacuate(name, dst, n_tiles, add=False):
                with v.Fori(0, 2) as i:
                    for s in range(4):
                        v.wait_ge(w_used, i * (4 * n_tiles) + (TB[name] + n_tiles * (s + 1)))
                        d = dst[:, bass.ds(i * 4 + s, 1), :]
                        if add:
                            TT(d, one(acc[s][:]), d, ALU.add).then_inc(c_free, 1)
                        else:
                            V.tensor_copy(d, one(acc[s][:])).then_inc(c_free, 1)
                v.wait_ge(c_free, CB[name] + 8)
            evacuate("wout", mo, 1)
            norm_dve("mix_post")
            residual("mix_post")
            norm_dve("ffn_pre")
            norm_apply("ffn_pre")
            with v.Fori(0, FC // 2) as i:
                for p in range(2):
                    v.wait_ge(s_silu, i * 2 + (p + 1))
                    v.wait_ge(w_used, i * 4 + (TB["gateup"] + 2 * p + 2))
                    TT(tmp[p][:], sil[:, p, :], acc[2 * p + 1][:], ALU.mult).then_inc(c_free, 2)
                    v.wait_ge(s_hi, i * 2 + (p + 1))
                    TT(hidl[:, bass.ds(i * 2 + p, 1), :], one(tmp[p][:]), hidh[:, bass.ds(i * 2 + p, 1), :].bitcast(F32),
                       ALU.subtract).then_inc(s_lo, 1)
            evacuate("down", ff_out, 3)
            norm_dve("ffn_post")
            residual("ffn_post")
            norm_dve("g_mix")
            norm_apply("g_mix")

            v.wait_ge(gmd, 1)
            for c in range(16):
                TT(vT[:, c, :], vT[:, c, :], mean[:], ALU.subtract).then_inc(gxc, 1)
            v.wait_ge(gstd, 1)
            for c in range(16):
                STT(out=vT[:, c, :], in0=vT[:, c, :], scalar=col("ln_g", c), in1=lrs[:], op0=ALU.mult, op1=ALU.mult).then_inc(gvt, 1)
            v.wait_ge(gws, 1)

            def g_lo(c):
                v.wait_ge(ghis, c + 1)
                TT(glo[:, c, :], gt[:, c % 2, 1, :], ghi[:, c, :].bitcast(F32), ALU.subtract).then_inc(glos, 1)
            for c in range(16):
                if c >= 2:
                    g_lo(c - 2)
                v.wait_ge(gsp, c + 1)
                TT(gt[:, c % 2, 0, :].rearrange("p (t n) -> p t n", n=P), acc[c % 4][:].rearrange("p (t n) -> p t n", n=P),
                   bsb[:, c // 2:c // 2 + 1, :].to_broadcast([P, NT, P]), ALU.add).then_inc(gta, 1)
                v.wait_ge(gta, c + 1)
                TT(gt[:, c % 2, 1, :], gt[:, c % 2, 0, :], guT[:, c, :], ALU.mult).then_inc(gtm, 1)
            g_lo(14)
            g_lo(15)
            evacuate("g_out", xT, 2, add=True)
            norm_dve("mlp0")
            norm_apply("mlp0")

            def mlp(layer):
                for half in range(2):
                    n = 16 * (layer * 2 + half)
                    with v.Fori(0, 4) as i:
                        for s in range(4):
                            v.wait_ge(c_free, i * 4 + (CB[f"up{layer}{'ab'[half]}"] + s + 1))
                            TT(tmp[s % 2][:], sq[s % 2][:], sq[s % 2][:], ALU.mult).then_inc(m_rsq, 1)
                            v.wait_ge(m_rhi, i * 4 + (n + s + 1))
                            TT(ml[:, bass.ds(i * 4 + s, 1), :], one(tmp[s % 2][:]), mh[:, bass.ds(i * 4 + s, 1), :].bitcast(F32),
                               ALU.subtract).then_inc(m_rlo, 1)
                    evacuate(f"dn{layer}{'ab'[half]}", xT, 2, add=True)
            mlp(0)

            V.memset(qa[64:66, :, :], 1.0).then_inc(x_ini, 1)
            V.memset(ka[64:66, :, :], 1.0).then_inc(x_ini, 1)
            norm_dve("fox")
            norm_apply("fox")
            v.wait_ge(x_lf, 4)
            then(V.memset(lf[:, 2, :], 1.0))
            then(STT(out=lf[:, 3, :], in0=lf[:, 0, :], scalar=0.0, in1=lf[:, 1, :], op0=ALU.min, op1=ALU.subtract))
            V.tensor_tensor_scan(cpos[:], lf[:, 2, :], lf[:, 3, :], 0.0, ALU.mult, ALU.add).then_inc(x_c, 1)
            v.wait_ge(x_c, 1)
            V.tensor_scalar(cneg[:], cpos[:], -1.0, None, ALU.mult).then_inc(x_c, 1)
            v.wait_ge(x_c, 2)
            def fox_dve(g, a_, b_, par):
                ap_ = 1 - par

                def head_out(pair, buf, e):
                    v.wait_ge(x_o, pair * 2 + (e + 1))
                    r = slice(64 * e, 64 * e + 64)
                    TT(fog[r, :], aux[3][r, :], fsg[r, buf, :], ALU.mult).then_inc(x_og, 1)

                def normalize(s):
                    rs = (std, rstd)[s]
                    v.wait_ge(x_std, g * 2 + (s + 1))
                    for e in range(2):
                        r = slice(64 * e, 64 * e + 64)
                        g_ = small[r, 7:8] if s == 0 else cols[r, COLS["k_g"]:COLS["k_g"] + 1]
                        m1 = STT(out=(qa, ka)[s][0:64, par, e, :], in0=acc[s][r, :], scalar=g_, in1=rs[r, :], op0=ALU.mult, op1=ALU.mult)
                    m1.then_inc(x_qk, 1)
                    v.wait_ge(x_qk, g * 2 + (s + 1))
                for n in range(8):
                    if a_ is not None:
                        e, qi = n // 4, n % 4
                        W = (qi + 1) * P
                        b = aux[qi % 2]
                        v.wait_ge(x_s, a_ * 8 + (n + 1))
                        TT(b[:, qi * P:W], b[:, qi * P:W], cmask[:], ALU.add).then_inc(x_mk, 1)
                        v.wait_ge(x_mk, a_ * 8 + (n + 1))
                        V.reduce_max(small[:, 56 + n:57 + n], b[:, 0:W], AX.X).then_inc(x_rc, 1)
                        v.wait_ge(x_rc, a_ * 8 + (n + 1))
                        V.tensor_scalar(small[:, 40 + n:41 + n], small[:, 56 + n:57 + n], -1.0, None, ALU.mult).then_inc(x_mx, 1)
                        if n == 0:
                            v.wait_ge(x_gt, a_ + 1)
                            V.tensor_scalar(fsg[:, ap_, :], fsg[:, ap_, :], 1e18, 1.0, ALU.min, ALU.add).then_inc(x_g1, 1)
                        if n == 6:
                            v.wait_ge(x_sg, a_ + 1)
                            head_out(a_, ap_, 0)
                    if b_ is not None:
                        if n == 2:
                            head_out(b_, par, 1)
                        if n == 4:
                            v.wait_ge(x_hi, b_ + 1)
                            TT(fol[:, bass.ds(b_, 1), :], one(fog[:]), foh[:, bass.ds(b_, 1), :].bitcast(F32), ALU.subtract).then_inc(x_lo, 1)
                    if g is not None and n in (5, 6):
                        normalize(n - 5)
                    if a_ is not None:
                        v.wait_ge(x_p, a_ * 8 + (n + 1))
                        V.reciprocal(small[:, 64 + n:65 + n], small[:, 48 + n:49 + n]).then_inc(x_rd, 1)
                        v.wait_ge(x_rd, a_ * 8 + (n + 1))
                        V.tensor_scalar(fp[:, qi % 2, 0:W], fp[:, qi % 2, 0:W], small[:, 64 + n:65 + n], None, ALU.mult).then_inc(x_pn, 1)
            fox_steps(v, fox_dve)
            v.wait_ge(x_lo, 8)
            V.memset(tmp[1][:, 0:1], 0.0).then_inc(c_free, 32)
            evacuate("fox_out", xT, 1, add=True)
            norm_dve("mlp1")
            norm_apply("mlp1")
            mlp(1)


def _tables(np):
    k = np.arange(L) + 0.5
    s = np.arange(L)
    w = 2 * np.pi / (2 * L)
    dft = np.stack([np.cos(w * np.outer(s, k)), np.sin(w * np.outer(s, k)),
                    np.cos(w * np.outer(s + 0.5, k)), np.sin(w * np.outer(s + 0.5, k))])
    dft = dft.reshape(4, NT, P, L).transpose(0, 2, 1, 3)
    bands = 16
    t = np.linspace(0.0, 1.0, L)
    ang = np.outer(np.linspace(1e-4, bands - 1, bands), 2 * np.pi / L * s)
    z = np.concatenate([t[None], np.cos(ang), -np.sin(ang)])
    deltas = np.abs(np.linspace(math.log(1e-2) / 1.5, math.log(1e-2) / 0.3, HY))
    dec = np.exp(-np.outer(t, deltas)).reshape(NT, P, HY)
    back = dec[0].copy()
    back[0] = 0.0
    dec = np.concatenate([dec, back[None]]).transpose(1, 0, 2)
    d = np.arange(P)
    pos = np.where((d % 64 < 32)[:, None], s[None] // 64, s[None] % 64)
    a = pos * (10000.0 ** (-(d % 16) / 16.0))[:, None]
    rope = np.stack([np.cos(a), np.sin(a)])
    rot = np.zeros((P, P))
    for m in range(P):
        if m % 32 < 16:
            rot[m + 16, m] = -1.0
        else:
            rot[m - 16, m] = 1.0
    cmask = np.where(d[:, None] >= d[None, :], 0.0, -1e30)
    out = {"dft": dft, "zT": z, "decay": dec, "rope": rope, "rot": rot, "cmask": cmask, "ident": np.eye(P)}
    return {n: np.ascontiguousarray(x.astype(np.float32)) for n, x in out.items()}


def _blocks(np, w):
    k, m = w.shape
    return w.reshape(k // P, P, m // P, P).transpose(2, 1, 0, 3)


def _layout(np, x):
    w_in = _blocks(np, x["w_in"][0])
    gate, up = _blocks(np, x["w_ffn_gate"][0]), _blocks(np, x["w_ffn_up"][0])
    hy_up, att_up = _blocks(np, x["w_hy_up"][0]), _blocks(np, x["w_att_up"][0])
    down = _blocks(np, x["w_ffn_down"][0])
    g_in, g_out = _blocks(np, x["gmlp_w_in_2"][0]), _blocks(np, x["gmlp_w_out_2"][0])
    fox = _blocks(np, x["fox_w_in_2"][0][:, :4096])
    n = ADA_T + TILES
    w = np.zeros((n, P, 8, P), np.float32)
    w[:ADA_T] = x["w_ada"][0].T.reshape(ADA_T, P, 8, P)
    w[ADA_T:ADA_T + 24] = w_in[:24]
    b = ADA_T + TB["mix"]
    w[b:b + 24:3] = w_in[24:32]
    w[b + 1:b + 24:3] = w_in[32:40]
    w[b + 2:b + 24:3, :, :4] = hy_up
    w[b + 2:b + 24:3, :, 4:] = att_up
    b = ADA_T + TB["wout"]
    w[b:b + 8] = _blocks(np, x["w_out"][0])
    b = ADA_T + TB["gateup"]
    w[b:b + 44:2] = gate
    w[b + 1:b + 44:2] = up
    b = ADA_T + TB["down"]
    for p in range(3):
        k = down[:, :, 8 * p:8 * p + 8]
        w[b + p:b + 24:3, :, :k.shape[2]] = k
    b = ADA_T + TB["g_in"]
    w[b:b + 16] = g_in[16:]
    w[b + 16:b + 32] = g_in[:16]

    def wide(name, m):
        b = ADA_T + TB[name]
        w[b:b + 16:2] = m[:, :, :8]
        w[b + 1:b + 16:2] = m[:, :, 8:]
    wide("g_out", g_out)
    for layer in range(2):
        w1, w2 = _blocks(np, x["mlp_w1_2"][layer]), _blocks(np, x["mlp_w2_2"][layer])
        for half in range(2):
            b = ADA_T + TB[f"up{layer}{'ab'[half]}"]
            w[b:b + 16] = w1[16 * half:16 * half + 16]
            wide(f"dn{layer}{'ab'[half]}", w2[:, :, 16 * half:16 * half + 16])
    b = ADA_T + TB["fox"]
    for p in range(4):
        w[b + p:b + 32:4] = fox[8 * p:8 * p + 8]
    b = ADA_T + TB["fox_out"]
    w[b:b + 8] = _blocks(np, x["fox_w_out_2"][0])

    cols = np.zeros((P, NCOLS), np.float32)

    def put(name, v, off=0, rows=P):
        v = np.asarray(v).reshape(-1, rows).T
        cols[:rows, COLS[name] + off:COLS[name] + off + v.shape[1]] = v
    for name in ("g_mix_pre", "g_mix_post", "g_ffn_pre", "g_ffn_post"):
        put(name, x[name][0])
    put("b_ada", x["b_ada"][0])
    put("conv_w", x["hy_conv_w"][0])
    put("conv_b", x["hy_conv_b"][0])
    put("subln", x["att_subln_g"][0])
    put("ln_g", x["gmlp_ln_g_2"][0])
    put("ln_b", x["gmlp_ln_b_2"][0])
    put("mixn", x["mix_norm_g_2"])
    put("mlpn", x["mlp_norm_g_2"])
    for name, src in (("q_g", "fox_q_g_2"), ("k_g", "fox_k_g_2")):
        cols[:64, COLS[name]] = cols[64:, COLS[name]] = x[src][0]
    put("b_f", x["fox_b_f_2"][0], rows=16)
    for j in (1, 2):
        put("lam_q", x[f"lambda_q{j}"][0], j - 1, 64)
        put("lam_k", x[f"lambda_k{j}"][0], j - 1, 64)
    put("fb1", x["hy_f_b1"][0], rows=64)
    put("fb2", x["hy_f_b2"][0], rows=64)
    put("freq", x["hy_f_freq"][0], rows=64)

    def chunked(m):
        return np.ascontiguousarray(m.T.reshape(-1, P, m.shape[0]).transpose(1, 0, 2))
    return {
        "w": w, "cols": cols, "xT": chunked(x["x"][0]), "ctxT": chunked(x["ctx"][0]),
        "fw1": x["hy_f_w1"][0], "fw2": x["hy_f_w2"][0], "fw3": np.concatenate([x["hy_f_w3"][0], x["hy_f_b3"]]),
        "hbias": x["hy_bias"],
        "cvec": np.ascontiguousarray(np.broadcast_to(np.stack([x["c"][0], x["c_ctx"].reshape(-1)]), (P, 2, D))),
        "ws": np.ascontiguousarray(x["gmlp_w_s_2"][0].transpose(2, 0, 1)),
        "bs": np.ascontiguousarray(np.broadcast_to(x["gmlp_b_s_2"], (P, 8, P))),
        "wf": np.ascontiguousarray(x["fox_w_in_2"][0][:, 4096:].reshape(KD, P, 16).transpose(1, 0, 2)),
    }


def kernel(**inputs):
    import numpy as np
    import concourse.bacc as bacc
    from concourse.bass_utils import run_bass_kernel_spmd

    x = {n: np.asarray(v) for n, v in inputs.items()}
    arrays = {**_tables(np), **_layout(np, x)}
    nc = bacc.Bacc("TRN2", target_bir_lowering=False, num_devices=1)
    args, given = {}, {}
    for n, v in arrays.items():
        given[f"in_{n}"] = np.ascontiguousarray(v)
        args[n] = nc.dram_tensor(f"in_{n}", v.shape, F32, kind="ExternalInput").ap()
    args["scratch"] = nc.dram_tensor("scratch", (2, 16, L), F32, kind="Internal").ap()
    args["out"] = nc.dram_tensor("out", (P, KD, L), F32, kind="ExternalOutput").ap()
    build(nc, args)
    got = run_bass_kernel_spmd(nc, [given], core_ids=[0]).results[0]["out"]
    return np.ascontiguousarray(got.transpose(2, 1, 0).reshape(1, L, D))
```

```python
import math
from contextlib import ExitStack

import concourse.bass as bass
from concourse import mybir

F32 = mybir.dt.float32
F32R = mybir.dt.float32r
ALU = mybir.AluOpType
ACT = mybir.ActivationFunctionType
AX = mybir.AxisListType

P = 128
D = 1024
KD = D // P
L = 512
NT = L // P
CTX = 256
NKEY = L + CTX
KT = NKEY // P
HEADS = 4
HY = 512
HC = HY // P
FF = 2816
FC = FF // P
EPS = 1e-6
LN_EPS = 1e-5
LAM_INIT = 0.2
MAGIC = 12582912.0
RING = 4

ADA_T = 48
CTX_T = 16
CTX_POOL = ADA_T // RING


def ada_chunk(u):
    return u // RING if u % RING == 0 else CTX_POOL + u // RING * 3 + u % RING - 1
PHASES = [("hyena", 12, 12), ("qkv", 12, 12), ("mix", 24, 32), ("wout", 8, 8), ("gateup", 44, 44),
          ("down", 24, 8), ("g_in", 32, 32), ("g_out", 16, 8),
          ("up0a", 16, 16), ("dn0a", 16, 8), ("up0b", 16, 16), ("dn0b", 16, 8),
          ("fox", 32, 32), ("fox_out", 8, 8),
          ("up1a", 16, 16), ("dn1a", 16, 8), ("up1b", 16, 16), ("dn1b", 16, 8)]
TB, CB = {}, {}
_t, _c = 0, RING
for _n, _nt, _nc in PHASES:
    TB[_n], CB[_n] = _t, _c
    _t += _nt
    _c += _nc
TILES = _t

COLS, NCOLS = {}, 0
for _n, _w in [("g_mix_pre", 8), ("g_mix_post", 8), ("g_ffn_pre", 8), ("g_ffn_post", 8), ("b_ada", 48),
               ("conv_w", 36), ("conv_b", 12), ("subln", 1), ("ln_g", 16), ("ln_b", 16),
               ("mixn", 16), ("mlpn", 16), ("q_g", 1), ("k_g", 1), ("b_f", 1),
               ("lam_q", 2), ("lam_k", 2), ("fb1", 1), ("fb2", 1), ("freq", 1)]:
    COLS[_n] = NCOLS
    NCOLS += _w

AFTER_POST = ["ffn_pre", "g_mix"]
NORMS = ["mix_pre", "ctx", "mix_post", "ffn_pre", "ffn_post", "g_mix", "mlp0", "fox", "mlp1"]


def build(nc, a):
    ctx = ExitStack()
    with ctx:
        def sb(name, shape, dt=F32):
            return ctx.enter_context(nc.sbuf_tensor(name, shape, dt))

        def sem(name):
            return ctx.enter_context(nc.semaphore(name))

        def overlay(start, specs):
            with ExitStack() as s:
                if start:
                    s.enter_context(nc.sbuf_tensor(f"gap_{specs[0][0]}", [P, start // 4], F32))
                return [s.enter_context(nc.sbuf_tensor(n, sh, dt)) for n, sh, dt in specs]

        KB = 1024
        raw = [sb(f"w_raw{i}", [P, 8, P]) for i in range(RING)]
        whi = [sb(f"w_hi{i}", [P, 8, P], F32R) for i in range(RING)]
        cprod = overlay(0, [(f"ada_ctx_prod{i}", [P, D], F32) for i in range(2)])
        wlo = [sb(f"w_lo{i}", [P, 8, P], F32R) for i in range(RING)]
        xT = sb("xT", [P, KD, L])
        cols = sb("cols", [P, NCOLS])
        ada = sb("ada", [P, ADA_T * 2])
        ones = sb("ones", [P, P])
        ones_d = sb("ones_d", [P, P])
        ones_hd = sb("ones_hd", [P, P])
        blk64 = sb("blk64", [P, P])
        ident = sb("ident", [P, P])
        rot = sb("rot", [P, P])
        cmask = sb("cmask", [P, P])
        acol = sb("acol", [P, 64])
        small = sb("small", [P, 96])
        zcol = sb("zcol", [P, 1])
        epsc = sb("epsc", [P, 2])
        work = sb("work", [P, 4, L])
        sq = [work[:, i, :] for i in range(2)]
        tmp = [work[:, 2 + i, :] for i in range(2)]
        std = sb("std", [P, L])
        ssq = sb("ssq", [P, L])
        rstd = sb("rstd", [P, L])

        cvec = work[:].rearrange("p (w a) n -> p w (a n)", w=2)

        HB = 0
        BIG = 32 * KB
        hh, hl = overlay(HB, [("h_hi", [P, KD, L], F32R), ("h_lo", [P, KD, L], F32R)])
        fE, fO = overlay(HB, [("filt_e", [P, NT, 2 * HY], F32), ("filt_o", [P, NT, 2 * HY], F32)])
        (ff_out,) = overlay(HB, [("ff_out", [P, KD, L], F32)])
        (ghi,) = overlay(HB, [("gate_hi", [P, 16, L], F32R)])
        Gr0, Gs0, Gr1, Gs1 = overlay(BIG, [(n, [P, NT, HY], F32) for n in ("gr0", "gs0", "gr1", "gs1")])
        Gr, Gs = [Gr0, Gr1], [Gs0, Gs1]
        C0, S0, dec, fw3, zT, fw1, fw2, hd, targ, tn, fab = overlay(BIG + 32 * KB, [
            ("c_int", [P, NT, HY], F32), ("s_int", [P, NT, HY], F32), ("decay", [P, 5, HY], F32),
            ("fw3", [65, 2048], F32), ("zT", [33, L], F32), ("fw1", [33, 64], F32), ("fw2", [64, 64], F32),
            ("hd", [65, L], F32), ("targ", [64, L], F32), ("tn", [64, L], F32), ("fab", [P, 2, 2, HY], F32)])
        (hb,) = overlay(BIG + 8 * KB, [("hbias", [1, 2, HY], F32)])
        (prod,) = overlay(BIG + 83 * KB, [("ada_prod", [P, 2, D], F32)])
        (xsq,) = overlay(BIG, [("x_squares", [P, 2, L], F32)])
        Cm, Sm, n0, n1, x2T, uT, pad0, pad1 = overlay(BIG + 32 * KB, [
            ("c_half", [P, NT, HY], F32), ("s_half", [P, NT, HY], F32), ("n0", [P, NT, HY], F32),
            ("n1", [P, NT, HY], F32), ("x2T", [P, HC, L], F32), ("uT", [P, 8, L], F32),
            ("pad0", [P, L + 2], F32), ("pad1", [P, L + 2], F32)])
        pads = [pad0, pad1]
        (pw,) = overlay(BIG + 72 * KB, [("pointwise", [P, 2, 4, L], F32)])
        zhi, zlo, ohi, olo = overlay(BIG, [("z_hi", [P, HC, L], F32R), ("z_lo", [P, HC, L], F32R),
                                           ("o_hi", [P, HC, L], F32R), ("o_lo", [P, HC, L], F32R)])
        hch, hcl, qT, kT, vN, cxT, cosT, sinT, qe, r1, r2 = overlay(BIG + 16 * KB, [
            ("hc_hi", [P, KD, CTX], F32R), ("hc_lo", [P, KD, CTX], F32R), ("qT", [P, HEADS, L], F32),
            ("kT", [P, HEADS, NKEY], F32), ("vN", [P, HEADS, KT, P], F32), ("ctxT", [P, KD, CTX], F32),
            ("cosT", [P, L], F32), ("sinT", [P, L], F32), ("qe", [P, 2, NKEY], F32),
            ("r1", [P, L], F32), ("r2", [P, L], F32)])
        pp, aT = overlay(BIG + 64 * KB, [("pp", [P, 2, 2, NKEY], F32), ("aT", [P, KT, L], F32)])
        mxh, mxl, sgm, mt = overlay(BIG + 32 * KB, [("mixed_hi", [P, KD, L], F32R), ("mixed_lo", [P, KD, L], F32R),
                                              ("sgm", [P, 2, 2, L], F32), ("mt", [P, 2, 2, L], F32)])
        (mo,) = overlay(BIG, [("mix_out", [P, KD, L], F32)])
        hidh, hidl, sil = overlay(BIG, [("hid_hi", [P, FC, L], F32R), ("hid_lo", [P, FC, L], F32R),
                                        ("silu", [P, 2, L], F32)])
        vT, guT, wsT, bsb, vn, gt, mean, lrs = overlay(BIG, [
            ("g_v", [P, 16, L], F32), ("g_u", [P, 16, L], F32), ("wsT", [P, 8, P], F32), ("bsb", [P, 8, P], F32),
            ("vn", [P, 2, L], F32), ("gt", [P, 2, 2, L], F32), ("lmean", [P, L], F32), ("lrs", [P, L], F32)])
        (glo,) = overlay(BIG, [("gate_lo", [P, 16, L], F32R)])
        mh, ml, = overlay(BIG, [("mlp_hi", [P, 16, L], F32R), ("mlp_lo", [P, 16, L], F32R)])
        foh, fol, fsq, qa, ka, fvT, fvn, fsg, fp, fog, fpT = overlay(BIG, [
            ("fo_hi", [P, KD, L], F32R), ("fo_lo", [P, KD, L], F32R), 
            ("fsq", [P, 2, L], F32),
            ("qa", [66, 2, 2, L], F32), ("ka", [66, 2, 2, L], F32), ("fvT", [P, L], F32), ("fvn", [P, 2, NT, P], F32),
            ("fsg", [P, 2, L], F32), ("fp", [P, 2, L], F32), ("fog", [P, L], F32), ("fpT", [P, 2, NT, L], F32)])
        wf, wfh, wfl = overlay(BIG + 88 * KB, [("wf", [P, KD, 16], F32), ("wf_hi", [P, KD, 16], F32R), ("wf_lo", [P, KD, 16], F32R)])
        lf, cpos, cneg = overlay(BIG + 76 * KB, [("lf", [16, 4, L], F32), ("cpos", [16, L], F32), ("cneg", [16, L], F32)])

        with ExitStack() as s:
            bank = [s.enter_context(nc.psum_tensor(f"bank{i}", [P, L], F32)) for i in range(8)]
        acc, aux = bank[0:4], bank[4:8]
        with ExitStack() as s:
            sc0, sc1, trT = (s.enter_context(nc.psum_tensor(n, [P, 2 * L], F32)) for n in ("scores0", "scores1", "weightsT"))
        scores = [sc0, sc1]

        w_landed = [sem(f"w_landed{i}") for i in range(RING)]
        w_hi, w_lo, w_used, ada_used, c_free = (sem(n) for n in ("w_hi", "w_lo", "w_used", "ada_used", "c_free"))
        d_cols, d_filt, d_dft, d_att, d_x, d_ws, d_wf, d_c, d_out, d_filt2 = (sem(n) for n in (
            "d_cols", "d_filt", "d_dft", "d_att", "d_x", "d_ws", "d_wf", "d_c", "d_out", "d_filt2"))
        f_odd = sem("f_odd")
        d_cvec, d_dft0, c_prod, c_sum = (sem(n) for n in ("d_cvec", "d_dft0", "ada_ctx_product", "ada_ctx_sum"))
        consts, c_silu, ada_ready, lam_prod, lam_mm, lam_exp, lam_ready = (sem(n) for n in (
            "consts", "c_silu", "ada_ready", "lam_prod", "lam_mm", "lam_exp", "lam_ready"))
        f_mm, f_arg, f_sin, f_ab, f_eo, g_mm, g_used, f_e0, f_dec = (sem(n) for n in (
            "f_mm", "f_arg", "f_sin", "f_ab", "f_eo", "g_mm", "g_used", "f_e0", "f_dec"))
        nm_sq, nm_sum, nm_std, nm_rstd, nm_tmp, h_hi, h_lo, x_new = (sem(n) for n in (
            "nm_sq", "nm_sum", "nm_std", "nm_rstd", "nm_tmp", "h_hi_s", "h_lo_s", "x_new"))
        nm_ssq, nm_dsq, nm_used, x_squared, x_summed = (sem(n) for n in ("nm_ssq", "nm_dsq", "nm_used", "x_squared", "x_summed"))
        hy_pad, hy_conv, hy_tr, hy_nat = (sem(n) for n in ("hy_pad", "hy_conv", "hy_tr", "hy_nat"))
        hy_u, hy_pw, hy_y, hy_inv, hy_yd, hy_z, hy_zhi, hy_zlo = (sem(n) for n in (
            "hy_u", "hy_pw", "hy_y", "hy_inv", "hy_yd", "hy_z", "hy_zhi", "hy_zlo"))
        v_step = sem("v_step")
        x_sg, x_g1, x_gl, x_ln, log_done = (sem(n) for n in ("x_sg", "x_g1", "x_gl", "x_ln", "log_done"))
        d_crow = [sem(f"d_crow{i}") for i in range(2)]
        kv_ev, q_rot, q_done, v_tr, v_nat = (sem(n) for n in (
            "kv_ev", "q_rot", "q_done", "v_tr", "v_nat"))
        a_s, a_mx, a_p, a_cm, a_tr, a_ev, a_o, a_sq, a_ss, a_std, a_tmp, a_hi, a_lo, a_ch = (sem(n) for n in (
            "a_s", "a_mx", "a_p", "a_cm", "a_tr", "a_ev", "a_o", "a_sq", "a_ss", "a_std", "a_tmp", "a_hi", "a_lo", "a_ch"))
        m_sg, m_t, m_sum, m_hi, m_lo = (sem(n) for n in ("m_sg", "m_t", "m_sum", "m_hi", "m_lo"))
        o_ev = sem("o_ev")
        s_silu, s_prod, s_hi, s_lo, f_ev = (sem(n) for n in ("s_silu", "s_prod", "s_hi", "s_lo", "f_ev"))
        gl, gmean, gxc, gsq, gss, gstd, grs, gvt, gv, gtr, gvn, gsp, gta, gtm, ghis, glos, gws = (sem(n) for n in (
            "g_gelu", "g_mean_mm", "g_xc", "g_sq", "g_ss", "g_std", "g_rs", "g_vt", "g_vdone", "g_tr", "g_vn",
            "g_sp", "g_ta", "g_tm", "g_his", "g_los", "g_ws"))
        gmd, gsm = sem("g_mean_done"), sem("g_sum")
        m_r, m_rsq, m_rhi, m_rlo, m_dn = (sem(n) for n in ("m_relu", "m_rsq", "m_rhi", "m_rlo", "m_dn"))
        x_fl, x_lf, x_c, x_ini = (sem(n) for n in ("x_fl", "x_lf", "x_c", "x_ini"))
        x_wfh, x_wfl = sem("x_wfh"), sem("x_wfl")
        x_sq, x_ss, x_std, x_qk, x_vt, x_vtr, x_vn, x_gt, x_s, x_mk, x_mx, x_p, x_rc, x_rd, x_pn, x_pt, x_pe, x_o, x_og, x_hi, x_lo = (
            sem(n) for n in ("x_sq", "x_ss", "x_std", "x_qk", "x_vt", "x_vtr", "x_vn", "x_gt", "x_s", "x_mk",
                             "x_mx", "x_p", "x_rc", "x_rd", "x_pn", "x_pt", "x_pe", "x_o", "x_og", "x_hi", "x_lo"))

        def col(name, k=0, n=1, rows=P):
            return cols[0:rows, COLS[name] + k:COLS[name] + k + n]

        ACOL = {"mix_pre": 0, "ctx": 8, "mix_post": 16, "ffn_pre": 24, "ffn_post": 32}

        def adac(part, k, which=0):
            m = (part * KD + k) * 2 + which
            return ada[:, m:m + 1]

        def norm_of(name):
            if name == "ctx":
                return cxT, (lambda k: acol[:, 8 + k:9 + k]), (lambda k: adac(0, k, 1)), hch, hcl, CTX
            if name == "mix_pre":
                return xT, (lambda k: acol[:, k:k + 1]), (lambda k: adac(0, k)), hh, hl, L
            if name == "ffn_pre":
                return xT, (lambda k: acol[:, 24 + k:25 + k]), (lambda k: adac(3, k)), hh, hl, L
            if name == "mix_post":
                return mo, (lambda k: acol[:, 16 + k:17 + k]), None, None, None, L
            if name == "ffn_post":
                return ff_out, (lambda k: acol[:, 32 + k:33 + k]), None, None, None, L
            g, o = {"g_mix": ("mixn", 0), "mlp0": ("mlpn", 0), "fox": ("mixn", 8), "mlp1": ("mlpn", 8)}[name]
            return xT, (lambda k: col(g, o + k)), (lambda k: zcol[:, 0:1]), hh, hl, L

        def fox_steps(engine, step):
            step(0, None, None, 0)
            step(1, 0, None, 1)
            with engine.Fori(0, 3) as j:
                step(j * 2 + 2, j * 2 + 1, j * 2, 0)
                step(j * 2 + 3, j * 2 + 2, j * 2 + 1, 1)
            step(None, 7, 6, 0)
            step(None, None, 7, 1)

        ATT_STEPS = HEADS * NT

        def att_col(n, m):
            return 8 + 8 * (n % 2) + 4 * m

        SUMMED = [n for n in NORMS[1:] if n not in AFTER_POST]
        EVAC = SUMMED[1:]
        POST = ["mix_post", "ffn_post"]
        PRE = [n for n in NORMS if n not in ("mix_post", "ffn_post")]

        block = ctx.enter_context(nc.Block())

        @block.sync
        def _(sp):
            sp.dma_start(cols[:], a["cols"]).then_inc(d_cols, 16)
            sp.dma_start(zT[:], a["zT"]).then_inc(d_filt, 16)
            sp.dma_start(fw1[:], a["fw1"]).then_inc(d_filt, 16)
            sp.dma_start(fw2[:], a["fw2"]).then_inc(d_filt, 16)
            sp.dma_start(xT[:], a["xT"]).then_inc(d_x, 16)
            sp.dma_start(fw3[:], a["fw3"]).then_inc(d_filt2, 16)
            sp.dma_start(dec[:], a["decay"]).then_inc(d_filt2, 16)
            sp.dma_start(hb[:], a["hbias"]).then_inc(d_filt2, 16)
            sp.dma_start(cvec, a["cvec"]).then_inc(d_cvec, 16)
            for s in range(RING):
                sp.dma_start(raw[s][:], a["w"][s:s + 1].rearrange("o p k n -> p (o k) n")).then_inc(w_landed[s], 16)
            sp.dma_start(C0[:], a["dft"][0]).then_inc(d_dft0, 16)
            sp.dma_start(S0[:], a["dft"][1]).then_inc(d_dft0, 16)
            with sp.Fori(1, ADA_T // RING) as i:
                for s in range(RING):
                    sp.wait_ge(ada_used, i * RING + (s - RING + 1))
                    if s == 0:
                        sp.wait_ge(c_prod, i)
                    sp.dma_start(raw[s][:], a["w"][bass.ds(i * RING + s, 1)].rearrange("o p k n -> p (o k) n")).then_inc(w_landed[s], 16)
            for s in range(RING):
                sp.wait_ge(ada_used, ADA_T - RING + s + 1)
                if s == 0:
                    sp.wait_ge(c_prod, CTX_POOL)
                sp.dma_start(raw[s][:], a["w"][ADA_T + s:ADA_T + s + 1].rearrange("o p k n -> p (o k) n")).then_inc(w_landed[s], 16)
            with sp.Fori(1, TILES // RING) as i:
                for s in range(RING):
                    sp.wait_ge(w_lo, i * RING + (s - RING + 1))
                    sp.dma_start(raw[s][:], a["w"][bass.ds(i * RING + (s + ADA_T), 1)].rearrange("o p k n -> p (o k) n")).then_inc(w_landed[s], 16)

        @block.gpsimd
        def _(g):
            g.memset(ones[:], 1.0)
            g.memset(ones_d[:], 1.0 / D)
            g.memset(ones_hd[:], 1.0 / P)
            g.memset(zcol[:], 0.0)
            g.memset(epsc[:, 0:1], EPS)
            g.memset(epsc[:, 1:2], LN_EPS)
            g.memset(blk64[:], 0.0).then_inc(consts, 1)
            g.wait_ge(consts, 1)
            g.memset(blk64[0:64, 0:64], 1.0 / 64)
            g.memset(blk64[64:128, 64:128], 1.0 / 64).then_inc(consts, 1)
            def ctx_product(j):
                g.wait_ge(w_landed[0], 16 * j + 16)
                if j >= 2:
                    g.wait_ge(c_sum, j - 1)
                g.tensor_tensor(cprod[j % 2][:], raw[0][:].rearrange("p k n -> p (k n)"), cvec[:, 1, :], ALU.mult).then_inc(c_prod, 1)

            g.wait_ge(consts, 2)
            for p in range(8):
                if p == 0:
                    g.wait_ge(c_silu, 1)
                o, t = p // 4, p % 4
                g.wait_ge(f_dec, p + 1)
                m1 = g.tensor_tensor(fE[:, t, o * HY:(o + 1) * HY], fab[:, p % 2, 0, :], fab[:, p % 2, 1, :], ALU.add)
                if t == 0:
                    m1.then_inc(f_e0, 1)
                    g.wait_ge(f_e0, o + 1)
                    m1 = g.tensor_tensor(fE[0:1, 0, o * HY:(o + 1) * HY], fE[0:1, 0, o * HY:(o + 1) * HY], hb[:, o, :], ALU.add)
                m1.then_inc(f_eo, 1)
                if p % 2 == 0:
                    ctx_product(p // 2)
            for j in range(4, CTX_POOL):
                ctx_product(j)
            with g.Fori(0, TB["g_in"] // RING) as i:
                for s in range(RING):
                    g.wait_ge(w_hi, i * RING + (s + 1))
                    g.tensor_tensor(wlo[s][:], raw[s][:], whi[s][:].bitcast(F32), ALU.subtract).then_inc(w_lo, 1)
            g.wait_ge(d_ws, 32)
            g.affine_select(out=wsT[:], in_=wsT[:], compare_op=ALU.is_ge, fill=0.0, base=0,
                            pattern=[[0, 8], [1, P]], channel_multiplier=-1).then_inc(gws, 1)
            with g.Fori(TB["g_in"] // RING, TILES // RING) as i:
                for s in range(RING):
                    g.wait_ge(w_hi, i * RING + (s + 1))
                    g.tensor_tensor(wlo[s][:], raw[s][:], whi[s][:].bitcast(F32), ALU.subtract).then_inc(w_lo, 1)

        @block.scalar
        def _(act):
            A = nc.scalar.activation
            act.wait_ge(d_filt, 48)
            act.dma_start(ident[:], a["ident"]).then_inc(d_x, 16)
            act.dma_start(rot[:], a["rot"]).then_inc(d_x, 16)
            act.dma_start(cmask[:], a["cmask"]).then_inc(d_x, 16)

            def one(ap):
                return ap.rearrange("p (o n) -> p o n", o=1)

            def hi_split(v, s, first=False):
                act.wait_ge(w_landed[s], v * 4 + (16 * (ADA_T // RING) + 16 - 4 * s))
                if not first:
                    act.wait_ge(w_used, v - (RING - 1))
                A(whi[s][:], raw[s][:], ACT.Copy).then_inc(w_hi, 1)

            roots = [0]

            def inverse_root(out, mean_square, done, eps=0, scale=1.0, W=L):
                A(std[:, 0:W], mean_square, ACT.Ln, bias=epsc[:, eps:eps + 1], scale=scale).then_inc(log_done, 1)
                roots[0] += 1
                act.wait_ge(log_done, roots[0])
                A(out, std[:, 0:W], ACT.Exp, scale=-0.5).then_inc(done, 1)

            def roots_table():
                act.preload_act_table_set("natural_log_exp_and_others")

            def norm_act(name):
                W = norm_of(name)[5]
                if name in AFTER_POST:
                    m = AFTER_POST.index(name)
                    for k in range(KD):
                        act.wait_ge(x_new, m * KD + k + 1)
                        if k >= 2:
                            act.wait_ge(nm_used, m * KD + k - 1)
                        A(sq[k % 2][:], xT[:, k, :], ACT.Square).then_inc(nm_sq, 1)
                    act.wait_ge(nm_used, m * KD + KD)
                elif name == "mix_pre":
                    act.wait_ge(x_summed, KD)
                else:
                    act.wait_ge(nm_sum, SUMMED.index(name) + 1)
                bank_ = acc[3] if name == "mix_pre" else aux[3]
                inverse_root(rstd[:, 0:W], bank_[:, 0:W], nm_std, W=W)

            def norm_apply_act(name):
                n = PRE.index(name)
                _, _, sh, hi_, _, W = norm_of(name)
                for k in range(KD):
                    act.wait_ge(nm_tmp, n * KD + k + 1)
                    A(hi_[:, k, :], tmp[k % 2][:, 0:W], ACT.Identity, bias=sh(k)).then_inc(h_hi, 1)

            act.wait_ge(d_cols, 16)
            for j in range(2):
                act.wait_ge(f_arg, j + 1)
                A(hd[0:64, :], tn[:], ACT.Sin).then_inc(f_sin, 1)
                if j == 0:
                    act.wait_ge(d_x, 64)
                    for k in range(KD):
                        if k >= 2:
                            act.wait_ge(x_summed, k - 1)
                        A(xsq[:, k % 2, :], xT[:, k, :], ACT.Square).then_inc(x_squared, 1)
            act.wait_ge(d_cvec, 16)
            A(cvec, cvec, ACT.Silu).then_inc(c_silu, 1)
            roots_table()
            act.wait_ge(lam_mm, 1)
            A(small[:, 0:2], acc[1][:, 0:2], ACT.Exp).then_inc(lam_exp, 1)
            norm_act("mix_pre")
            def ctx_sum(j):
                act.wait_ge(c_prod, j + 1)
                A(cprod[j % 2][:], cprod[j % 2][:], ACT.Copy, accum_out=ada[:, 2 * j + 1:2 * j + 2]).then_inc(c_sum, 1)

            for q in range(8):
                o, f = q // 4, q % 4
                for j in (range(0, 4), [4], [5], [6], [7], [8, 9], [10], [11])[q]:
                    ctx_sum(j)
                if q == 7:
                    hi_split(0, 0, True)
                    hi_split(1, 1, True)
                act.wait_ge(g_mm, q + 1)
                A(Gr[o][:, f, :], aux[2 * (q % 2)][:], ACT.Copy, scale=1.0 / HY)
                A(Gs[o][:, f, :], aux[2 * (q % 2) + 1][:], ACT.Copy, scale=1.0 / HY).then_inc(g_used, 1)
            act.dma_start(Cm[:], a["dft"][2]).then_inc(d_dft, 16)
            act.dma_start(Sm[:], a["dft"][3]).then_inc(d_dft, 16)

            norm_apply_act("mix_pre")

            for u in range(12):
                if u + 2 < RING:
                    hi_split(u + 2, u + 2, True)
                else:
                    hi_split(u + 2, (u + 2) % RING)
                act.wait_ge(w_used, u + 1)
                if u == 0:
                    act.wait_ge(hy_pad, 1)
                if u >= 2:
                    act.wait_ge(hy_conv, u - 1)
                A(pads[u % 2][:, 1:L + 1], acc[u % 4][:], ACT.Copy).then_inc(c_free, 1)
            for c in range(8):
                act.wait_ge(hy_tr, c + 1)
                dst = n0 if c < 4 else n1
                A(dst[:, :, (c % 4) * P:(c % 4 + 1) * P], aux[c % 2][:].rearrange("p (t n) -> p t n", t=NT), ACT.Copy).then_inc(hy_nat, 1)
            for c in range(HC):
                act.wait_ge(hy_z, c + 1)
                A(zhi[:, c, :], tmp[c % 2][:], ACT.Copy).then_inc(hy_zhi, 1)
            act.wait_ge(hy_zlo, HC)
            act.dma_start(cxT[:], a["ctxT"]).then_inc(d_att, 16)
            act.dma_start(cosT[:], a["rope"][0]).then_inc(d_att, 16)
            act.dma_start(sinT[:], a["rope"][1]).then_inc(d_att, 16)
            def v_natural(h):
                act.wait_ge(v_tr, h + 1)
                A(vN[:, h, 0:4, :], aux[2][:].rearrange("p (t n) -> p t n", t=4), ACT.Copy)
                A(vN[:, h, 4:6, :], aux[3][:, 0:CTX].rearrange("p (t n) -> p t n", t=2), ACT.Copy).then_inc(v_nat, 1)

            for u in range(12):
                t = TB["qkv"] + u
                hi_split(t + 2, (t + 2) % RING)
                act.wait_ge(w_used, t + 1)
                if 2 <= u < 10:
                    act.wait_ge(q_done, u - 1)
                if u >= 10:
                    act.wait_ge(v_tr, u - 9)
                A(qe[:, u % 2, 0:L], acc[t % 4][:], ACT.Copy).then_inc(c_free, 1)
                if u == 2:
                    norm_act("ctx")
                if u == 3:
                    norm_apply_act("ctx")
                if u >= 4:
                    A(kT[:, u - 4, L:NKEY] if u < 8 else qe[:, u % 2, L:NKEY], aux[u % 2][:, 0:CTX], ACT.Copy).then_inc(kv_ev, 1)
                if u >= 9:
                    v_natural(u - 9)
            v_natural(3)

            for n in range(ATT_STEPS + 4):
                if n < ATT_STEPS:
                    if n > 1:
                        act.wait_ge(a_tr, n - 1)
                    for m in range(2):
                        b = att_col(n, m)
                        act.wait_ge(a_mx, 2 * n + m + 1)
                        A(pp[:, n % 2, m, :], scores[m][:, 0:NKEY], ACT.Exp, bias=small[:, b:b + 1], scale=0.125,
                          accum_out=small[:, b + 1:b + 2]).then_inc(a_p, 1)
                if 2 <= n < ATT_STEPS + 2:
                    qi, h = (n - 2) % NT, (n - 2) // NT
                    act.wait_ge(a_tr, n - 1)
                    if qi == 0 and h:
                        act.wait_ge(a_o, h)
                    A(aT[:, 0:4, qi * P:(qi + 1) * P], trT[:, 0:L].rearrange("p (t n) -> p t n", t=4), ACT.Copy)
                    A(aT[:, 4:6, qi * P:(qi + 1) * P], trT[:, L:NKEY].rearrange("p (t n) -> p t n", t=2), ACT.Copy).then_inc(a_ev, 1)
                if n > NT:
                    h = (n - 2) // NT - 1
                    if n % NT == 2:
                        act.wait_ge(a_o, h + 1)
                        A(sq[0][:], aux[2][:], ACT.Square).then_inc(a_sq, 1)
                    if n % NT == 3:
                        act.wait_ge(a_ss, h + 1)
                        inverse_root(rstd[:], aux[3][:], a_std)
                    if n % NT == 0 and h >= 0:
                        act.wait_ge(a_tmp, h + 1)
                        A(ohi[:, h, :], tmp[0][:], ACT.Copy).then_inc(a_hi, 1)
            act.wait_ge(a_tmp, HEADS)
            A(ohi[:, HEADS - 1, :], tmp[0][:], ACT.Copy).then_inc(a_hi, 1)

            act.preload_act_table(ACT.Sigmoid)
            with act.Fori(0, 2) as i:
                for jj in range(4):
                    t = i * 12 + (TB["mix"] + 3 * jj)
                    hi_split(t + 2, (3 * jj + 2) % RING)
                    act.wait_ge(w_used, t + 1)
                    A(sgm[:, jj % 2, 0, :], acc[0][:], ACT.Sigmoid)
                    hi_split(t + 3, (3 * jj + 3) % RING)
                    act.wait_ge(w_used, t + 2)
                    A(sgm[:, jj % 2, 1, :], acc[1][:], ACT.Sigmoid).then_inc(m_sg, 1)
                    hi_split(t + 4, (3 * jj + 4) % RING)
                    act.wait_ge(m_sum, i * 4 + (jj + 1))
                    A(mxh[:, bass.ds(i * 4 + jj, 1), :], one(mt[:, jj % 2, 0, :]), ACT.Copy).then_inc(m_hi, 1)
            roots_table()

            for u in range(8):
                t = TB["wout"] + u
                hi_split(t + 2, (t + 2) % RING)
            norm_act("mix_post")
            norm_act("ffn_pre")
            norm_apply_act("ffn_pre")

            act.preload_act_table(ACT.Silu)
            with act.Fori(0, FC // 2) as i:
                for s in range(RING):
                    v = i * RING + (TB["gateup"] + s)
                    p = s // 2
                    hi_split(v + 2, (s + 2) % RING)
                    if s % 2 == 0:
                        act.wait_ge(w_used, v + 1)
                        A(sil[:, p, :], acc[s][:], ACT.Silu).then_inc(s_silu, 1)
                    else:
                        act.wait_ge(c_free, i * RING + (CB["gateup"] + s + 1))
                        A(hidh[:, bass.ds(i * 2 + p, 1), :], one(tmp[p][:]), ACT.Copy).then_inc(s_hi, 1)
            roots_table()
            for v in range(TB["down"], TB["down"] + 24):
                hi_split(v + 2, (v + 2) % RING)
            norm_act("ffn_post")
            act.dma_start(wsT[:], a["ws"]).then_inc(d_ws, 16)
            act.dma_start(bsb[:], a["bs"]).then_inc(d_ws, 16)
            norm_act("g_mix")
            norm_apply_act("g_mix")

            act.preload_act_table(ACT.Gelu_apprx_tanh)
            with act.Fori(0, 4) as i:
                for s in range(RING):
                    v = i * RING + (TB["g_in"] + s)
                    hi_split(v + 2, (s + 2) % RING)
                    act.wait_ge(w_used, v + 1)
                    A(vT[:, bass.ds(i * 4 + s, 1), :], acc[s][:].rearrange("p (o n) -> p o n", o=1), ACT.Gelu_apprx_tanh).then_inc(c_free, 1)
            def g_u(i):
                for s in range(RING):
                    v = i * RING + (TB["g_in"] + 16 + s)
                    hi_split(v + 2, (s + 2) % RING)
                    act.wait_ge(w_used, v + 1)
                    A(guT[:, bass.ds(i * 4 + s, 1), :], acc[s][:].rearrange("p (o n) -> p o n", o=1), ACT.Gelu_apprx_tanh).then_inc(c_free, 1)
            g_u(0)
            act.wait_ge(gmean, 1)
            A(mean[:], aux[0][:], ACT.Copy, scale=0.5).then_inc(gmd, 1)
            with act.Fori(1, 3) as i:
                g_u(i)
            roots_table()
            act.wait_ge(gss, 1)
            inverse_root(lrs[:], aux[1][:], gstd, eps=1, scale=0.5)
            act.preload_act_table(ACT.Gelu_apprx_tanh)
            g_u(3)
            roots_table()
            for c in range(16):
                act.wait_ge(gtr, c + 1)
                if c >= 2:
                    act.wait_ge(gsp, c - 1)
                A(vn[:, c % 2, :], aux[c % 2][:], ACT.Copy).then_inc(gvn, 1)
                if c >= 1:
                    act.wait_ge(gtm, c)
                    A(ghi[:, c - 1, :], gt[:, (c - 1) % 2, 1, :], ACT.Copy).then_inc(ghis, 1)
            act.wait_ge(gtm, 16)
            A(ghi[:, 15, :], gt[:, 1, 1, :], ACT.Copy).then_inc(ghis, 1)
            for v in range(TB["g_out"], TB["g_out"] + 16):
                hi_split(v + 2, (v + 2) % RING)

            def mlp_up(i, base, nbase):
                for s in range(RING):
                    v = i * RING + (base + s)
                    hi_split(v + 2, (s + 2) % RING)
                    act.wait_ge(w_used, v + 1)
                    A(sq[s % 2][:], acc[s][:], ACT.Relu).then_inc(c_free, 1)
                    act.wait_ge(m_rsq, i * RING + (nbase + s + 1))
                    A(mh[:, bass.ds(i * 4 + s, 1), :], tmp[s % 2][:].rearrange("p (o n) -> p o n", o=1), ACT.Copy).then_inc(m_rhi, 1)

            def mlp(layer, last):
                for half in range(2):
                    n = layer * 2 + half
                    with act.Fori(0, 4) as i:
                        mlp_up(i, TB[f"up{layer}{'ab'[half]}"], n * 16)
                    b = TB[f"dn{layer}{'ab'[half]}"]
                    for v in range(b, b + 16):
                        if v + 2 < TILES:
                            hi_split(v + 2, (v + 2) % RING)

            act.dma_start(wf[:], a["wf"]).then_inc(d_wf, 16)
            act.wait_ge(d_wf, 16)
            A(wfh[:], wf[:], ACT.Copy).then_inc(x_wfh, 1)
            norm_act("mlp0")
            norm_apply_act("mlp0")
            mlp(0, False)

            norm_act("fox")
            norm_apply_act("fox")
            act.wait_ge(x_fl, 1)
            A(lf[:, 0, :], aux[0][0:16, :], ACT.Identity, bias=col("b_f", rows=16)).then_inc(x_lf, 1)
            act.wait_ge(x_lf, 1)
            A(lf[:, 1, :], lf[:, 0, :], ACT.Abs).then_inc(x_lf, 1)
            act.wait_ge(x_lf, 2)
            A(lf[:, 2, :], lf[:, 1, :], ACT.Exp, scale=-1.0).then_inc(x_lf, 1)
            act.wait_ge(x_lf, 3)
            A(lf[:, 1, :], lf[:, 2, :], ACT.Ln, bias=ones[0:16, 0:1]).then_inc(x_lf, 1)
            act.wait_ge(x_c, 2)
            act.dma_start(a["scratch"][0], cpos[:]).then_inc(d_c, 16)
            act.dma_start(a["scratch"][1], cneg[:]).then_inc(d_c, 16)
            act.wait_ge(d_c, 32)
            act.wait_ge(x_ini, 2)

            def fox_act(g, a_, b_, par):
                if g is not None:
                    v0 = g * RING + TB["fox"]
                    for e in range(2):
                        act.dma_start(qa[65:66, par, e, :], a["scratch"][0, one_of(g * 2 + e), :]).then_inc(d_crow[par], 16)
                        act.dma_start(ka[64:65, par, e, :], a["scratch"][1, one_of(g * 2 + e), :]).then_inc(d_crow[par], 16)

                def weights_out(pair, n):
                    e, qi = n // 4, n % 4
                    act.wait_ge(x_pt, pair * 8 + (n + 1))
                    A(fpT[:, e, 0:qi + 1, qi * P:(qi + 1) * P], aux[2][:, 0:(qi + 1) * P].rearrange("p (t n) -> p t n", n=P), ACT.Copy).then_inc(x_pe, 1)
                for n in range(8):
                    if g is not None:
                        if n in (2, 4):
                            s = n // 2 - 1
                            act.wait_ge(w_used, v0 + (s + 1))
                            A(fsq[:, s, :], acc[s][:], ACT.Square).then_inc(x_sq, 1)
                        if n == 6:
                            act.wait_ge(w_used, v0 + 3)
                            A(fvT[:], acc[2][:], ACT.Copy).then_inc(x_vt, 1)
                        if n == 7:
                            act.wait_ge(x_vtr, g + 1)
                            A(fvn[:, par, :, :], aux[3][:].rearrange("p (t n) -> p t n", t=NT), ACT.Copy).then_inc(x_vn, 1)
                        if n % 2 == 0:
                            hi_split(v0 + (n // 2 + 2), (n // 2 + 2) % RING)
                    if a_ is not None:
                        e, qi = n // 4, n % 4
                        W = (qi + 1) * P
                        act.wait_ge(x_mx, a_ * 8 + (n + 1))
                        A(fp[:, qi % 2, 0:W], aux[qi % 2][:, 0:W], ACT.Exp, bias=small[:, 40 + n:41 + n],
                          accum_out=small[:, 48 + n:49 + n]).then_inc(x_p, 1)
                        if n:
                            weights_out(a_, n - 1)
                        if n == 1:
                            act.wait_ge(x_g1, a_ + 1)
                            A(fsg[:, 1 - par, :], fsg[:, 1 - par, :], ACT.Ln).then_inc(x_gl, 1)
                        if n == 2:
                            act.wait_ge(x_gl, a_ + 1)
                            A(fsg[:, 1 - par, :], fsg[:, 1 - par, :], ACT.Exp, scale=-1.0).then_inc(x_sg, 1)
                    if b_ is not None:
                        if n == 0:
                            weights_out(b_, 7)
                        if n == 3:
                            act.wait_ge(x_og, b_ * 2 + 2)
                            A(foh[:, one_of(b_), :], one(fog[:]), ACT.Copy).then_inc(x_hi, 1)
                    if g is not None and n in (4, 5):
                        s = n - 4
                        r = (std, rstd)[s][:]
                        act.wait_ge(x_ss, g * 2 + (s + 1))
                        A(r, (aux[3], acc[3])[s][:], ACT.Ln, bias=epsc[:, 0:1]).then_inc(x_ln, 1)
                        act.wait_ge(x_ln, g * 2 + (s + 1))
                        A(r, r, ACT.Exp, scale=-0.5).then_inc(x_std, 1)
                if g is not None:
                    act.wait_ge(w_used, v0 + 4)
                    A(fsg[:, par, :], acc[3][:], ACT.Exp, scale=-1.0).then_inc(x_gt, 1)

            def one_of(index):
                return bass.ds(index, 1)
            fox_steps(act, fox_act)
            for v in range(TB["fox_out"], TB["fox_out"] + 8):
                hi_split(v + 2, (v + 2) % RING)
            norm_act("mlp1")
            norm_apply_act("mlp1")
            mlp(1, True)
            for k in range(KD):
                act.wait_ge(c_free, CB["dn1b"] + k + 1)
                act.dma_start(a["out"][:, k, :], xT[:, k, :]).then_inc(d_out, 16)
            act.wait_ge(d_out, 16 * KD)

        @block.tensor
        def _(pe):
            mm = nc.tensor.matmul

            def tile(v, s, bank_, xh, xl, blocks=8, start=True, stop=True, last=True, first_block=0, free=None, last_in=None):
                pe.wait_ge(w_lo, v + 1)
                if free is not None:
                    pe.wait_ge(c_free, free)
                for k in range(blocks):
                    b = first_block + k
                    if last_in is not None and k == blocks - 1:
                        pe.wait_ge(*last_in)
                    m1 = mm(bank_, whi[s][:, b, :], xh[k], start=start and k == 0, stop=False)
                    mm(bank_, whi[s][:, b, :], xl[k], start=False, stop=False)
                    m1 = mm(bank_, wlo[s][:, b, :], xh[k], start=False, stop=stop and k == blocks - 1)
                if last:
                    m1.then_inc(w_used, 1)

            def chunks(t, n0, n1):
                return [t[:, k, :] for k in range(n0, n1)]

            def norm_pe(name):
                W = norm_of(name)[5]
                if name in AFTER_POST:
                    m = AFTER_POST.index(name)
                    for k in range(KD):
                        pe.wait_ge(nm_sq, m * KD + k + 1)
                        mm(aux[3][:], ones_d[:], sq[k % 2][:], start=k == 0, stop=k == KD - 1).then_inc(nm_used, 1)
                elif name == "mix_pre":
                    for k in range(KD):
                        pe.wait_ge(x_squared, k + 1)
                        mm(acc[3][:], ones_d[:], xsq[:, k % 2, :], start=k == 0, stop=k == KD - 1).then_inc(x_summed, 1)
                else:
                    pe.wait_ge(nm_ssq, (SUMMED.index(name) + 1) * KD)
                    mm(aux[3][:, 0:W], ones_d[:], ssq[:, 0:W], start=True, stop=True).then_inc(nm_sum, 1)

            def first_tiles(v, norm):
                n = PRE.index(norm)
                pe.wait_ge(w_lo, v + 2)
                for k in range(KD):
                    pe.wait_ge(h_lo, n * KD + k + 1)
                    for s in range(2):
                        mm(acc[s][:], whi[s][:, k, :], hh[:, k, :], start=k == 0, stop=False)
                        mm(acc[s][:], whi[s][:, k, :], hl[:, k, :], start=False, stop=False)
                        m1 = mm(acc[s][:], wlo[s][:, k, :], hh[:, k, :], start=False, stop=k == KD - 1)
                        if k == KD - 1:
                            m1.then_inc(w_used, 1)

            def first_group(name, norm):
                pe.wait_ge(c_free, CB[name])
                first_tiles(TB[name], norm)
                for s in range(2, 4):
                    tile(TB[name] + s, s, acc[s][:], *H)

            H = (chunks(hh, 0, KD), chunks(hl, 0, KD))

            pe.wait_ge(d_filt, 48)
            mm(aux[0][0:64, :], fw1[:], zT[:], start=True, stop=True).then_inc(f_mm, 1)
            pe.wait_ge(consts, 2)
            pe.wait_ge(lam_prod, 1)
            mm(acc[1][:, 0:2], ones[0:64, :], small[0:64, 4:6], start=True, stop=True).then_inc(lam_mm, 1)
            pe.wait_ge(f_sin, 1)
            mm(aux[1][0:64, :], fw2[:], hd[0:64, :], start=True, stop=True).then_inc(f_mm, 1)
            norm_pe("mix_pre")
            pe.wait_ge(f_sin, 2)
            pe.wait_ge(d_filt2, 48)
            for p in range(8):
                o, t = p // 4, p % 4
                if p >= 2:
                    pe.wait_ge(f_dec, p - 1)
                for d in range(2):
                    m1 = mm(aux[2 * (p % 2) + d][:], hd[0:65, t * P:(t + 1) * P], fw3[:, (2 * o + d) * HY:(2 * o + d + 1) * HY],
                            start=True, stop=True)
                m1.then_inc(f_ab, 1)
            pe.wait_ge(d_dft0, 32)
            pe.wait_ge(f_eo, 8)
            pe.wait_ge(f_odd, 8)
            for q in range(8):
                o, f = q // 4, q % 4
                if q >= 2:
                    pe.wait_ge(g_used, q - 1)
                for r, (mat, src) in enumerate(((C0, fE), (S0, fO))):
                    for t in range(NT):
                        m1 = mm(aux[2 * (q % 2) + r][:], mat[:, t, f * P:(f + 1) * P], src[:, t, o * HY:(o + 1) * HY],
                                start=t == 0, stop=t == NT - 1)
                m1.then_inc(g_mm, 1)

            pe.wait_ge(g_used, 8)
            first_group("hyena", "mix_pre")
            for u in range(4, 12):
                tile(u, u % 4, acc[u % 4][:], *H, free=CB["hyena"] + u - 3)
            pe.wait_ge(d_x, 64)
            for c in range(8):
                pe.wait_ge(hy_conv, c + 1)
                if c >= 2:
                    pe.wait_ge(hy_nat, c - 1)
                for t in range(NT):
                    m1 = nc.tensor.transpose(aux[c % 2][:, t * P:(t + 1) * P], uT[:, c, t * P:(t + 1) * P], ident[:])
                m1.then_inc(hy_tr, 1)
            pe.wait_ge(hy_nat, 8)
            pe.wait_ge(d_dft, 32)
            pe.wait_ge(c_free, CB["qkv"])
            for o in range(2):
                if o:
                    pe.wait_ge(hy_yd, NT)
                for f in range(4):
                    if o * 4 + f >= 2:
                        pe.wait_ge(hy_pw, o * 4 + f - 1)
                    for r, mat in enumerate((Cm, Sm)):
                        for t in range(NT):
                            m1 = mm(aux[2 * (f % 2) + r][:], mat[:, t, f * P:(f + 1) * P], n0[:, t, :],
                                    start=t == 0, stop=t == NT - 1)
                    m1.then_inc(hy_u, 1)
                pe.wait_ge(hy_y, o * 4 + 4)
                for t in range(NT):
                    for r, (mat, y) in enumerate(((Cm, Gr[o]), (Sm, Gs[o]))):
                        for f in range(4):
                            lhs, rhs = (mat, y) if o == 0 else (y, mat)
                            m1 = mm(acc[t][:], lhs[:, f, t * P:(t + 1) * P], rhs[:, f, :],
                                    start=(r == 0 and f == 0), stop=(r == 1 and f == 3))
                    m1.then_inc(hy_inv, 1)

            def rotate(u):
                pe.wait_ge(c_free, CB["qkv"] + u + 1)
                if u:
                    pe.wait_ge(q_done, u)
                mm(aux[2][:], rot[:], qe[:, u % 2, 0:L], start=True, stop=True).then_inc(q_rot, 1)

            def v_transposes(h):
                pe.wait_ge(c_free, CB["qkv"] + h + 9)
                pe.wait_ge(kv_ev, h + 5)
                if h == 0:
                    pe.wait_ge(q_done, 8)
                else:
                    pe.wait_ge(v_nat, h)
                for t in range(KT):
                    b = aux[2] if t < 4 else aux[3]
                    m1 = nc.tensor.transpose(b[:, (t % 4) * P:(t % 4 + 1) * P], qe[:, h % 2, t * P:(t + 1) * P], ident[:])
                m1.then_inc(v_tr, 1)

            for u in range(12):
                v = TB["qkv"] + u
                if u < 4:
                    pe.wait_ge(hy_z, u + 1)
                tile(v, v % 4, acc[v % 4][:], *H, free=CB["qkv"] + u - 3, last=u < 4)
                if u >= 4:
                    if u == 4:
                        pe.wait_ge(h_lo, 2 * KD)
                    if u >= 6:
                        pe.wait_ge(kv_ev, u - 5)
                    for k in range(KD):
                        b = aux[u % 2][:, 0:CTX]
                        mm(b, whi[v % 4][:, k, :], hch[:, k, :], start=k == 0, stop=False)
                        mm(b, whi[v % 4][:, k, :], hcl[:, k, :], start=False, stop=False)
                        m1 = mm(b, wlo[v % 4][:, k, :], hch[:, k, :], start=False, stop=k == KD - 1)
                    m1.then_inc(w_used, 1)
                if u == 2:
                    norm_pe("ctx")
                if 1 <= u < 9:
                    rotate(u - 1)
                if u >= 9:
                    v_transposes(u - 9)
            v_transposes(3)

            pe.wait_ge(c_free, CB["mix"])
            pe.wait_ge(kv_ev, 8)
            pe.wait_ge(q_done, 8)
            pe.wait_ge(v_nat, 4)
            for n in range(ATT_STEPS + 4):
                if n < ATT_STEPS:
                    h, qi = n // NT, n % NT
                    for m in range(2):
                        if n:
                            pe.wait_ge(a_p, 2 * n + m - 1)
                        r = slice(64 * m, 64 * m + 64)
                        mm(scores[m][:, 0:L], qT[r, h, qi * P:(qi + 1) * P], kT[r, h, 0:L], start=True, stop=True)
                        mm(scores[m][:, L:NKEY], qT[r, h, qi * P:(qi + 1) * P], kT[r, h, L:NKEY], start=True, stop=True).then_inc(a_s, 1)
                if 2 <= n < ATT_STEPS + 2:
                    pe.wait_ge(a_cm, n - 1)
                    if n > 2:
                        pe.wait_ge(a_ev, n - 2)
                    for t in range(KT):
                        m1 = nc.tensor.transpose(trT[:, t * P:(t + 1) * P], pp[:, n % 2, 0, t * P:(t + 1) * P], ident[:])
                    m1.then_inc(a_tr, 1)
                h = (n - 1) // NT - 1
                if n > NT and n % NT in (1, 2):
                    pe.wait_ge(a_ev, NT * h + NT)
                    if h:
                        pe.wait_ge(a_tmp, h)
                    half = n % NT - 1
                    for t in range(3 * half, 3 * half + 3):
                        m1 = mm(aux[2][:], vN[:, h, t, :], aT[:, t, :], start=t == 0, stop=t == KT - 1)
                    if half:
                        m1.then_inc(a_o, 1)
                if n > NT and n % NT == 3:
                    pe.wait_ge(a_sq, h + 1)
                    mm(aux[3][:], ones_hd[:], sq[0][:], start=True, stop=True).then_inc(a_ss, 1)

            pe.wait_ge(a_p, 2 * ATT_STEPS)
            with pe.Fori(0, 2) as i:
                for jj in range(4):
                    v = i * 12 + (TB["mix"] + 3 * jj)
                    c = i * 16 + (CB["mix"] + 4 * jj)
                    tile(v, (3 * jj) % 4, acc[0][:], *H)
                    tile(v + 1, (3 * jj + 1) % 4, acc[1][:], *H)
                    s = (3 * jj + 2) % 4
                    if jj == 0:
                        pe.wait_ge(a_lo, HEADS)
                    tile(v + 2, s, acc[2][:], chunks(zhi, 0, 4), chunks(zlo, 0, 4), blocks=4, last=False, free=c)
                    tile(v + 2, s, acc[3][:], chunks(ohi, 0, 4), chunks(olo, 0, 4), blocks=4, first_block=4)
                    pe.wait_ge(m_sg, i * 4 + (jj + 1))

            pe.wait_ge(m_lo, KD - 1)
            with pe.Fori(0, 2) as i:
                for s in range(4):
                    tile(i * 4 + (TB["wout"] + s), s, acc[s][:], chunks(mxh, 0, KD), chunks(mxl, 0, KD),
                         free=i * 4 + (CB["wout"] + s - 3), last_in=(m_lo, KD) if s == 0 else None)
            norm_pe("mix_post")
            norm_pe("ffn_pre")
            first_group("gateup", "ffn_pre")
            with pe.Fori(1, FC // 2) as i:
                for s in range(4):
                    tile(i * 4 + (TB["gateup"] + s), s, acc[s][:], *H, free=i * 4 + (CB["gateup"] + s - 3))
            pe.wait_ge(s_lo, FC - 1)
            with pe.Fori(0, 2) as i:
                for cc in range(4):
                    for part in range(3):
                        n0_, n1_ = 8 * part, min(8 * part + 8, FC)
                        s = (3 * cc + part) % 4
                        tile(i * 12 + (TB["down"] + 3 * cc + part), s, acc[cc][:], chunks(hidh, n0_, n1_), chunks(hidl, n0_, n1_),
                             blocks=n1_ - n0_, start=part == 0, stop=part == 2, last_in=(s_lo, FC) if cc == 0 and part == 2 else None,
                             free=i * 4 + (CB["down"] + cc - 3) if part == 0 else None)
            norm_pe("ffn_post")
            norm_pe("g_mix")

            def g_in(i):
                for s in range(4):
                    tile(i * 4 + (TB["g_in"] + s), s, acc[s][:], *H, free=i * 4 + (CB["g_in"] + s - 3))
            first_group("g_in", "g_mix")
            with pe.Fori(1, 4) as i:
                g_in(i)
            g_in(4)
            pe.wait_ge(gsm, 16)
            mm(aux[0][:], ones_d[:], ssq[:], start=True, stop=True).then_inc(gmean, 1)
            with pe.Fori(5, 7) as i:
                g_in(i)
            pe.wait_ge(gsq, 1)
            mm(aux[1][:], ones_d[:], ssq[:], start=True, stop=True).then_inc(gss, 1)
            g_in(7)
            pe.wait_ge(c_free, CB["g_out"])
            pe.wait_ge(gws, 1)
            pe.wait_ge(gstd, 1)

            def spatial(c):
                pe.wait_ge(gvn, c + 1)
                if c >= 4:
                    pe.wait_ge(gta, c - 3)
                for t in range(NT):
                    m1 = mm(acc[c % 4][:, t * P:(t + 1) * P], vn[:, c % 2, t * P:(t + 1) * P], wsT[:, c // 2, :], start=True, stop=True)
                m1.then_inc(gsp, 1)
            for c in range(16):
                pe.wait_ge(gv, c + 1)
                if c >= 2:
                    pe.wait_ge(gvn, c - 1)
                for t in range(NT):
                    m1 = nc.tensor.transpose(aux[c % 2][:, t * P:(t + 1) * P], vT[:, c, t * P:(t + 1) * P], ident[:])
                m1.then_inc(gtr, 1)
                if c:
                    spatial(c - 1)
            spatial(15)
            pe.wait_ge(gta, 16)
            pe.wait_ge(glos, 15)

            def wide(name, xh, xl, lo_done, count):
                with pe.Fori(0, 2) as i:
                    for cc in range(4):
                        for part in range(2):
                            tile(i * 8 + (TB[name] + 2 * cc + part), (2 * cc + part) % 4, acc[cc][:], chunks(xh, 8 * part, 8 * part + 8),
                                 chunks(xl, 8 * part, 8 * part + 8), start=part == 0, stop=part == 1,
                                 free=i * 4 + (CB[name] + cc - 3) if part == 0 else None,
                                 last_in=(lo_done, count) if cc == 0 and part == 1 else None)
            wide("g_out", ghi, glo, glos, 16)

            def mlp(layer):
                for half in range(2):
                    up, dn = f"up{layer}{'ab'[half]}", f"dn{layer}{'ab'[half]}"
                    if half == 0:
                        first_group(up, f"mlp{layer}")
                    with pe.Fori(1 if half == 0 else 0, 4) as i:
                        for s in range(4):
                            tile(i * 4 + (TB[up] + s), s, acc[s][:], *H, free=i * 4 + (CB[up] + s - 3),
                                 last_in=(c_free, CB[up]) if s == 0 else None)
                    n = 16 * (layer * 2 + half + 1)
                    pe.wait_ge(m_rlo, n - 1)
                    wide(dn, mh, ml, m_rlo, n)
            norm_pe("mlp0")
            mlp(0)

            norm_pe("fox")
            pe.wait_ge(x_wfl, 1)
            for k in range(KD):
                pe.wait_ge(h_lo, PRE.index("fox") * KD + k + 1)
                mm(aux[0][0:16, :], wfh[:, k, :], hh[:, k, :], start=k == 0, stop=False)
                mm(aux[0][0:16, :], wfh[:, k, :], hl[:, k, :], start=False, stop=False)
                m1 = mm(aux[0][0:16, :], wfl[:, k, :], hh[:, k, :], start=False, stop=k == KD - 1)
            m1.then_inc(x_fl, 1)
            pe.wait_ge(c_free, CB["fox"])
            pe.wait_ge(x_lf, 1)
            def fox_pe(g, a_, b_, par):
                ap_ = 1 - par

                def half(n):
                    s, part = n // 2, n % 2
                    if part == 0 and a_ is not None:
                        freed, count = ((x_qk, g * 2 - 1), (x_qk, g * 2), (x_vt, g), (x_gt, g))[s]
                        pe.wait_ge(freed, count)
                    if n == 6:
                        pe.wait_ge(x_std, g * 2 + 2)
                    tile(g * RING + (TB["fox"] + s), s, acc[s][:], chunks(hh, 4 * part, 4 * part + 4), chunks(hl, 4 * part, 4 * part + 4),
                         blocks=4, first_block=4 * part, start=part == 0, stop=part == 1, last=part == 1)

                def score(n):
                    e, qi = n // 4, n % 4
                    if n == 0:
                        pe.wait_ge(x_qk, a_ * 2 + 2)
                        pe.wait_ge(d_crow[ap_], a_ * 32 + (64 if ap_ == 0 else 32))
                    if n >= 2 or b_ is not None:
                        pe.wait_ge(x_p, a_ * 8 + (n - 1))
                    mm(aux[qi % 2][:, 0:(qi + 1) * P], qa[:, ap_, e, qi * P:(qi + 1) * P], ka[:, ap_, e, 0:(qi + 1) * P],
                       start=True, stop=True).then_inc(x_s, 1)

                def weights_t(pair, n):
                    e, qi = n // 4, n % 4
                    pe.wait_ge(x_pn, pair * 8 + (n + 1))
                    if n or b_ is not None:
                        pe.wait_ge(x_pe, pair * 8 + n)
                    for t in range(qi + 1):
                        m1 = nc.tensor.transpose(aux[2][:, t * P:(t + 1) * P], fp[:, qi % 2, t * P:(t + 1) * P], ident[:])
                    m1.then_inc(x_pt, 1)

                def out(pair, buf, e):
                    pe.wait_ge(x_pe, pair * 8 + (4 * e + 4))
                    r = slice(64 * e, 64 * e + 64)
                    for t in range(NT):
                        m1 = mm(aux[3][r, t * P:L], fvn[:, buf, t, r], fpT[:, e, t, t * P:L], start=t == 0, stop=t == NT - 1)
                    m1.then_inc(x_o, 1)

                for n in range(8):
                    if a_ is not None:
                        score(n)
                    if g is not None:
                        half(n)
                    if b_ is not None and n == 0:
                        weights_t(b_, 7)
                    if b_ is not None and n == 1:
                        if a_ is not None:
                            pe.wait_ge(x_vn, a_ + 1)
                        out(b_, par, 1)
                    if a_ is not None and n:
                        weights_t(a_, n - 1)
                    if g is not None and n == 3:
                        if b_ is not None:
                            pe.wait_ge(x_og, b_ * 2 + 2)
                        if a_ is not None:
                            pe.wait_ge(x_vn, a_ + 1)
                        pe.wait_ge(x_sq, g * 2 + 1)
                        mm(aux[3][:], blk64[:], fsq[:, 0, :], start=True, stop=True).then_inc(x_ss, 1)
                    if g is not None and n == 4:
                        if a_ is not None:
                            pe.wait_ge(x_gt, g)
                        pe.wait_ge(x_sq, g * 2 + 2)
                        mm(acc[3][:], blk64[:], fsq[:, 1, :], start=True, stop=True).then_inc(x_ss, 1)
                    if n == 5 and a_ is not None:
                        if g is not None:
                            pe.wait_ge(x_std, g * 2 + 1)
                        if g is None:
                            pe.wait_ge(x_og, b_ * 2 + 2)
                        out(a_, ap_, 0)
                    if n == 6 and g is not None:
                        pe.wait_ge(x_vt, g + 1)
                        if a_ is not None:
                            pe.wait_ge(x_og, a_ * 2 + 1)
                        for t in range(NT):
                            m1 = nc.tensor.transpose(aux[3][:, t * P:(t + 1) * P], fvT[:, t * P:(t + 1) * P], ident[:])
                        m1.then_inc(x_vtr, 1)
            fox_steps(pe, fox_pe)
            pe.wait_ge(c_free, CB["fox_out"])
            pe.wait_ge(x_lo, KD)
            with pe.Fori(0, 2) as i:
                for s in range(4):
                    tile(i * 4 + (TB["fox_out"] + s), s, acc[s][:], chunks(foh, 0, KD), chunks(fol, 0, KD), free=i * 4 + (CB["fox_out"] + s - 3))
            norm_pe("mlp1")
            mlp(1)

        @block.vector
        def _(v):
            V = nc.vector
            TT = V.tensor_tensor
            STT = V.scalar_tensor_tensor
            step = [0]

            def then(ins):
                step[0] += 1
                ins.then_inc(v_step, 1)
                v.wait_ge(v_step, step[0])

            def one(ap):
                return ap.rearrange("p (o n) -> p o n", o=1)

            def sum_squares(name):
                src, W = norm_of(name)[0], norm_of(name)[5]
                for k in range(KD):
                    if k == 0:
                        then(TT(ssq[:, 0:W], src[:, 0, 0:W], src[:, 0, 0:W], ALU.mult))
                        continue
                    then(TT(sq[0][:, 0:W], src[:, k, 0:W], src[:, k, 0:W], ALU.mult))
                    m1 = TT(ssq[:, 0:W], ssq[:, 0:W], sq[0][:, 0:W], ALU.add)
                    if k < KD - 1:
                        then(m1)
                m1.then_inc(nm_ssq, KD)

            def norm_dve(name):
                v.wait_ge(nm_std, NORMS.index(name) + 1)

            def norm_apply(name):
                n = PRE.index(name)
                src, g, sh, hi_, lo_, W = norm_of(name)

                def lo_of(k):
                    v.wait_ge(h_hi, n * KD + k + 1)
                    STT(out=lo_[:, k, :], in0=tmp[k % 2][:, 0:W], scalar=sh(k), in1=hi_[:, k, :].bitcast(F32), op0=ALU.add,
                        op1=ALU.subtract).then_inc(h_lo, 1)
                for k in range(KD):
                    if k >= 2:
                        lo_of(k - 2)
                        v.wait_ge(h_lo, n * KD + k - 1)
                    STT(out=tmp[k % 2][:, 0:W], in0=src[:, k, :], scalar=g(k), in1=rstd[:, 0:W], op0=ALU.mult, op1=ALU.mult).then_inc(nm_tmp, 1)
                lo_of(KD - 2)
                lo_of(KD - 1)
                v.wait_ge(h_lo, n * KD + KD)

            def residual(name):
                src, g = norm_of(name)[0:2]
                n = POST.index(name)
                for k in range(KD):
                    then(STT(out=tmp[k % 2][:], in0=src[:, k, :], scalar=g(k), in1=rstd[:], op0=ALU.mult, op1=ALU.mult))
                    TT(xT[:, k, :], xT[:, k, :], tmp[k % 2][:], ALU.add).then_inc(x_new, 1)
                v.wait_ge(x_new, (n + 1) * KD)

            V.memset(hd[64:65, :], 1.0)
            v.wait_ge(d_cols, 16)
            TT(small[0:64, 4:6], col("lam_q", 0, 2, 64), col("lam_k", 0, 2, 64), ALU.mult).then_inc(lam_prod, 1)
            V.tensor_scalar(small[:, 6:7], col("subln"), 1.0 - LAM_INIT, None, ALU.mult)
            V.tensor_scalar(small[:, 7:8], col("q_g"), 0.125, None, ALU.mult)
            for j in range(2):
                v.wait_ge(f_mm, j + 1)
                then(V.tensor_scalar(targ[:], aux[j][0:64, :], col(("fb1", "fb2")[j], rows=64), col("freq", rows=64), ALU.add, ALU.mult))
                then(V.tensor_scalar(tn[:], targ[:], 1.0 / (2 * math.pi), MAGIC, ALU.mult, ALU.add))
                then(V.tensor_scalar(tn[:], tn[:], -MAGIC, None, ALU.add))
                then(STT(out=targ[:], in0=tn[:], scalar=-6.28125, in1=targ[:], op0=ALU.mult, op1=ALU.add))
                then(STT(out=targ[:], in0=tn[:], scalar=-(2 * math.pi - 6.28125), in1=targ[:], op0=ALU.mult, op1=ALU.add))
                V.tensor_scalar(tn[:], targ[:], 3.1415925, -3.1415925, ALU.min, ALU.max).then_inc(f_arg, 1)
            v.wait_ge(lam_exp, 1)
            then(TT(small[:, 2:3], small[:, 1:2], small[:, 0:1], ALU.subtract))
            then(V.tensor_scalar(small[:, 3:4], small[:, 2:3], -LAM_INIT, None, ALU.add))
            am = ada[:].rearrange("p (m w) -> p m w", w=2)

            def modulation(t0, t1):
                for u in range(t0, t1):
                    v.wait_ge(w_landed[u % RING], 16 * (u // RING) + 16)
                    t = ada_chunk(u)
                    row = raw[u % RING][:].rearrange("p k n -> p (k n)")
                    if CTX_POOL <= t < CTX_T:
                        if u >= 2:
                            v.wait_ge(ada_used, u)
                        then(STT(out=prod[:, u % 2, :], in0=row, scalar=1.0, in1=cvec[:, 1, :], op0=ALU.mult, op1=ALU.mult,
                                 accum_out=am[:, t, 1:2]))
                    elif u >= 2:
                        v.wait_ge(ada_used, u - 1)
                    STT(out=prod[:, u % 2, :], in0=row, scalar=1.0, in1=cvec[:, 0, :], op0=ALU.mult, op1=ALU.mult,
                        accum_out=am[:, t, 0:1]).then_inc(ada_used, 1)

            v.wait_ge(d_filt2, 48)
            for p in range(8):
                o, t = p // 4, p % 4
                v.wait_ge(f_ab, p + 1)
                if p >= 2:
                    v.wait_ge(f_eo, p - 1)
                    v.wait_ge(f_odd, p - 1)
                TT(fab[:, p % 2, 0, :], aux[2 * (p % 2)][:], dec[:, t, :], ALU.mult)
                TT(fab[:, p % 2, 1, :], aux[2 * (p % 2) + 1][:], dec[:, 4 if t == 0 else t, :], ALU.mult).then_inc(f_dec, 1)
                v.wait_ge(f_dec, p + 1)
                TT(fO[:, t, o * HY:(o + 1) * HY], fab[:, p % 2, 0, :], fab[:, p % 2, 1, :], ALU.subtract).then_inc(f_odd, 1)
                if p == 0:
                    v.wait_ge(c_silu, 1)
                modulation(2 * p, 2 * p + 2)

            modulation(16, ADA_T)
            v.wait_ge(ada_used, ADA_T)
            v.wait_ge(c_sum, CTX_POOL)
            TT(am[:, :, 0], am[:, :, 0], col("b_ada", 0, 48), ALU.add)
            TT(am[:, 0:16, 1], am[:, 0:16, 1], col("b_ada", 0, 16), ALU.add).then_inc(c_free, RING)
            v.wait_ge(c_free, RING)
            STT(out=acol[:, 0:8], in0=am[:, 8:16, 0], scalar=1.0, in1=col("g_mix_pre", 0, 8), op0=ALU.add, op1=ALU.mult)
            STT(out=acol[:, 8:16], in0=am[:, 8:16, 1], scalar=1.0, in1=col("g_mix_pre", 0, 8), op0=ALU.add, op1=ALU.mult)
            TT(acol[:, 16:24], am[:, 16:24, 0], col("g_mix_post", 0, 8), ALU.mult)
            STT(out=acol[:, 24:32], in0=am[:, 32:40, 0], scalar=1.0, in1=col("g_ffn_pre", 0, 8), op0=ALU.add, op1=ALU.mult)
            then(TT(acol[:, 32:40], am[:, 40:48, 0], col("g_ffn_post", 0, 8), ALU.mult))
            V.memset(pad0[:, 0:1], 0.0)
            V.memset(pad0[:, L + 1:L + 2], 0.0)
            V.memset(pad1[:, 0:1], 0.0)
            V.memset(pad1[:, L + 1:L + 2], 0.0).then_inc(hy_pad, 1)
            v.wait_ge(d_x, 64)
            v.wait_ge(consts, 2)
            norm_dve("mix_pre")
            norm_apply("mix_pre")

            for u in range(12):
                v.wait_ge(c_free, CB["hyena"] + u + 1)
                p = pads[u % 2]
                dst = uT[:, u, :] if u < 8 else x2T[:, u - 8, :]
                w = lambda tap: col("conv_w", tap * 12 + u)
                then(V.tensor_scalar(tmp[0][:], p[:, 0:L], w(0), col("conv_b", u), ALU.mult, ALU.add))
                then(STT(out=tmp[1][:], in0=p[:, 1:L + 1], scalar=w(1), in1=tmp[0][:], op0=ALU.mult, op1=ALU.add))
                STT(out=dst, in0=p[:, 2:L + 2], scalar=w(2), in1=tmp[1][:], op0=ALU.mult, op1=ALU.add).then_inc(hy_conv, 1)
            v.wait_ge(hy_nat, 8)

            def z_lo(c):
                v.wait_ge(hy_zhi, c + 1)
                TT(zlo[:, c, :], tmp[c % 2][:], zhi[:, c, :].bitcast(F32), ALU.subtract).then_inc(hy_zlo, 1)
            for o in range(2):
                for f in range(4):
                    v.wait_ge(hy_u, o * 4 + f + 1)
                    uc, us = aux[2 * (f % 2)][:], aux[2 * (f % 2) + 1][:]
                    gr, gs = Gr[o][:, f, :], Gs[o][:, f, :]
                    t = [pw[:, f % 2, n, :] for n in range(4)]
                    TT(t[0], gr, uc, ALU.mult)
                    TT(t[1], gs, us, ALU.mult)
                    TT(t[2], gs, uc, ALU.mult)
                    TT(t[3], gr, us, ALU.mult).then_inc(hy_pw, 1)
                    v.wait_ge(hy_pw, o * 4 + f + 1)
                    TT(gr, t[0], t[1], ALU.subtract)
                    TT(gs, t[2], t[3], ALU.add).then_inc(hy_y, 1)
                for t in range(NT):
                    v.wait_ge(hy_inv, o * 4 + t + 1)
                    if o == 0:
                        TT(n0[:, t, :], acc[t][:], n1[:, t, :], ALU.mult).then_inc(hy_yd, 1)
                    else:
                        if t >= 2:
                            z_lo(t - 2)
                            v.wait_ge(hy_zlo, t - 1)
                        TT(tmp[t % 2][:], acc[t][:], x2T[:, t, :], ALU.mult).then_inc(hy_z, 1)
            z_lo(2)
            z_lo(3)
            v.wait_ge(d_att, 48)
            sum_squares("ctx")

            for u in range(8):
                v.wait_ge(c_free, CB["qkv"] + u + 1)
                if u:
                    v.wait_ge(q_done, u)
                TT(r1[:], qe[:, u % 2, 0:L], cosT[:], ALU.mult)
                v.wait_ge(q_rot, u + 1)
                then(TT(r2[:], aux[2][:], sinT[:], ALU.mult))
                TT(qT[:, u, :] if u < 4 else kT[:, u - 4, 0:L], r1[:], r2[:], ALU.add).then_inc(q_done, 1)
                if u == 1:
                    v.wait_ge(q_done, 2)
                    norm_dve("ctx")
                    norm_apply("ctx")

            for n in range(ATT_STEPS + 4):
                if n < ATT_STEPS:
                    for m in range(2):
                        b = att_col(n, m)
                        v.wait_ge(a_s, 2 * n + m + 1)
                        then(V.reduce_max(small[:, b + 2:b + 3], scores[m][:, 0:NKEY], AX.X))
                        V.tensor_scalar(small[:, b:b + 1], small[:, b + 2:b + 3], -0.125, None, ALU.mult).then_inc(a_mx, 1)
                if 1 <= n <= ATT_STEPS:
                    b0, b1 = att_col(n - 1, 0), att_col(n - 1, 1)
                    v.wait_ge(a_p, 2 * n)
                    V.reciprocal(small[:, b0 + 3:b0 + 4], small[:, b0 + 1:b0 + 2])
                    then(V.reciprocal(small[:, b1 + 3:b1 + 4], small[:, b1 + 1:b1 + 2]))
                    then(V.tensor_scalar(small[:, b1 + 2:b1 + 3], small[:, b1 + 3:b1 + 4], small[:, 3:4], None, ALU.mult))
                    p0, p1 = pp[:, (n - 1) % 2, 0, :], pp[:, (n - 1) % 2, 1, :]
                    then(V.tensor_scalar(p0, p0, small[:, b0 + 3:b0 + 4], None, ALU.mult))
                    STT(out=p0, in0=p1, scalar=small[:, b1 + 2:b1 + 3], in1=p0, op0=ALU.mult, op1=ALU.add).then_inc(a_cm, 1)
                if n > NT:
                    h = (n - 3) // NT - 1
                    if n % NT == 3:
                        v.wait_ge(a_std, h + 1)
                        if h:
                            v.wait_ge(a_lo, h)
                        STT(out=tmp[0][:], in0=aux[2][:], scalar=small[:, 6:7], in1=rstd[:], op0=ALU.mult, op1=ALU.mult).then_inc(a_tmp, 1)
                    if n % NT == 0 and h >= 0:
                        v.wait_ge(a_hi, h + 1)
                        TT(olo[:, h, :], tmp[0][:], ohi[:, h, :].bitcast(F32), ALU.subtract).then_inc(a_lo, 1)
            v.wait_ge(a_hi, HEADS)
            TT(olo[:, HEADS - 1, :], tmp[0][:], ohi[:, HEADS - 1, :].bitcast(F32), ALU.subtract).then_inc(a_lo, 1)

            with v.Fori(0, 2) as i:
                for jj in range(4):
                    b = jj % 2
                    v.wait_ge(m_sg, i * 4 + (jj + 1))
                    v.wait_ge(w_used, i * 12 + (TB["mix"] + 3 * jj + 3))
                    TT(mt[:, b, 0, :], sgm[:, b, 0, :], acc[2][:], ALU.mult)
                    TT(mt[:, b, 1, :], sgm[:, b, 1, :], acc[3][:], ALU.mult).then_inc(c_free, 4)
                    v.wait_ge(c_free, i * 16 + (CB["mix"] + 4 * jj + 4))
                    TT(mt[:, b, 0, :], mt[:, b, 0, :], mt[:, b, 1, :], ALU.add).then_inc(m_sum, 1)
                    v.wait_ge(m_hi, i * 4 + (jj + 1))
                    TT(mxl[:, bass.ds(i * 4 + jj, 1), :], one(mt[:, b, 0, :]), mxh[:, bass.ds(i * 4 + jj, 1), :].bitcast(F32),
                       ALU.subtract).then_inc(m_lo, 1)

            def evacuate(name, dst, n_tiles, add=False, norm=None):
                if norm:
                    e = EVAC.index(norm)
                    V.memset(ssq[:], 0.0)
                with v.Fori(0, 2) as i:
                    for s in range(4):
                        v.wait_ge(w_used, i * (4 * n_tiles) + (TB[name] + n_tiles * (s + 1)))
                        d = dst[:, bass.ds(i * 4 + s, 1), :]
                        if add:
                            TT(d, one(acc[s][:]), d, ALU.add).then_inc(c_free, 1)
                        else:
                            V.tensor_copy(d, one(acc[s][:])).then_inc(c_free, 1)
                        if norm:
                            v.wait_ge(c_free, i * 4 + (CB[name] + s + 1))
                            TT(one(sq[0][:]), d, d, ALU.mult).then_inc(nm_dsq, 1)
                            v.wait_ge(nm_dsq, i * 4 + (e * KD + s + 1))
                            TT(ssq[:], ssq[:], sq[0][:], ALU.add).then_inc(nm_ssq, 1)
                v.wait_ge(c_free, CB[name] + 8)
            evacuate("wout", mo, 1, norm="mix_post")
            norm_dve("mix_post")
            residual("mix_post")
            norm_dve("ffn_pre")
            norm_apply("ffn_pre")
            with v.Fori(0, FC // 2) as i:
                for p in range(2):
                    v.wait_ge(s_silu, i * 2 + (p + 1))
                    v.wait_ge(w_used, i * 4 + (TB["gateup"] + 2 * p + 2))
                    TT(tmp[p][:], sil[:, p, :], acc[2 * p + 1][:], ALU.mult).then_inc(c_free, 2)
                    v.wait_ge(s_hi, i * 2 + (p + 1))
                    TT(hidl[:, bass.ds(i * 2 + p, 1), :], one(tmp[p][:]), hidh[:, bass.ds(i * 2 + p, 1), :].bitcast(F32),
                       ALU.subtract).then_inc(s_lo, 1)
            evacuate("down", ff_out, 3, norm="ffn_post")
            norm_dve("ffn_post")
            residual("ffn_post")
            norm_dve("g_mix")
            norm_apply("g_mix")

            then(V.memset(ssq[:], 0.0))
            with v.Fori(0, 4) as i:
                for s in range(4):
                    v.wait_ge(c_free, i * 4 + (CB["g_in"] + s + 1))
                    TT(one(ssq[:]), one(ssq[:]), vT[:, bass.ds(i * 4 + s, 1), :], ALU.add).then_inc(gsm, 1)
                    v.wait_ge(gsm, i * 4 + (s + 1))
            v.wait_ge(gmd, 1)
            for c in range(16):
                then(TT(vT[:, c, :], vT[:, c, :], mean[:], ALU.subtract))
                if c == 0:
                    then(TT(ssq[:], vT[:, 0, :], vT[:, 0, :], ALU.mult))
                    continue
                then(TT(sq[0][:], vT[:, c, :], vT[:, c, :], ALU.mult))
                m1 = TT(ssq[:], ssq[:], sq[0][:], ALU.add)
            m1.then_inc(gsq, 1)
            v.wait_ge(gstd, 1)
            for c in range(16):
                then(STT(out=vT[:, c, :], in0=vT[:, c, :], scalar=col("ln_g", c), in1=lrs[:], op0=ALU.mult, op1=ALU.mult))
                V.tensor_scalar(vT[:, c, :], vT[:, c, :], col("ln_b", c), None, ALU.add).then_inc(gv, 1)
            v.wait_ge(gws, 1)

            def g_lo(c):
                v.wait_ge(ghis, c + 1)
                TT(glo[:, c, :], gt[:, c % 2, 1, :], ghi[:, c, :].bitcast(F32), ALU.subtract).then_inc(glos, 1)
            for c in range(16):
                if c >= 2:
                    g_lo(c - 2)
                v.wait_ge(gsp, c + 1)
                TT(gt[:, c % 2, 0, :].rearrange("p (t n) -> p t n", n=P), acc[c % 4][:].rearrange("p (t n) -> p t n", n=P),
                   bsb[:, c // 2:c // 2 + 1, :].to_broadcast([P, NT, P]), ALU.add).then_inc(gta, 1)
                v.wait_ge(gta, c + 1)
                TT(gt[:, c % 2, 1, :], gt[:, c % 2, 0, :], guT[:, c, :], ALU.mult).then_inc(gtm, 1)
            g_lo(14)
            g_lo(15)
            evacuate("g_out", xT, 2, add=True, norm="mlp0")
            v.wait_ge(x_wfh, 1)
            TT(wfl[:], wf[:], wfh[:].bitcast(F32), ALU.subtract).then_inc(x_wfl, 1)
            norm_dve("mlp0")
            norm_apply("mlp0")

            def mlp(layer):
                for half in range(2):
                    n = 16 * (layer * 2 + half)
                    with v.Fori(0, 4) as i:
                        for s in range(4):
                            v.wait_ge(c_free, i * 4 + (CB[f"up{layer}{'ab'[half]}"] + s + 1))
                            TT(tmp[s % 2][:], sq[s % 2][:], sq[s % 2][:], ALU.mult).then_inc(m_rsq, 1)
                            v.wait_ge(m_rhi, i * 4 + (n + s + 1))
                            TT(ml[:, bass.ds(i * 4 + s, 1), :], one(tmp[s % 2][:]), mh[:, bass.ds(i * 4 + s, 1), :].bitcast(F32),
                               ALU.subtract).then_inc(m_rlo, 1)
                    evacuate(f"dn{layer}{'ab'[half]}", xT, 2, add=True, norm="fox" if layer == 0 and half == 1 else None)
            mlp(0)

            V.memset(qa[64:66, :, :], 1.0).then_inc(x_ini, 1)
            V.memset(ka[64:66, :, :], 1.0).then_inc(x_ini, 1)
            norm_dve("fox")
            norm_apply("fox")
            v.wait_ge(x_lf, 4)
            then(V.memset(lf[:, 2, :], 1.0))
            then(STT(out=lf[:, 3, :], in0=lf[:, 0, :], scalar=0.0, in1=lf[:, 1, :], op0=ALU.min, op1=ALU.subtract))
            V.tensor_tensor_scan(cpos[:], lf[:, 2, :], lf[:, 3, :], 0.0, ALU.mult, ALU.add).then_inc(x_c, 1)
            v.wait_ge(x_c, 1)
            V.tensor_scalar(cneg[:], cpos[:], -1.0, None, ALU.mult).then_inc(x_c, 1)
            v.wait_ge(x_c, 2)
            def fox_dve(g, a_, b_, par):
                ap_ = 1 - par

                def head_out(pair, buf, e):
                    v.wait_ge(x_o, pair * 2 + (e + 1))
                    r = slice(64 * e, 64 * e + 64)
                    TT(fog[r, :], aux[3][r, :], fsg[r, buf, :], ALU.mult).then_inc(x_og, 1)

                def normalize(s):
                    rs = (std, rstd)[s]
                    v.wait_ge(x_std, g * 2 + (s + 1))
                    for e in range(2):
                        r = slice(64 * e, 64 * e + 64)
                        g_ = small[r, 7:8] if s == 0 else cols[r, COLS["k_g"]:COLS["k_g"] + 1]
                        m1 = STT(out=(qa, ka)[s][0:64, par, e, :], in0=acc[s][r, :], scalar=g_, in1=rs[r, :], op0=ALU.mult, op1=ALU.mult)
                    m1.then_inc(x_qk, 1)
                    v.wait_ge(x_qk, g * 2 + (s + 1))
                for n in range(8):
                    if a_ is not None:
                        e, qi = n // 4, n % 4
                        W = (qi + 1) * P
                        b = aux[qi % 2]
                        v.wait_ge(x_s, a_ * 8 + (n + 1))
                        TT(b[:, qi * P:W], b[:, qi * P:W], cmask[:], ALU.add).then_inc(x_mk, 1)
                        v.wait_ge(x_mk, a_ * 8 + (n + 1))
                        V.reduce_max(small[:, 56 + n:57 + n], b[:, 0:W], AX.X).then_inc(x_rc, 1)
                        v.wait_ge(x_rc, a_ * 8 + (n + 1))
                        V.tensor_scalar(small[:, 40 + n:41 + n], small[:, 56 + n:57 + n], -1.0, None, ALU.mult).then_inc(x_mx, 1)
                        if n == 0:
                            v.wait_ge(x_gt, a_ + 1)
                            V.tensor_scalar(fsg[:, ap_, :], fsg[:, ap_, :], 1e18, 1.0, ALU.min, ALU.add).then_inc(x_g1, 1)
                        if n == 6:
                            v.wait_ge(x_sg, a_ + 1)
                            head_out(a_, ap_, 0)
                    if b_ is not None:
                        if n == 2:
                            head_out(b_, par, 1)
                        if n == 4:
                            v.wait_ge(x_hi, b_ + 1)
                            TT(fol[:, bass.ds(b_, 1), :], one(fog[:]), foh[:, bass.ds(b_, 1), :].bitcast(F32), ALU.subtract).then_inc(x_lo, 1)
                    if g is not None and n in (5, 6):
                        normalize(n - 5)
                    if a_ is not None:
                        v.wait_ge(x_p, a_ * 8 + (n + 1))
                        V.reciprocal(small[:, 64 + n:65 + n], small[:, 48 + n:49 + n]).then_inc(x_rd, 1)
                        v.wait_ge(x_rd, a_ * 8 + (n + 1))
                        V.tensor_scalar(fp[:, qi % 2, 0:W], fp[:, qi % 2, 0:W], small[:, 64 + n:65 + n], None, ALU.mult).then_inc(x_pn, 1)
            fox_steps(v, fox_dve)
            v.wait_ge(x_lo, 8)
            V.memset(tmp[1][:, 0:1], 0.0).then_inc(c_free, 32)
            evacuate("fox_out", xT, 1, add=True, norm="mlp1")
            norm_dve("mlp1")
            norm_apply("mlp1")
            mlp(1)


def _tables(np):
    k = np.arange(L) + 0.5
    s = np.arange(L)
    w = 2 * np.pi / (2 * L)
    dft = np.stack([np.cos(w * np.outer(s, k)), np.sin(w * np.outer(s, k)),
                    np.cos(w * np.outer(s + 0.5, k)), np.sin(w * np.outer(s + 0.5, k))])
    dft = dft.reshape(4, NT, P, L).transpose(0, 2, 1, 3)
    bands = 16
    t = np.linspace(0.0, 1.0, L)
    ang = np.outer(np.linspace(1e-4, bands - 1, bands), 2 * np.pi / L * s)
    z = np.concatenate([t[None], np.cos(ang), -np.sin(ang)])
    deltas = np.abs(np.linspace(math.log(1e-2) / 1.5, math.log(1e-2) / 0.3, HY))
    dec = np.exp(-np.outer(t, deltas)).reshape(NT, P, HY)
    back = dec[0].copy()
    back[0] = 0.0
    dec = np.concatenate([dec, back[None]]).transpose(1, 0, 2)
    d = np.arange(P)
    pos = np.where((d % 64 < 32)[:, None], s[None] // 64, s[None] % 64)
    a = pos * (10000.0 ** (-(d % 16) / 16.0))[:, None]
    rope = np.stack([np.cos(a), np.sin(a)])
    rot = np.zeros((P, P))
    for m in range(P):
        if m % 32 < 16:
            rot[m + 16, m] = -1.0
        else:
            rot[m - 16, m] = 1.0
    cmask = np.where(d[:, None] >= d[None, :], 0.0, -1e30)
    out = {"dft": dft, "zT": z, "decay": dec, "rope": rope, "rot": rot, "cmask": cmask, "ident": np.eye(P)}
    return {n: np.ascontiguousarray(x.astype(np.float32)) for n, x in out.items()}


def _blocks(np, w):
    k, m = w.shape
    return w.reshape(k // P, P, m // P, P).transpose(2, 1, 0, 3)


def _layout(np, x):
    w_in = _blocks(np, x["w_in"][0])
    gate, up = _blocks(np, x["w_ffn_gate"][0]), _blocks(np, x["w_ffn_up"][0])
    hy_up, att_up = _blocks(np, x["w_hy_up"][0]), _blocks(np, x["w_att_up"][0])
    down = _blocks(np, x["w_ffn_down"][0])
    g_in, g_out = _blocks(np, x["gmlp_w_in_2"][0]), _blocks(np, x["gmlp_w_out_2"][0])
    fox = _blocks(np, x["fox_w_in_2"][0][:, :4096])
    n = ADA_T + TILES
    w = np.zeros((n, P, 8, P), np.float32)
    w[:ADA_T] = x["w_ada"][0].T.reshape(ADA_T, P, 8, P)[[ada_chunk(u) for u in range(ADA_T)]]
    w[ADA_T:ADA_T + 24] = w_in[:24]
    b = ADA_T + TB["mix"]
    w[b:b + 24:3] = w_in[24:32]
    w[b + 1:b + 24:3] = w_in[32:40]
    w[b + 2:b + 24:3, :, :4] = hy_up
    w[b + 2:b + 24:3, :, 4:] = att_up
    b = ADA_T + TB["wout"]
    w[b:b + 8] = _blocks(np, x["w_out"][0])
    b = ADA_T + TB["gateup"]
    w[b:b + 44:2] = gate
    w[b + 1:b + 44:2] = up
    b = ADA_T + TB["down"]
    for p in range(3):
        k = down[:, :, 8 * p:8 * p + 8]
        w[b + p:b + 24:3, :, :k.shape[2]] = k
    b = ADA_T + TB["g_in"]
    w[b:b + 16] = g_in[16:]
    w[b + 16:b + 32] = g_in[:16]

    def wide(name, m):
        b = ADA_T + TB[name]
        w[b:b + 16:2] = m[:, :, :8]
        w[b + 1:b + 16:2] = m[:, :, 8:]
    wide("g_out", g_out)
    for layer in range(2):
        w1, w2 = _blocks(np, x["mlp_w1_2"][layer]), _blocks(np, x["mlp_w2_2"][layer])
        for half in range(2):
            b = ADA_T + TB[f"up{layer}{'ab'[half]}"]
            w[b:b + 16] = w1[16 * half:16 * half + 16]
            wide(f"dn{layer}{'ab'[half]}", w2[:, :, 16 * half:16 * half + 16])
    b = ADA_T + TB["fox"]
    for p in range(4):
        w[b + p:b + 32:4] = fox[8 * p:8 * p + 8]
    b = ADA_T + TB["fox_out"]
    w[b:b + 8] = _blocks(np, x["fox_w_out_2"][0])

    cols = np.zeros((P, NCOLS), np.float32)

    def put(name, v, off=0, rows=P):
        v = np.asarray(v).reshape(-1, rows).T
        cols[:rows, COLS[name] + off:COLS[name] + off + v.shape[1]] = v
    for name in ("g_mix_pre", "g_mix_post", "g_ffn_pre", "g_ffn_post"):
        put(name, x[name][0])
    put("b_ada", x["b_ada"][0])
    put("conv_w", x["hy_conv_w"][0])
    put("conv_b", x["hy_conv_b"][0])
    put("subln", x["att_subln_g"][0])
    put("ln_g", x["gmlp_ln_g_2"][0])
    put("ln_b", x["gmlp_ln_b_2"][0])
    put("mixn", x["mix_norm_g_2"])
    put("mlpn", x["mlp_norm_g_2"])
    for name, src in (("q_g", "fox_q_g_2"), ("k_g", "fox_k_g_2")):
        cols[:64, COLS[name]] = cols[64:, COLS[name]] = x[src][0]
    put("b_f", x["fox_b_f_2"][0], rows=16)
    for j in (1, 2):
        put("lam_q", x[f"lambda_q{j}"][0], j - 1, 64)
        put("lam_k", x[f"lambda_k{j}"][0], j - 1, 64)
    put("fb1", x["hy_f_b1"][0], rows=64)
    put("fb2", x["hy_f_b2"][0], rows=64)
    put("freq", x["hy_f_freq"][0], rows=64)

    def chunked(m):
        return np.ascontiguousarray(m.T.reshape(-1, P, m.shape[0]).transpose(1, 0, 2))
    return {
        "w": w, "cols": cols, "xT": chunked(x["x"][0]), "ctxT": chunked(x["ctx"][0]),
        "fw1": x["hy_f_w1"][0], "fw2": x["hy_f_w2"][0], "fw3": np.concatenate([x["hy_f_w3"][0], x["hy_f_b3"]]),
        "hbias": x["hy_bias"],
        "cvec": np.ascontiguousarray(np.broadcast_to(np.stack([x["c"][0], x["c_ctx"].reshape(-1)]), (P, 2, D))),
        "ws": np.ascontiguousarray(x["gmlp_w_s_2"][0].transpose(2, 0, 1)),
        "bs": np.ascontiguousarray(np.broadcast_to(x["gmlp_b_s_2"], (P, 8, P))),
        "wf": np.ascontiguousarray(x["fox_w_in_2"][0][:, 4096:].reshape(KD, P, 16).transpose(1, 0, 2)),
    }


def kernel(**inputs):
    import numpy as np
    import concourse.bacc as bacc
    from concourse.bass_utils import run_bass_kernel_spmd

    x = {n: np.asarray(v) for n, v in inputs.items()}
    arrays = {**_tables(np), **_layout(np, x)}
    nc = bacc.Bacc("TRN2", target_bir_lowering=False, num_devices=1)
    args, given = {}, {}
    for n, v in arrays.items():
        given[f"in_{n}"] = np.ascontiguousarray(v)
        args[n] = nc.dram_tensor(f"in_{n}", v.shape, F32, kind="ExternalInput").ap()
    args["scratch"] = nc.dram_tensor("scratch", (2, 16, L), F32, kind="Internal").ap()
    args["out"] = nc.dram_tensor("out", (P, KD, L), F32, kind="ExternalOutput").ap()
    build(nc, args)
    got = run_bass_kernel_spmd(nc, [given], core_ids=[0]).results[0]["out"]
    return np.ascontiguousarray(got.transpose(2, 1, 0).reshape(1, L, D))
```
